# Optimizing a Trainium2 kernel written in Bass

```python
import math
import jax, jax.numpy as jnp
from jax import lax
import numpy as np

D_MODEL = 1024
BATCH = 1
SEQ = 512
DEPTH = 2

NORM_EPS = 1e-6
D_FF = 2816
D_MIX = D_MODEL
MLA_HEADS = 8
MLA_NOPE_DIM = 64
MLA_ROPE_DIM = 32
MLA_V_DIM = 64
MLA_QK_DIM = MLA_NOPE_DIM + MLA_ROPE_DIM
MLA_Q_RANK = 256
MLA_KV_RANK = 128
MLA_WIDTH = MLA_HEADS * MLA_V_DIM
ROPE_THETA = 10000.0
Q_BLOCK = 128
CONV_WIDTH = D_MIX // 4
CONV_KERNEL = 31
HY_WIDTH = D_MIX - MLA_WIDTH - CONV_WIDTH
HY_ORDER = 2
HY_SHORT_KERNEL = 3
HY_EMB_DIM = 33
HY_FILTER_DIM = 64
HY_FAST_DECAY_PCT = 0.3
HY_SLOW_DECAY_PCT = 1.5
HY_DECAY_TARGET = 1e-2
HY_FILTER_OUT = HY_ORDER * 2 * HY_WIDTH
IN_MLA_Q = MLA_Q_RANK
IN_MLA_KV = MLA_KV_RANK
IN_MLA_KPE = MLA_ROPE_DIM
IN_CONV = 2 * CONV_WIDTH
IN_HY = (HY_ORDER + 1) * HY_WIDTH
OFF_Q = 0
OFF_KV = OFF_Q + IN_MLA_Q
OFF_KPE = OFF_KV + IN_MLA_KV
OFF_CONV = OFF_KPE + IN_MLA_KPE
OFF_HY = OFF_CONV + IN_CONV
IN_COLS = OFF_HY + IN_HY


def rmsnorm(x, g):
    xf = x.astype(jnp.float32)
    xf = xf * lax.rsqrt(jnp.mean(xf * xf, axis=-1, keepdims=True) + NORM_EPS)
    return (xf * g.astype(jnp.float32)).astype(x.dtype)

def layernorm(x, g, b):
    xf = x.astype(jnp.float32)
    mu = jnp.mean(xf, axis=-1, keepdims=True)
    var = jnp.mean(jnp.square(xf - mu), axis=-1, keepdims=True)
    y = (xf - mu) * lax.rsqrt(var + NORM_EPS)
    return (y * g.astype(jnp.float32) + b.astype(jnp.float32)).astype(x.dtype)

def swiglu(h, w_gate, w_up, w_down):
    return (jax.nn.silu(h @ w_gate) * (h @ w_up)) @ w_down

def depthwise_conv(u, w, b):
    k, c = w.shape
    pad = k // 2
    y = lax.conv_general_dilated(u, w[:, None, :].astype(u.dtype), window_strides=(1,),
                                 padding=[(pad, pad)], dimension_numbers=('NWC', 'WIO', 'NWC'),
                                 feature_group_count=c)
    return y + b.astype(u.dtype)

def rope_cos_sin(positions, dtype):
    inv_freq = 1.0 / (ROPE_THETA ** (jnp.arange(0, MLA_ROPE_DIM, 2, dtype=jnp.float32) / MLA_ROPE_DIM))
    ang = positions.astype(jnp.float32)[..., None] * inv_freq
    return jnp.cos(ang).astype(dtype), jnp.sin(ang).astype(dtype)

def apply_rope(x, cos, sin):
    x1, x2 = jnp.split(x, 2, axis=-1)
    return jnp.concatenate([x1 * cos - x2 * sin, x1 * sin + x2 * cos], axis=-1)

def mla_mixer(h_q, h_kv, k_pe, positions, q_norm, w_qb, kv_norm, w_kvb):
    b, l, _ = h_q.shape
    cos, sin = rope_cos_sin(positions, h_q.dtype)
    q = (rmsnorm(h_q, q_norm) @ w_qb).reshape(b, l, MLA_HEADS, MLA_QK_DIM)
    q_pe = apply_rope(q[..., MLA_NOPE_DIM:], cos[:, :, None], sin[:, :, None])
    q = jnp.concatenate([q[..., :MLA_NOPE_DIM], q_pe], axis=-1) * (MLA_QK_DIM ** -0.5)
    kv = (rmsnorm(h_kv, kv_norm) @ w_kvb).reshape(b, l, MLA_HEADS, MLA_NOPE_DIM + MLA_V_DIM)
    k_pe = apply_rope(k_pe, cos, sin)
    k = jnp.concatenate([kv[..., :MLA_NOPE_DIM],
                         jnp.broadcast_to(k_pe[:, :, None], (b, l, MLA_HEADS, MLA_ROPE_DIM))], axis=-1)
    v = kv[..., MLA_NOPE_DIM:]
    n_blk = l // Q_BLOCK
    q_blocks = q.reshape(b, n_blk, Q_BLOCK, MLA_HEADS, MLA_QK_DIM).transpose(1, 0, 2, 3, 4)

    def attend(qb):
        s = jnp.einsum('bqhd,bkhd->bhqk', qb, k).astype(jnp.float32)
        p = jax.nn.softmax(s, axis=-1).astype(v.dtype)
        return jnp.einsum('bhqk,bkhd->bqhd', p, v)

    o = lax.map(attend, q_blocks)
    return o.transpose(1, 0, 2, 3, 4).reshape(b, l, MLA_WIDTH)

def conformer_conv_mixer(h_conv, dw_w, dw_b, ln_g, ln_b):
    a, g = jnp.split(h_conv, 2, axis=-1)
    u = a * jax.nn.sigmoid(g)
    u = depthwise_conv(u, dw_w, dw_b)
    return jax.nn.silu(layernorm(u, ln_g, ln_b))

def hyena_filters(l, w1, b1, w2, b2, w3, b3, w4, freq):
    f32 = jnp.float32
    t = jnp.linspace(0.0, 1.0, l, dtype=f32)[:, None]
    bands = (HY_EMB_DIM - 1) // 2
    ang = 2.0 * math.pi * jnp.arange(l, dtype=f32)[:, None] / l
    fb = jnp.linspace(1e-4, bands - 1, bands, dtype=f32)[None, :]
    z = jnp.concatenate([t, jnp.cos(fb * ang), -jnp.sin(fb * ang)], axis=-1)
    fr = freq.astype(f32)
    hdn = jnp.sin(fr * (z @ w1.astype(f32) + b1.astype(f32)))
    hdn = jnp.sin(fr * (hdn @ w2.astype(f32) + b2.astype(f32)))
    hdn = jnp.sin(fr * (hdn @ w3.astype(f32) + b3.astype(f32)))
    h = (hdn @ w4.astype(f32)).reshape(l, HY_ORDER, 2, HY_WIDTH)
    max_decay = math.log(HY_DECAY_TARGET) / HY_FAST_DECAY_PCT
    min_decay = math.log(HY_DECAY_TARGET) / HY_SLOW_DECAY_PCT
    deltas = jnp.linspace(min_decay, max_decay, HY_WIDTH, dtype=f32)
    h = h * jnp.exp(-t * jnp.abs(deltas))[:, None, None, :]
    fwd, bwd = h[:, :, 0], h[:, :, 1]
    k = jnp.concatenate([fwd, jnp.zeros_like(fwd[:1]), jnp.flip(bwd[1:], axis=0)], axis=0)
    return k / jnp.sum(jnp.abs(k), axis=0, keepdims=True)

def fft_long_conv(u, k, d):
    l = u.shape[1]
    uf = u.astype(jnp.float32)
    uk = jnp.fft.rfft(uf, n=2 * l, axis=1) * jnp.fft.rfft(k, axis=0)[None]
    y = jnp.fft.irfft(uk, n=2 * l, axis=1)[:, :l]
    return (y + uf * d.astype(jnp.float32)).astype(u.dtype)

def hyena_mixer(h_hy, short_w, short_b, w1, b1, w2, b2, w3, b3, w4, freq, bias_d):
    u = depthwise_conv(h_hy, short_w, short_b)
    v, x1, x2 = jnp.split(u, HY_ORDER + 1, axis=-1)
    k = hyena_filters(h_hy.shape[1], w1, b1, w2, b2, w3, b3, w4, freq)
    z = x1 * fft_long_conv(v, k[:, 0], bias_d[0])
    return x2 * fft_long_conv(z, k[:, 1], bias_d[1])

def first_inputs(seed: int = 0) -> dict:
    key = jax.random.key(seed)
    ks = iter(jax.random.split(key, 64))
    f32 = jnp.float32

    def nrm(shape, scale):
        return jax.random.normal(next(ks), shape, f32) * scale

    def gain(shape):
        return 1.0 + nrm(shape, 0.05)

    dd = DEPTH
    return {
        "x": nrm((BATCH, SEQ, D_MODEL), 1.0),
        "positions": jnp.broadcast_to(jnp.arange(SEQ, dtype=jnp.int32)[None], (BATCH, SEQ)),
        "ffn1_norm": gain((dd, D_MODEL)),
        "ffn1_w_gate": nrm((dd, D_MODEL, D_FF), D_MODEL ** -0.5),
        "ffn1_w_up": nrm((dd, D_MODEL, D_FF), D_MODEL ** -0.5),
        "ffn1_w_down": nrm((dd, D_FF, D_MODEL), D_FF ** -0.5),
        "mix_norm": gain((dd, D_MODEL)),
        "w_in": nrm((dd, D_MODEL, IN_COLS), D_MODEL ** -0.5),
        "mla_q_norm": gain((dd, MLA_Q_RANK)),
        "mla_w_qb": nrm((dd, MLA_Q_RANK, MLA_HEADS * MLA_QK_DIM), MLA_Q_RANK ** -0.5),
        "mla_kv_norm": gain((dd, MLA_KV_RANK)),
        "mla_w_kvb": nrm((dd, MLA_KV_RANK, MLA_HEADS * (MLA_NOPE_DIM + MLA_V_DIM)), MLA_KV_RANK ** -0.5),
        "conv_dw_w": nrm((dd, CONV_KERNEL, CONV_WIDTH), CONV_KERNEL ** -0.5),
        "conv_dw_b": nrm((dd, CONV_WIDTH), 0.02),
        "conv_ln_g": gain((dd, CONV_WIDTH)),
        "conv_ln_b": nrm((dd, CONV_WIDTH), 0.02),
        "hy_short_w": nrm((dd, HY_SHORT_KERNEL, IN_HY), HY_SHORT_KERNEL ** -0.5),
        "hy_short_b": nrm((dd, IN_HY), 0.02),
        "hy_filt_w1": nrm((dd, HY_EMB_DIM, HY_FILTER_DIM), HY_EMB_DIM ** -0.5),
        "hy_filt_b1": nrm((dd, HY_FILTER_DIM), 0.1),
        "hy_filt_w2": nrm((dd, HY_FILTER_DIM, HY_FILTER_DIM), HY_FILTER_DIM ** -0.5),
        "hy_filt_b2": nrm((dd, HY_FILTER_DIM), 0.1),
        "hy_filt_w3": nrm((dd, HY_FILTER_DIM, HY_FILTER_DIM), HY_FILTER_DIM ** -0.5),
        "hy_filt_b3": nrm((dd, HY_FILTER_DIM), 0.1),
        "hy_filt_w4": nrm((dd, HY_FILTER_DIM, HY_FILTER_OUT), HY_FILTER_DIM ** -0.5),
        "hy_filt_freq": gain((dd, HY_FILTER_DIM)),
        "hy_bias_d": nrm((dd, HY_ORDER, HY_WIDTH), 0.5),
        "out_norm": gain((dd, D_MIX)),
        "w_out": nrm((dd, D_MIX, D_MODEL), D_MIX ** -0.5),
        "ffn2_norm": gain((dd, D_MODEL)),
        "ffn2_w_gate": nrm((dd, D_MODEL, D_FF), D_MODEL ** -0.5),
        "ffn2_w_up": nrm((dd, D_MODEL, D_FF), D_MODEL ** -0.5),
        "ffn2_w_down": nrm((dd, D_FF, D_MODEL), D_FF ** -0.5),
        "final_norm": gain((D_MODEL,)),
    }

def first_block(x, positions, ffn1_norm, ffn1_w_gate, ffn1_w_up, ffn1_w_down, mix_norm, w_in,
              mla_q_norm, mla_w_qb, mla_kv_norm, mla_w_kvb, conv_dw_w, conv_dw_b, conv_ln_g, conv_ln_b,
              hy_short_w, hy_short_b, hy_filt_w1, hy_filt_b1, hy_filt_w2, hy_filt_b2, hy_filt_w3, hy_filt_b3,
              hy_filt_w4, hy_filt_freq, hy_bias_d, out_norm, w_out, ffn2_norm, ffn2_w_gate, ffn2_w_up,
              ffn2_w_down, final_norm):
    e1 = MLA_WIDTH
    e2 = MLA_WIDTH + CONV_WIDTH
    for i in range(DEPTH):
        x = x + 0.5 * swiglu(rmsnorm(x, ffn1_norm[i]), ffn1_w_gate[i], ffn1_w_up[i], ffn1_w_down[i])
        h = rmsnorm(x, mix_norm[i]) @ w_in[i]
        y_mla = mla_mixer(h[..., OFF_Q:OFF_KV], h[..., OFF_KV:OFF_KPE], h[..., OFF_KPE:OFF_CONV], positions,
                          mla_q_norm[i], mla_w_qb[i], mla_kv_norm[i], mla_w_kvb[i])
        y_conv = conformer_conv_mixer(h[..., OFF_CONV:OFF_HY], conv_dw_w[i], conv_dw_b[i],
                                      conv_ln_g[i], conv_ln_b[i])
        y_hy = hyena_mixer(h[..., OFF_HY:], hy_short_w[i], hy_short_b[i], hy_filt_w1[i], hy_filt_b1[i],
                           hy_filt_w2[i], hy_filt_b2[i], hy_filt_w3[i], hy_filt_b3[i], hy_filt_w4[i],
                           hy_filt_freq[i], hy_bias_d[i])
        g = out_norm[i]
        y = jnp.concatenate([rmsnorm(y_mla, g[:e1]), rmsnorm(y_conv, g[e1:e2]), rmsnorm(y_hy, g[e2:])], axis=-1)
        x = x + y @ w_out[i]
        x = x + 0.5 * swiglu(rmsnorm(x, ffn2_norm[i]), ffn2_w_gate[i], ffn2_w_up[i], ffn2_w_down[i])
    return rmsnorm(x, final_norm)


DEPTH_2 = 1

MEM_LEN = 256
HEAD_DIM = 64
NSA_HEADS = 16
NSA_KV_GROUPS = 4
NSA_HPG = NSA_HEADS // NSA_KV_GROUPS
CMP_LEN = 32
CMP_STRIDE = 16
CMP_HIDDEN = 256
SEL_BLOCK = 64
SEL_TOPK = 8
WINDOW = 512
ROPE_THETA_2 = 500000.0
ROPE_DIM = HEAD_DIM // 4
RNN_WIDTH = D_MODEL
RNN_BLOCKS = 16
RNN_BLOCK_DIM = RNN_WIDTH // RNN_BLOCKS
CONV_WIDTH_2 = 4
RGLRU_C = 8.0
XATTN_HEADS = 4
XATTN_WIDTH = XATTN_HEADS * HEAD_DIM
D_FF_2 = 4 * D_MODEL
N_BRANCHES = 3
RMS_EPS = 1e-6

NSA_Q = NSA_HEADS * HEAD_DIM
NSA_KV = NSA_KV_GROUPS * HEAD_DIM
NSA_GATES = NSA_HEADS * 3
IN_WIDTHS = (NSA_Q, NSA_KV, NSA_KV, NSA_KV, NSA_KV, NSA_KV, NSA_KV, NSA_GATES,
             RNN_WIDTH, RNN_WIDTH, XATTN_WIDTH, N_BRANCHES * D_MODEL)
D_IN = sum(IN_WIDTHS)


def rms_norm(x, g):
    xf = x.astype(jnp.float32)
    y = xf * lax.rsqrt(jnp.mean(xf * xf, axis=-1, keepdims=True) + RMS_EPS)
    return (y * g.astype(jnp.float32)).astype(x.dtype)

def masked_softmax(s, mask):
    s = jnp.where(mask, s.astype(jnp.float32), -jnp.inf)
    m = jnp.max(s, axis=-1, keepdims=True)
    m = jnp.where(jnp.isfinite(m), m, 0.0)
    e = jnp.exp(s - m)
    return e / jnp.maximum(jnp.sum(e, axis=-1, keepdims=True), 1e-30)

def rope_tables(pos):
    inv = 1.0 / (ROPE_THETA_2 ** (jnp.arange(0, ROPE_DIM, 2, dtype=jnp.float32) / ROPE_DIM))
    ang = pos.astype(jnp.float32)[:, None] * inv[None, :]
    return jnp.cos(ang), jnp.sin(ang)

def apply_partial_rope(x, cos, sin):
    half = ROPE_DIM // 2
    xf = x.astype(jnp.float32)
    x1 = xf[..., :half]
    x2 = xf[..., half:ROPE_DIM]
    out = jnp.concatenate([x1 * cos - x2 * sin, x2 * cos + x1 * sin, xf[..., ROPE_DIM:]], axis=-1)
    return out.astype(x.dtype)

def cmp_to_sel_weights(n_cmp, n_sel):
    c0 = np.arange(n_cmp)[:, None] * CMP_STRIDE
    s0 = np.arange(n_sel)[None, :] * SEL_BLOCK
    ov = np.clip(np.minimum(c0 + CMP_LEN, s0 + SEL_BLOCK) - np.maximum(c0, s0), 0, None)
    return (ov / CMP_LEN).astype(np.float32)

def compress_blocks(kv, pos_emb, w1, w2):
    B, G, S, hd = kv.shape
    n_cmp = (S - CMP_LEN) // CMP_STRIDE + 1
    idx = jnp.arange(n_cmp)[:, None] * CMP_STRIDE + jnp.arange(CMP_LEN)[None, :]
    blocks = kv[:, :, idx, :] + pos_emb
    flat = blocks.reshape(B, G, n_cmp, CMP_LEN * hd)
    return jax.nn.gelu(flat @ w1) @ w2

def nsa_mixer(q, k_c, v_c, k_s, v_s, k_w, v_w, gates):
    B, G, Hg, S, hd = q.shape
    n_cmp = k_c.shape[2]
    n_sel = S // SEL_BLOCK
    n_top = min(SEL_TOPK, n_sel)
    nq = S // Q_BLOCK
    scale = HEAD_DIM ** -0.5
    c2s = jnp.asarray(cmp_to_sel_weights(n_cmp, n_sel))
    cmp_end = jnp.arange(n_cmp) * CMP_STRIDE + (CMP_LEN - 1)
    ks_blocks = k_s.reshape(B, G, n_sel, SEL_BLOCK, hd)
    vs_blocks = v_s.reshape(B, G, n_sel, SEL_BLOCK, hd)
    kw_pad = jnp.pad(k_w, ((0, 0), (0, 0), (WINDOW, 0), (0, 0)))
    vw_pad = jnp.pad(v_w, ((0, 0), (0, 0), (WINDOW, 0), (0, 0)))
    bi = jnp.arange(B)[:, None, None, None]
    gi = jnp.arange(G)[None, :, None, None]
    blk_ids = jnp.arange(n_sel)

    def block(args):
        i, q_b, g_b = args
        t = i * Q_BLOCK + jnp.arange(Q_BLOCK)
        s_c = jnp.einsum('bghqd,bgnd->bghqn', q_b, k_c) * scale
        p_c = masked_softmax(s_c, cmp_end[None, :] <= t[:, None])
        o_c = jnp.einsum('bghqn,bgnd->bghqd', p_c.astype(q_b.dtype), v_c)
        imp = jnp.einsum('bghqn,ns->bgqs', p_c, c2s)
        cur = (t // SEL_BLOCK)[:, None]
        forced = (blk_ids == 0) | (blk_ids == cur) | (blk_ids == cur - 1)
        future = blk_ids * SEL_BLOCK > t[:, None]
        imp = jnp.where(forced, jnp.inf, jnp.where(future, -jnp.inf, imp))
        _, idx = lax.top_k(imp, n_top)
        k_g = ks_blocks[bi, gi, idx]
        v_g = vs_blocks[bi, gi, idx]
        key_pos = (idx[..., None] * SEL_BLOCK + jnp.arange(SEL_BLOCK)).reshape(B, G, 1, Q_BLOCK, n_top * SEL_BLOCK)
        s_s = jnp.einsum('bghqd,bgqkld->bghqkl', q_b, k_g).reshape(B, G, Hg, Q_BLOCK, n_top * SEL_BLOCK) * scale
        p_s = masked_softmax(s_s, key_pos <= t[:, None])
        o_s = jnp.einsum('bghqkl,bgqkld->bghqd',
                         p_s.astype(q_b.dtype).reshape(B, G, Hg, Q_BLOCK, n_top, SEL_BLOCK), v_g)
        start = i * Q_BLOCK
        k_b = lax.dynamic_slice_in_dim(kw_pad, start, Q_BLOCK + WINDOW, axis=2)
        v_b = lax.dynamic_slice_in_dim(vw_pad, start, Q_BLOCK + WINDOW, axis=2)
        w_pos = start - WINDOW + jnp.arange(Q_BLOCK + WINDOW)
        mask_w = (w_pos[None, :] <= t[:, None]) & (w_pos[None, :] > t[:, None] - WINDOW)
        s_w = jnp.einsum('bghqd,bgkd->bghqk', q_b, k_b) * scale
        p_w = masked_softmax(s_w, mask_w)
        o_w = jnp.einsum('bghqk,bgkd->bghqd', p_w.astype(q_b.dtype), v_b)
        return g_b[..., 0:1] * o_c + g_b[..., 1:2] * o_s + g_b[..., 2:3] * o_w

    q_blocks = jnp.moveaxis(q.reshape(B, G, Hg, nq, Q_BLOCK, hd), 3, 0)
    g_blocks = jnp.moveaxis(gates.reshape(B, G, Hg, nq, Q_BLOCK, 3), 3, 0)
    out = lax.map(block, (jnp.arange(nq), q_blocks, g_blocks))
    out = jnp.moveaxis(out, 0, 3).reshape(B, G, Hg, S, hd)
    return out.transpose(0, 3, 1, 2, 4).reshape(B, S, G * Hg * hd)

def causal_depthwise_conv(x, w, b):
    S = x.shape[1]
    xp = jnp.pad(x, ((0, 0), (CONV_WIDTH_2 - 1, 0), (0, 0)))
    y = b
    for k in range(CONV_WIDTH_2):
        y = y + xp[:, k:k + S, :] * w[k]
    return y

def rg_lru(xr, w_a, b_a, w_i, b_i, lam):
    B, S, C = xr.shape
    xb = xr.reshape(B, S, RNN_BLOCKS, RNN_BLOCK_DIM)
    r = jax.nn.sigmoid(jnp.einsum('bsnk,nkj->bsnj', xb, w_a).reshape(B, S, C) + b_a)
    gi = jax.nn.sigmoid(jnp.einsum('bsnk,nkj->bsnj', xb, w_i).reshape(B, S, C) + b_i)
    log_a = -RGLRU_C * r.astype(jnp.float32) * jax.nn.softplus(-lam.astype(jnp.float32))
    a = jnp.exp(log_a)
    mult = jnp.sqrt(-jnp.expm1(2.0 * log_a))
    u = mult * (gi * xr).astype(jnp.float32)

    def combine(c1, c2):
        a1, b1 = c1
        a2, b2 = c2
        return a1 * a2, a2 * b1 + b2

    _, h = lax.associative_scan(combine, (a, u), axis=1)
    return h.astype(xr.dtype)

def cross_attention(q_x, mem, g_mem, w_mem_kv, w_xo):
    B, S, _ = q_x.shape
    M = mem.shape[1]
    q = q_x.reshape(B, S, XATTN_HEADS, HEAD_DIM)
    kv = (rms_norm(mem, g_mem) @ w_mem_kv).reshape(B, M, 2, XATTN_HEADS, HEAD_DIM)
    s = jnp.einsum('bshd,bmhd->bhsm', q, kv[:, :, 0]) * (HEAD_DIM ** -0.5)
    p = jax.nn.softmax(s.astype(jnp.float32), axis=-1).astype(q.dtype)
    o = jnp.einsum('bhsm,bmhd->bshd', p, kv[:, :, 1]).reshape(B, S, XATTN_WIDTH)
    return o @ w_xo

def second_inputs(seed: int = 0) -> dict:
    key = jax.random.key(seed)
    ks = jax.random.split(key, 32)
    L = DEPTH_2

    def nrm(k, shape, fan_in):
        return jax.random.normal(k, shape, jnp.float32) * (fan_in ** -0.5)

    def gain(k, shape):
        return 1.0 + 0.02 * jax.random.normal(k, shape, jnp.float32)

    def small(k, shape):
        return 0.02 * jax.random.normal(k, shape, jnp.float32)

    u = jax.random.uniform(ks[20], (L, RNN_WIDTH), jnp.float32, 0.9, 0.999) ** (1.0 / RGLRU_C)
    rg_lambda = jnp.log(u) - jnp.log1p(-u)
    return {
        "x": jax.random.normal(ks[0], (BATCH, SEQ, D_MODEL), jnp.float32),
        "mem": jax.random.normal(ks[1], (BATCH, MEM_LEN, D_MODEL), jnp.float32),
        "g_mix": gain(ks[2], (L, D_MODEL)),
        "w_in": nrm(ks[3], (L, D_MODEL, D_IN), D_MODEL),
        "cmp_pos_k": small(ks[4], (L, CMP_LEN, HEAD_DIM)),
        "cmp_pos_v": small(ks[5], (L, CMP_LEN, HEAD_DIM)),
        "w_cmp_k1": nrm(ks[6], (L, CMP_LEN * HEAD_DIM, CMP_HIDDEN), CMP_LEN * HEAD_DIM),
        "w_cmp_k2": nrm(ks[7], (L, CMP_HIDDEN, HEAD_DIM), CMP_HIDDEN),
        "w_cmp_v1": nrm(ks[8], (L, CMP_LEN * HEAD_DIM, CMP_HIDDEN), CMP_LEN * HEAD_DIM),
        "w_cmp_v2": nrm(ks[9], (L, CMP_HIDDEN, HEAD_DIM), CMP_HIDDEN),
        "conv_w": nrm(ks[10], (L, CONV_WIDTH_2, RNN_WIDTH), CONV_WIDTH_2),
        "conv_b": small(ks[11], (L, RNN_WIDTH)),
        "w_rg_a": nrm(ks[12], (L, RNN_BLOCKS, RNN_BLOCK_DIM, RNN_BLOCK_DIM), RNN_BLOCK_DIM),
        "b_rg_a": small(ks[13], (L, RNN_WIDTH)),
        "w_rg_i": nrm(ks[14], (L, RNN_BLOCKS, RNN_BLOCK_DIM, RNN_BLOCK_DIM), RNN_BLOCK_DIM),
        "b_rg_i": small(ks[15], (L, RNN_WIDTH)),
        "rg_lambda": rg_lambda,
        "g_mem": gain(ks[16], (L, D_MODEL)),
        "w_mem_kv": nrm(ks[17], (L, D_MODEL, 2 * XATTN_WIDTH), D_MODEL),
        "w_xo": nrm(ks[18], (L, XATTN_WIDTH, D_MODEL), XATTN_WIDTH),
        "w_o": nrm(ks[19], (L, D_MODEL, D_MODEL), D_MODEL),
        "g_mlp": gain(ks[21], (L, D_MODEL)),
        "w_up": nrm(ks[22], (L, D_MODEL, D_FF_2), D_MODEL),
        "w_down": nrm(ks[23], (L, D_FF_2, D_MODEL), D_FF_2),
        "g_final": gain(ks[24], (D_MODEL,)),
    }

def second_block(x, mem, g_mix, w_in, cmp_pos_k, cmp_pos_v, w_cmp_k1, w_cmp_k2, w_cmp_v1, w_cmp_v2,
              conv_w, conv_b, w_rg_a, b_rg_a, w_rg_i, b_rg_i, rg_lambda, g_mem, w_mem_kv, w_xo,
              w_o, g_mlp, w_up, w_down, g_final):
    B, S, D = x.shape
    G, Hg, hd = NSA_KV_GROUPS, NSA_HPG, HEAD_DIM
    offsets = np.cumsum(IN_WIDTHS)[:-1].tolist()
    cos, sin = rope_tables(jnp.arange(S))
    n_cmp = (S - CMP_LEN) // CMP_STRIDE + 1
    cos_c, sin_c = rope_tables(jnp.arange(n_cmp) * CMP_STRIDE + (CMP_LEN - 1))

    def to_groups(t):
        return t.reshape(B, S, G, hd).transpose(0, 2, 1, 3)

    h = x
    for l in range(DEPTH_2):
        u = rms_norm(h, g_mix[l])
        z = u @ w_in[l]
        (q_n, kc_raw, vc_raw, k_s, v_s, k_w, v_w, nsa_g,
         x_rnn, g_rnn, q_x, merge_g) = jnp.split(z, offsets, axis=-1)

        q = q_n.reshape(B, S, G, Hg, hd).transpose(0, 2, 3, 1, 4)
        q = apply_partial_rope(q, cos, sin)
        k_s = apply_partial_rope(to_groups(k_s), cos, sin)
        k_w = apply_partial_rope(to_groups(k_w), cos, sin)
        k_c = compress_blocks(to_groups(kc_raw), cmp_pos_k[l], w_cmp_k1[l], w_cmp_k2[l])
        k_c = apply_partial_rope(k_c, cos_c, sin_c)
        v_c = compress_blocks(to_groups(vc_raw), cmp_pos_v[l], w_cmp_v1[l], w_cmp_v2[l])
        nsa_gates = jax.nn.sigmoid(nsa_g).reshape(B, S, G, Hg, 3).transpose(0, 2, 3, 1, 4)
        y_nsa = nsa_mixer(q, k_c, v_c, k_s, to_groups(v_s), k_w, to_groups(v_w), nsa_gates)

        xc = causal_depthwise_conv(x_rnn, conv_w[l], conv_b[l])
        hr = rg_lru(xc, w_rg_a[l], b_rg_a[l], w_rg_i[l], b_rg_i[l], rg_lambda[l])
        y_rnn = jax.nn.gelu(g_rnn) * hr

        y_x = cross_attention(q_x, mem, g_mem[l], w_mem_kv[l], w_xo[l])

        gm = jax.nn.sigmoid(merge_g).reshape(B, S, N_BRANCHES, D)
        y = gm[:, :, 0] * y_nsa + gm[:, :, 1] * y_rnn + gm[:, :, 2] * y_x
        h = h + y @ w_o[l]

        v = rms_norm(h, g_mlp[l])
        h = h + jnp.square(jax.nn.relu(v @ w_up[l])) @ w_down[l]

    return rms_norm(h, g_final)


def setup_inputs(seed=0):
    out = dict(first_inputs(seed))
    for name, value in second_inputs(seed + 1).items():
        if name != "x":
            out[name + "_2"] = value
    return out


def reference(
    x, positions, ffn1_norm, ffn1_w_gate, ffn1_w_up, ffn1_w_down, mix_norm, w_in, mla_q_norm,
    mla_w_qb, mla_kv_norm, mla_w_kvb, conv_dw_w, conv_dw_b, conv_ln_g, conv_ln_b, hy_short_w,
    hy_short_b, hy_filt_w1, hy_filt_b1, hy_filt_w2, hy_filt_b2, hy_filt_w3, hy_filt_b3,
    hy_filt_w4, hy_filt_freq, hy_bias_d, out_norm, w_out, ffn2_norm, ffn2_w_gate, ffn2_w_up,
    ffn2_w_down, final_norm, mem_2, g_mix_2, w_in_2, cmp_pos_k_2, cmp_pos_v_2, w_cmp_k1_2,
    w_cmp_k2_2, w_cmp_v1_2, w_cmp_v2_2, conv_w_2, conv_b_2, w_rg_a_2, b_rg_a_2, w_rg_i_2,
    b_rg_i_2, rg_lambda_2, g_mem_2, w_mem_kv_2, w_xo_2, w_o_2, g_mlp_2, w_up_2, w_down_2,
    g_final_2,
):
    x = first_block(
        x, positions, ffn1_norm, ffn1_w_gate, ffn1_w_up, ffn1_w_down, mix_norm, w_in,
        mla_q_norm, mla_w_qb, mla_kv_norm, mla_w_kvb, conv_dw_w, conv_dw_b, conv_ln_g,
        conv_ln_b, hy_short_w, hy_short_b, hy_filt_w1, hy_filt_b1, hy_filt_w2, hy_filt_b2,
        hy_filt_w3, hy_filt_b3, hy_filt_w4, hy_filt_freq, hy_bias_d, out_norm, w_out, ffn2_norm,
        ffn2_w_gate, ffn2_w_up, ffn2_w_down, final_norm,
    )
    return second_block(
        x, mem_2, g_mix_2, w_in_2, cmp_pos_k_2, cmp_pos_v_2, w_cmp_k1_2, w_cmp_k2_2, w_cmp_v1_2,
        w_cmp_v2_2, conv_w_2, conv_b_2, w_rg_a_2, b_rg_a_2, w_rg_i_2, b_rg_i_2, rg_lambda_2,
        g_mem_2, w_mem_kv_2, w_xo_2, w_o_2, g_mlp_2, w_up_2, w_down_2, g_final_2,
    )


_drawn_inputs = setup_inputs


def setup_inputs(seed=0):
    import zlib

    import numpy as np

    out = dict(_drawn_inputs(seed))
    spreads = {}
    factors = {'conv_ln_b': 2.895,
     'hy_filt_freq': 5.54,
     'g_mix_2': 3.128,
     'cmp_pos_k_2': 64.0,
     'cmp_pos_v_2': 64.0,
     'b_rg_a_2': 33.855,
     'b_rg_i_2': 8.0,
     'g_mem_2': 8.0,
     'g_mlp_2': 10.204,
     'g_final_2': 8.065,
     'conv_b_2': 3.632}
    for name, (base, spread) in spreads.items():
        noise = np.random.default_rng([zlib.crc32(name.encode()), seed]).standard_normal(out[name].shape)
        drawn = base * np.exp(spread * noise) if base else spread * noise
        out[name] = __import__('jax').numpy.asarray(drawn.astype(out[name].dtype))
    for name, factor in factors.items():
        out[name] = (out[name] * factor).astype(out[name].dtype)
    return out
```

```python
import math
from contextlib import ExitStack

import numpy as np
import concourse.bass as bass
from concourse import mybir

F32 = mybir.dt.float32
F32R = mybir.dt.float32r
I32 = mybir.dt.int32
ALU = mybir.AluOpType
ACT = mybir.ActivationFunctionType
AX = mybir.AxisListType

P = 128
T = 512
TB = T // P
D = 1024
KC = D // P
F = 2816
PARTS = (12, 10)
DEPTH = 2
EPS = 1e-6

HEADS, NOPE, ROPE, VDIM = 8, 64, 32, 64
QK = NOPE + ROPE
QRANK, KVRANK = 256, 128
TAPS = 31
CONVC = 256
HYC = 256
HYF = 64
EMB = 33

MEM = 256
HEADS2, GROUPS = 16, 4
HD = 64
NCMP = (T - 32) // 16 + 1
XHEADS = 4
PARTS2 = (12, 12, 8)

RING = 4
SPLIT = 2
SLOT = 12 * P
MAGIC = 1.5 * 2.0 ** 23
TWO_PI = (6.28125, 1.93500518798828125e-3, 3.0199159819567e-7)
NEG = -1e30
FLOOR = -1e29

LAYER_COLS = [("g_ffn1", 8), ("g_mix", 8), ("g_q", 2), ("g_kv", 1), ("conv_w", 2 * TAPS), ("conv_b", 2),
              ("ln_g", 2), ("ln_b", 2), ("short_w", 18), ("short_b", 6), ("fb", 3), ("freq", 1),
              ("hy_d", 4), ("g_out", 8), ("g_ffn2", 8)]
LAST_COLS = [("g_final1", 8), ("g_mix2", 8), ("conv_w2", 32), ("conv_b2", 8), ("b_a", 8), ("b_i", 8),
             ("lam", 8), ("g_mem", 8), ("g_mlp", 8), ("g_final2", 8), ("pos_k", 16), ("pos_v", 16),
             ("eps", 1), ("npad", 4), ("padfloor", 4), ("invf", 1)]


def column_places():
    at, places = 0, {}
    for layer in range(DEPTH):
        for name, n in LAYER_COLS:
            places[name, layer] = at
            at += n
    for name, n in LAST_COLS:
        places[name] = at
        at += n
    return places, at


def stream():
    first = {8: 0, 10: 0, 12: 0}
    out = []

    def add(k, n):
        out.append((k, first[k], n))
        first[k] += n

    def ffn(parts, per):
        for part in parts:
            add(8, per * part)
            add(part, 8)

    for _ in range(DEPTH):
        ffn(PARTS, 2)
        add(8, 14)
        add(8, 8)
        ffn(PARTS, 2)
    add(8, 24)
    add(8, 6)
    add(8, 8)
    add(8, 21)
    add(8, 8)
    add(8, 8)
    ffn(PARTS2, 1)
    return out, first


class Walk:

    def __init__(self):
        self.n = self.m = self.aux = self.sq = self.norm = self.full = self.split = 0
        self.tables = self.hid = self.rope = self.unit = self.group = self.vec = self.act = self.loads = 0

    def gemm(self):
        self.n += 1
        self.m += 1
        return self.n - 1, self.m - 1

    def small(self):
        self.aux += 1
        self.m += 1
        return self.aux - 1, self.m - 1

    def bank(self):
        self.m += 1
        return self.m - 1


def at_turn(base, per, i):
    return base if i is None else i * per + base


def build(nc, d):
    places, ncols = column_places()
    plan, _ = stream()
    ctx = ExitStack()
    with ctx:
        base0 = (nc.sbuf_base + 31) // 32 * 32

        def place(name, shape, dt, at):
            return nc.alloc_sbuf_tensor_at(name, shape, dt, offset=base0 + at)

        K1 = 1024
        KB2 = T * 4
        X_AT, U_AT, RING_AT = 0, 16 * K1, 48 * K1
        H_AT = 96 * K1
        TMP_AT = 144 * K1
        ROPE_AT = 166 * K1
        SMALL_AT = 170 * K1
        x = place("x", [P, KC, T], F32, X_AT)
        u_hi = place("u_hi", [P, KC, T], F32R, U_AT)
        u_lo = place("u_lo", [P, KC, T], F32R, U_AT + 16 * K1)
        w_raw = [place(f"w_raw{i}", [P, SLOT], F32, RING_AT + i * SLOT * 4) for i in range(RING)]
        w_hi = [place(f"w_hi{i}", [P, SLOT], F32R, RING_AT + (4 + i) * SLOT * 4) for i in range(SPLIT)]
        w_lo = [place(f"w_lo{i}", [P, SLOT], F32R, RING_AT + (6 + i) * SLOT * 4) for i in range(SPLIT)]
        h_hi = place("h_hi", [P, 12, T], F32R, H_AT)
        h_lo = place("h_lo", [P, 12, T], F32R, H_AT + 24 * K1)
        sq = [place(f"sq{i}", [P, T], F32, TMP_AT + i * KB2) for i in range(2)]
        std = place("std", [P, T], F32, TMP_AT + 2 * KB2)
        rinv = place("rinv", [P, T], F32, TMP_AT + 3 * KB2)
        full = [place(f"full{i}", [P, T], F32, TMP_AT + (4 + i) * KB2) for i in range(3)]
        sg = [place(f"sg{i}", [P, T], F32, TMP_AT + (7 + i) * KB2) for i in range(2)]
        htmp = [place(f"htmp{i}", [P, T], F32, TMP_AT + (9 + i) * KB2) for i in range(2)]
        cosq = place("cosq", [P, T], F32, ROPE_AT)
        sinq = place("sinq", [P, T], F32, ROPE_AT + KB2)
        cols = place("cols", [P, ncols], F32, SMALL_AT)
        at = SMALL_AT + (ncols * 4 + 31) // 32 * 32
        ident = place("ident", [P, P], F32, at)
        ones = place("ones", [P, P], F32, at + 512)
        rot = place("rot", [P, P], F32, at + 1024)
        mx = place("mx", [P, 4], F32, at + 1536)
        nb = place("nb", [P, 4], F32, at + 1568)
        sums = place("sums", [P, 4], F32, at + 1600)
        den = place("den", [P, 4], F32, at + 1632)
        e0 = place("e0", [P, 4], F32, at + 1664)
        ri = place("ri", [P, 4], F32, at + 1696)
        assert at + 1728 <= 175 * K1
        R_AT = 175 * K1

        def mid(name, shape, at, dt=F32):
            return place(name, shape, dt, at)

        hm_q = mid("hm_q", [P, 4, T], R_AT)
        a_in = mid("a_in", [P, 2, T], R_AT + 8 * K1)
        g_sig = mid("g_sig", [P, 2, T], R_AT + 12 * K1)
        y_mla = mid("y_mla", [P, 4, T], R_AT + 8 * K1)
        hy = mid("hy", [P, 6, T], R_AT + 16 * K1)
        y_conv = mid("y_conv", [P, 2, T], R_AT + 28 * K1)
        PADW = T + TAPS - 1
        conv_pad = mid("conv_pad", [P, 2, PADW], H_AT)
        conv_acc = mid("conv_acc", [P, 2, T], H_AT + 5 * K1)
        conv_c = mid("conv_c", [P, 2, T], H_AT + 9 * K1)
        f_w1 = mid("f_w1", [EMB, HYF], H_AT)
        f_w23 = mid("f_w23", [HYF, 2, HYF], H_AT + 256)
        f_w4 = mid("f_w4", [HYF, 1024], H_AT + 1 * K1)
        f_z = mid("f_z", [EMB, T], H_AT + 5 * K1)
        f_h = [mid(f"f_h{i}", [HYF, T], H_AT + (7 + 2 * i) * K1) for i in range(2)]
        f_n = mid("f_n", [P, T], H_AT + 11 * K1)
        f_a = mid("f_a", [P, T], H_AT + 13 * K1)
        f_abs = [mid(f"f_abs{i}", [P, T], H_AT + (15 + 2 * i) * K1) for i in range(2)]
        spec = mid("spec", [P, 2, 4, 3, HYC], H_AT)
        dft = mid("dft", [P, 2, TB, T], H_AT + 24 * K1)
        decay = mid("decay", [P, TB, T], H_AT + 40 * K1)
        filt = mid("filt", [P, 2, TB, 2, HYC], U_AT)
        fsum = mid("fsum", [P, TB, 2, HYC], U_AT + 16 * K1)
        fdif = mid("fdif", [P, TB, 2, HYC], U_AT + 24 * K1)
        idft = mid("idft", [P, 2, TB, T], U_AT)
        v_tok = mid("v_tok", [P, TB, HYC], U_AT + 16 * K1)
        y_spec = mid("y_spec", [P, TB, 2, HYC], U_AT + 20 * K1)
        prod = [mid(f"prod{i}", [P, 2, HYC], U_AT + (28 + 2 * i) * K1) for i in range(2)]
        qn = mid("qn", [P, 2, T], H_AT)
        kvn = mid("kvn", [P, 1, T], H_AT + 4 * K1)
        q_all = mid("q_all", [P, HEADS, T], H_AT + 6 * K1)
        k_all = mid("k_all", [P, HEADS, T], H_AT + 22 * K1)
        v_all = mid("v_all", [P, TB, T], H_AT + 38 * K1)
        kpe_r = mid("kpe_r", [P, T], H_AT + 46 * K1)
        w_qb = mid("w_qb", [P, 2, HEADS * QK], U_AT)
        w_kvb = mid("w_kvb", [P, 2, T], U_AT + 6 * K1)
        pt = [mid(f"pt{i}", [P, TB, T], U_AT + 8 * i * K1) for i in range(2)]
        y2 = mid("y2", [P, KC, T], R_AT)
        gm0 = mid("gm0", [P, KC, T], R_AT + 16 * K1)
        w_ra = mid("w_ra", [P, 2, KC, P], H_AT)
        xpad = [mid(f"xpad{i}", [P, T + 3], H_AT + 8 * K1 + i * 2080) for i in range(2)]
        xc = [mid(f"xc{i}", [P, T], H_AT + (13 + 2 * i) * K1) for i in range(2)]
        rs = mid("rs", [P, T], H_AT + 17 * K1)
        isg = mid("isg", [P, T], H_AT + 19 * K1)
        th = mid("th", [P, T], H_AT + 21 * K1)
        sqt = mid("sqt", [P, T], H_AT + 23 * K1)
        gel = mid("gel", [P, T], H_AT + 25 * K1)
        gm1 = mid("gm1", [P, T], H_AT + 27 * K1)
        rw = mid("rw", [P, T], H_AT + 29 * K1)
        ra = mid("ra", [P, T], H_AT + 31 * K1)
        ru = mid("ru", [P, T], H_AT + 33 * K1)
        rh = mid("rh", [P, T], H_AT + 35 * K1)
        lamt = mid("lamt", [P, 8, KC], H_AT + 37 * K1)
        mem_t = mid("mem_t", [P, KC, MEM], H_AT)
        mem_hi = mid("mem_hi", [P, KC, MEM], H_AT + 8 * K1, F32R)
        mem_lo = mid("mem_lo", [P, KC, MEM], H_AT + 16 * K1, F32R)
        kx = mid("kx", [P, 2, MEM], H_AT + 24 * K1)
        vx = mid("vx", [P, 2, MEM], H_AT + 26 * K1)
        qx = mid("qx", [P, 2, T], H_AT + 28 * K1)
        ox = mid("ox", [P, 2, T], H_AT + 32 * K1)
        w_xo = mid("w_xo", [P, 2, D], H_AT + 36 * K1)
        gm2 = [mid(f"gm2{i}", [P, T], H_AT + (44 + 2 * i) * K1) for i in range(2)]
        ptx = [mid(f"ptx{i}", [P, TB, T], R_AT + (16 + 8 * i) * K1) for i in range(2)]
        q2 = mid("q2", [P, KC, T], H_AT)
        k2 = mid("k2", [P, 2, GROUPS, T], H_AT + 16 * K1)
        v2 = mid("v2", [P, 2, TB, 2, P], H_AT + 32 * K1)
        c_raw = mid("c_raw", [P, 4, T], H_AT + 40 * K1)
        w_c1 = mid("w_c1", [P, 16, 256], U_AT)
        c_dup = mid("c_dup", [P, GROUPS, T], U_AT + 16 * K1)
        c_blk = mid("c_blk", [P, 16, GROUPS, NCMP], U_AT + 24 * K1)
        c_hid = mid("c_hid", [P, 2, GROUPS * NCMP], TMP_AT + 7 * KB2)
        w_c2 = mid("w_c2", [P, 2, HD], TMP_AT + 8 * KB2)
        pt2 = [mid(f"pt2{i}", [P, TB, T], U_AT + 8 * i * K1) for i in range(2)]
        k_cmp = mid("k_cmp", [P, GROUPS, NCMP], TMP_AT + 2 * KB2)
        v_cmp = mid("v_cmp", [NCMP, GROUPS, HD], TMP_AT + 2 * KB2 + 512)
        gates = mid("gates", [P, TB, 48], TMP_AT + 3 * KB2)
        cmask = mid("cmask", [P, TB, NCMP], TMP_AT + 3 * KB2 + 800)
        causal = mid("causal", [P, P], TMP_AT + 3 * KB2 + 1312)
        cos_c = mid("cos_c", [HD, 2, GROUPS * NCMP], TMP_AT + 8 * KB2 + 768)

        out_t = mid("out_t", [P, KC, T], H_AT)

        psum = [ctx.enter_context(nc.psum_tensor(f"bank{i}", [P, T], F32)) for i in range(8)]
        ring = psum[0:4]
        score = psum[4:6]
        turned = psum[6:8]

        def sem(name):
            return ctx.enter_context(nc.semaphore(name))

        w_loaded = [sem(f"w_loaded{i}") for i in range(RING)]
        w_hi_ready = sem("w_hi_ready")
        w_split = sem("w_split")
        gemm_done = sem("gemm_done")
        aux_done = sem("aux_done")
        taken = [sem(f"taken{i}") for i in range(4)]
        sq_ready = sem("sq_ready")
        sq_used = sem("sq_used")
        rinv_ready = sem("rinv_ready")
        u_full = sem("u_full")
        u_hi_ready = sem("u_hi_ready")
        u_ready = sem("u_ready")
        h_hi_ready = sem("h_hi_ready")
        h_ready = sem("h_ready")
        dve_link = sem("dve_link")
        vec_ready = sem("vec_ready")
        act_ready = sem("act_ready")
        rope_done = sem("rope_done")
        s_full = sem("s_full")
        s_max = sem("s_max")
        exp_done = sem("exp_done")
        p_norm = sem("p_norm")
        t_full = sem("t_full")
        t_taken = sem("t_taken")
        pv_done = sem("pv_done")
        consts_in = sem("consts_in")
        small_in = sem("small_in")
        tables_in = sem("tables_in")
        out_ready = sem("out_ready")
        pool_tick = sem("pool_tick")
        act_tick = sem("act_tick")
        out_written = sem("out_written")

        block = ctx.enter_context(nc.Block())

        def col(name, layer, k, rows=P):
            c = places[(name, layer) if layer is not None else name] + k
            return cols[0:rows, c:c + 1]

        def wait_taken(eng, m, i=None):
            eng.wait_ge(taken[m % 4], at_turn(m // 4 + 1, 1, i))

        def weights(n, k):
            hi = w_hi[n % SPLIT][:, 0:k * P].rearrange("p (k n) -> p k n", n=P)
            lo = w_lo[n % SPLIT][:, 0:k * P].rearrange("p (k n) -> p k n", n=P)
            return hi, lo

        def mla_units():
            return [dict(head=h, i=i, last=(i == TB - 1), kind="plain", n=T, scale=QK ** -0.5, gate=None,
                         q=q_all[0:QK, h, P * i:P * i + P], k=k_all[0:QK, h, :],
                         pv=[(v_all[:, j, VDIM * h:VDIM * h + VDIM], P, j, 0) for j in range(TB)],
                         opens=True, closes=True)
                    for h in range(HEADS) for i in range(TB)]

        def cross_units():
            return [dict(head=h, i=i, last=(i == TB - 1), kind="plain", n=MEM, scale=HD ** -0.5, gate=None,
                         q=qx[HD * (h % 2):HD * (h % 2) + HD, h // 2, P * i:P * i + P],
                         k=kx[HD * (h % 2):HD * (h % 2) + HD, h // 2, :],
                         pv=[(vx[:, j, HD * h:HD * h + HD], P, j, 0) for j in range(MEM // P)],
                         opens=True, closes=True)
                    for h in range(XHEADS) for i in range(TB)]

        def nsa_units():
            out = []
            for h in range(HEADS2):
                g = h // (HEADS2 // GROUPS)
                qr = HD * (h % 2)
                for b, kind in enumerate(("cmp", "causal", "window")):
                    for i in range(TB):
                        if kind == "cmp":
                            k = k_cmp[qr:qr + HD, g, :]
                            n = NCMP
                            pv = [(v_cmp[:, g, :], NCMP, 0, 0)]
                        else:
                            n = P * (i + 1)
                            k = k2[qr:qr + HD, b - 1, g, 0:n]
                            pv = [(v2[:, b - 1, j, g // 2, HD * (g % 2):HD * (g % 2) + HD], P, j, P * j)
                                  for j in range(TB)]
                        out.append(dict(head=h, i=i, last=(i == TB - 1), kind=kind, n=n, scale=HD ** -0.5,
                                        gate=gates[:, i, 3 * h + b:3 * h + b + 1],
                                        q=q2[qr:qr + HD, h // 2, P * i:P * i + P], k=k, pv=pv,
                                        opens=(b == 0), closes=(b == 2)))
            return out

        def chunks(n):
            return [(c, min(P, n - P * c)) for c in range((n + P - 1) // P)]

        @block.sync
        def _(sp):
            sp.dma_start(x[:, :, :], d["xt"]).then_inc(consts_in, 16)
            sp.dma_start(cols[:, :], d["cols"]).then_inc(consts_in, 16)
            sp.dma_start(ident[:, :], d["ident"]).then_inc(consts_in, 16)
            n = 0
            for k, first, count in plan:
                src = d[f"w{k}"]

                def load(j, i=None):
                    slot = (n + j) % RING
                    if i is not None or n + j >= RING:
                        sp.wait_ge(w_split, at_turn(n + j - RING + 1, RING, i))
                    index = first + j if i is None else i * RING + (first + j)
                    block_ = src[bass.ds(index, 1)].rearrange("o p f -> (o p) f")
                    sp.dma_start(w_raw[slot][:, 0:k * P], block_).then_inc(w_loaded[slot], 16)

                if count % RING:
                    for j in range(count):
                        load(j)
                else:
                    for j in range(RING):
                        load(j)
                    with sp.Fori(1, count // RING) as i:
                        for j in range(RING):
                            load(j, i)
                n += count
            for c in range(KC):
                sp.wait_ge(out_ready, c + 1)
                sp.dma_start(d["out"][:, c, :], out_t[:, c, :]).then_inc(out_written, 16)
            sp.wait_ge(out_written, 16 * KC)

        @block.gpsimd
        def _(pool):
            n = 0
            for k, first, count in plan:
                def split(j, i=None):
                    m = n + j
                    raw = w_raw[m % RING][:, 0:k * P]
                    hi = w_hi[m % SPLIT][:, 0:k * P]
                    lo = w_lo[m % SPLIT][:, 0:k * P]
                    pool.wait_ge(w_loaded[m % RING], at_turn(16 * (m // RING + 1), 16, i))
                    if i is not None:
                        pool.sem_inc(pool_tick, 1)
                    if i is not None or m >= SPLIT:
                        pool.wait_ge(gemm_done, at_turn(m - SPLIT + 1, RING, i))
                        if i is not None:
                            pool.sem_inc(pool_tick, 1)
                    pool.tensor_scalar(hi, raw, 1.0, 1.0, ALU.mult, ALU.mult).then_inc(w_hi_ready, 1)
                    pool.wait_ge(w_hi_ready, at_turn(m + 1, RING, i))
                    pool.tensor_tensor(lo, raw, hi.bitcast(F32), ALU.subtract).then_inc(w_split, 1)

                if count % RING:
                    for j in range(count):
                        split(j)
                else:
                    for j in range(RING):
                        split(j)
                    with pool.Fori(1, count // RING) as i:
                        for j in range(RING):
                            split(j, i)
                n += count

        @block.tensor
        def _(pe):
            w = Walk()

            def open_bank(m, i=None):
                if i is not None or m >= 4:
                    pe.wait_ge(taken[m % 4], at_turn(m // 4, 1, i))
                return ring[m % 4]

            def multiply(n, out, k, rhs_hi, rhs_lo, i=None, ready=None):
                pe.wait_ge(w_split, at_turn(n + 1, RING, i))
                hi, lo = weights(n, k)
                for c in range(k):
                    if ready is not None:
                        ready(c)
                    pe.matmul(out, hi[:, c, :], rhs_hi(c), start=(c == 0), stop=False)
                    pe.matmul(out, hi[:, c, :], rhs_lo(c), start=False, stop=False)
                    mm = pe.matmul(out, lo[:, c, :], rhs_hi(c), start=False, stop=(c == k - 1))
                mm.then_inc(gemm_done, 1)

            def of_u(ready=None):
                n, m = w.gemm()
                multiply(n, open_bank(m)[:, :], KC, lambda c: u_hi[:, c, :], lambda c: u_lo[:, c, :],
                         ready=ready)

            def u_arrives(c):
                pe.wait_ge(u_ready, w.split - KC + c + 1)

            def norm(tiles, size=T, split=True):
                m = w.bank()
                out = open_bank(m)
                for c in range(tiles):
                    pe.wait_ge(sq_ready, w.sq + 1)
                    pe.matmul(out[:, 0:size], ones[:, :], sq[w.sq % 2][:, 0:size], start=(c == 0),
                              stop=(c == tiles - 1)).then_inc(sq_used, 1)
                    w.sq += 1
                w.full += tiles
                w.norm += 1
                if split:
                    w.split += tiles

            def looped(count, body):
                for j in range(4):
                    body(j, None)
                with pe.Fori(1, count // 4) as i:
                    for j in range(4):
                        body(j, i)
                w.n += count
                w.m += count

            def ffn(parts, per):
                for p, part in enumerate(parts):
                    def up(j, i):
                        ready = u_arrives if i is None and j == 0 and p == 0 else None
                        multiply(w.n + j, open_bank(w.m + j, i)[:, :], KC, lambda c: u_hi[:, c, :],
                                 lambda c: u_lo[:, c, :], i, ready)

                    looped(per * part, up)

                    def down(j, i):
                        ready = (lambda c: pe.wait_ge(h_ready, w.hid + c + 1)) if i is None and j == 0 else None
                        multiply(w.n + j, open_bank(w.m + j, i)[:, :], part, lambda c: h_hi[:, c, :],
                                 lambda c: h_lo[:, c, :], i, ready)

                    looped(8, down)
                    w.hid += part

            def attention(units):
                u0, g0 = w.unit, w.group
                ends = [s for s, u in enumerate(units) if u["last"]]
                o_bank = [None]
                for s in range(len(units) + 3):
                    if s < len(units):
                        u, k = units[s], u0 + s
                        if k >= 2:
                            pe.wait_ge(exp_done, k - 1)
                        pe.matmul(score[k % 2][:, 0:u["n"]], u["q"], u["k"], start=True,
                                  stop=True).then_inc(s_full, 1)
                    if 0 <= s - 2 < len(units):
                        u, k = units[s - 2], u0 + s - 2
                        pe.wait_ge(p_norm, k + 1)
                        if k >= 2:
                            pe.wait_ge(t_taken, k - 1)
                        for c, rows in chunks(u["n"]):
                            mm = pe.transpose(turned[k % 2][0:rows, P * c:P * c + P],
                                              full[k % 3][:, P * c:P * c + rows], ident[:, :])
                        mm.then_inc(t_full, 1)
                    if s - 3 in ends:
                        u, k = units[s - 3], u0 + s - 3
                        pe.wait_ge(t_taken, k + 1)
                        if u["opens"]:
                            o_bank[0] = open_bank(w.bank())
                        r0 = HD * (u["head"] % 2)
                        buf = u["ptbuf"][(g0 + ends.index(s - 3)) % 2]
                        for c, (v, rows, j, q0) in enumerate(u["pv"]):
                            mm = pe.matmul(o_bank[0][r0:r0 + HD, q0:T], v, buf[0:rows, j, q0:T],
                                           start=(u["opens"] and c == 0),
                                           stop=(u["closes"] and c == len(u["pv"]) - 1),
                                           skip_group_check=True)
                        mm.then_inc(pv_done, 1)
                w.unit += len(units)
                w.group += len(ends)

            def rope_product(raw, rows, cols_, m_raw):
                a, m = w.small()
                out = open_bank(m)
                if m_raw is not None:
                    wait_taken(pe, m_raw)
                pe.matmul(out[0:rows, 0:cols_], rot[0:rows, 0:rows], raw, start=True,
                          stop=True).then_inc(aux_done, 1)
                w.rope += 1

            def mixer(layer):
                norm(KC)
                for k in range(14):
                    of_u(u_arrives if k == 0 else None)
                v0 = w.vec
                a, m = w.small()
                out = open_bank(m)
                for t in range(2):
                    pe.wait_ge(vec_ready, v0 + 1 + t)
                    mm = pe.matmul(out[:, :], ones[:, :], conv_acc[:, t, :], start=(t == 0), stop=(t == 1))
                mm.then_inc(aux_done, 1)
                m = w.bank()
                out = open_bank(m)
                for t in range(2):
                    pe.wait_ge(sq_ready, w.sq + 1)
                    pe.matmul(out[:, :], ones[:, :], sq[w.sq % 2][:, :], start=(t == 0),
                              stop=(t == 1)).then_inc(sq_used, 1)
                    w.sq += 1
                w.norm += 1
                w.vec += 6
                w.act += 2
                w.loads += 4
                pe.wait_ge(small_in, 16 * w.loads)
                for l in range(3):
                    a, m = w.small()
                    if l == 0:
                        lhs, rhs = f_w1[:, :], f_z[:, :]
                    else:
                        pe.wait_ge(act_ready, w.act + l)
                        lhs, rhs = f_w23[:, l - 1, :], f_h[(l - 1) % 2][:, :]
                    pe.matmul(open_bank(m)[0:HYF, :], lhs, rhs, start=True, stop=True).then_inc(aux_done, 1)
                pe.wait_ge(act_ready, w.act + 3)
                for t in range(TB):
                    for o in range(2):
                        a, m = w.small()
                        pe.matmul(open_bank(m)[:, :], f_h[0][:, P * t:P * t + P],
                                  f_w4[:, T * o:T * o + T], start=True, stop=True).then_inc(aux_done, 1)
                w.vec += 3
                w.act += 3
                for o in range(2):
                    m = w.bank()
                    out = open_bank(m)
                    for t in range(TB):
                        pe.wait_ge(sq_ready, w.sq + 1)
                        for b in range(2):
                            mm = pe.matmul(out[:, 0:HYC], ones[:, :],
                                           f_abs[t % 2][:, HYC * b:HYC * b + HYC],
                                           start=(t == 0 and b == 0), stop=(t == TB - 1 and b == 1))
                        mm.then_inc(sq_used, 1)
                        w.sq += 1
                w.tables += 2
                pe.wait_ge(tables_in, 16 * w.tables)
                pe.wait_ge(vec_ready, w.vec + 9)
                for j in range(TB):
                    for part, src in ((0, fsum), (1, fdif)):
                        a, m = w.small()
                        out = open_bank(m)
                        for t in range(TB):
                            mm = pe.matmul(out[:, :], dft[:, part, t, P * j:P * j + P],
                                           src[:, t, :, :].rearrange("p o c -> p (o c)"),
                                           start=(t == 0), stop=(t == TB - 1))
                        mm.then_inc(aux_done, 1)
                w.vec += 10
                w.tables += 1
                for o in range(2):
                    v0 = w.vec
                    if o == 1:
                        pe.wait_ge(vec_ready, v0)
                    jobs = []
                    for t in range(TB):
                        a, m = w.small()
                        out = open_bank(m)
                        for c in range(2):
                            mm = pe.transpose(out[:, P * c:P * c + P], hy[:, 2 * o + c, P * t:P * t + P],
                                              ident[:, :])
                        mm.then_inc(aux_done, 1)
                        jobs.append(m)
                    for m in jobs:
                        wait_taken(pe, m)
                    for j in range(TB):
                        a, m = w.small()
                        out = open_bank(m)
                        for part in range(2):
                            for t in range(TB):
                                mm = pe.matmul(out[:, HYC * part:HYC * part + HYC],
                                               dft[:, part, t, P * j:P * j + P], v_tok[:, t, :],
                                               start=(t == 0), stop=(t == TB - 1), skip_group_check=True)
                        mm.then_inc(aux_done, 1)
                    if o == 0:
                        pe.wait_ge(tables_in, 16 * w.tables)
                    for c in range(2):
                        a, m = w.small()
                        out = open_bank(m)
                        for j in range(TB):
                            if c == 0:
                                pe.wait_ge(vec_ready, v0 + j + 1)
                            for part in range(2):
                                mm = pe.matmul(out[:, :], y_spec[:, j, part, P * c:P * c + P],
                                               idft[:, part, j, :], start=(j == 0 and part == 0),
                                               stop=(j == TB - 1 and part == 1))
                        mm.then_inc(aux_done, 1)
                    w.vec += TB + 2
                norm(2, split=False)
                norm(1, split=False)
                w.loads += 2
                pe.wait_ge(small_in, 16 * w.loads)
                pe.wait_ge(u_full, w.full)
                for t in range(TB):
                    a, m = w.small()
                    pe.matmul(open_bank(m)[:, :], kvn[:, 0, P * t:P * t + P], w_kvb[:, 1, :], start=True,
                              stop=True).then_inc(aux_done, 1)
                for h in range(0, HEADS, 2):
                    a, m = w.small()
                    pe.matmul(open_bank(m)[:, :], w_kvb[:, 0, NOPE * h:NOPE * h + P], kvn[:, 0, :],
                              start=True, stop=True).then_inc(aux_done, 1)
                rope_product(hm_q[0:QK, 3, :], QK, T, None)
                prev = None
                for h in range(HEADS + 1):
                    this = None
                    if h < HEADS:
                        a, m = w.small()
                        out = open_bank(m)
                        for c in range(2):
                            mm = pe.matmul(out[0:QK, :], w_qb[:, c, QK * h:QK * h + QK], qn[:, c, :],
                                           start=(c == 0), stop=(c == 1))
                        mm.then_inc(aux_done, 1)
                        this = m
                    if prev is not None:
                        rope_product(htmp[(h - 1) % 2][0:QK, :], QK, T, prev)
                    prev = this
                pe.wait_ge(rope_done, w.rope)
                w.vec += 1
                pe.wait_ge(vec_ready, w.vec)
                attention([dict(u, ptbuf=pt) for u in mla_units()])
                norm(4)
                norm(2)
                norm(2)

                def project(j, i):
                    ready = u_arrives if i is None and j == 0 else None
                    multiply(w.n + j, open_bank(w.m + j, i)[:, :], KC, lambda c: u_hi[:, c, :],
                             lambda c: u_lo[:, c, :], i, ready)

                looped(8, project)

            pe.wait_ge(consts_in, 16 * 3)
            pe.wait_ge(vec_ready, 1)
            w.vec += 1
            w.loads += 2
            for layer in range(DEPTH):
                norm(KC)
                ffn(PARTS, 2)
                if layer == 0:
                    w.vec += 2
                    w.act += 2
                mixer(layer)
                norm(KC)
                ffn(PARTS, 2)
            norm(KC, split=False)

            norm(KC)
            w.loads += 1
            pe.wait_ge(small_in, 16 * w.loads)
            w.vec += 1
            w.act += 2
            for t in range(KC):
                for k in range(3):
                    of_u(u_arrives if t == 0 and k == 0 else None)
                w.vec += 1
                pe.wait_ge(vec_ready, w.vec)
                for k in range(2):
                    a, m = w.small()
                    pe.matmul(open_bank(m)[:, :], w_ra[:, k, t, :], xc[t % 2][:, :], start=True,
                              stop=True).then_inc(aux_done, 1)
                w.act += 2
                w.vec += 1
            w.loads += 2
            norm(KC, size=MEM)
            for k in range(2):
                n, m = w.gemm()
                multiply(n, open_bank(m)[:, 0:MEM], KC, lambda c: mem_hi[:, c, :],
                         lambda c: mem_lo[:, c, :], ready=u_arrives if k == 0 else None)
            for k in range(2):
                n, m = w.gemm()
                out = open_bank(m)
                pe.wait_ge(w_split, n + 1)
                hi, lo = weights(n, KC)
                for tc in range(2):
                    for c in range(KC):
                        for q, (a_, b_) in enumerate(((mem_hi, hi), (mem_lo, hi), (mem_hi, lo))):
                            mm = pe.matmul(out[:, P * tc:P * tc + P], a_[:, c, P * tc:P * tc + P], b_[:, c, :],
                                           start=(c == 0 and q == 0), stop=(c == KC - 1 and q == 2),
                                           skip_group_check=True)
                mm.then_inc(gemm_done, 1)
            for k in range(2):
                of_u()
            wait_taken(pe, w.m - 1)
            attention([dict(u, ptbuf=ptx) for u in cross_units()])
            pe.wait_ge(small_in, 16 * w.loads)
            wait_taken(pe, w.m - 1)
            for t in range(KC):
                of_u()
                a, m = w.small()
                out = open_bank(m)
                for c in range(2):
                    mm = pe.matmul(out[:, :], w_xo[:, c, P * t:P * t + P], ox[:, c, :], start=(c == 0),
                                   stop=(c == 1))
                mm.then_inc(aux_done, 1)
            w.vec += KC
            w.loads += 3
            pe.wait_ge(small_in, 16 * w.loads)
            prev = None
            for k in range(13):
                this = None
                if k < 12:
                    of_u()
                    this = w.m - 1
                if prev is not None:
                    rope_product(htmp[(k - 1) % 2][:, :], P, T, prev)
                prev = this
            for k in range(4):
                of_u()
                src = w.m - 1
                a, m = w.small()
                out = open_bank(m)
                wait_taken(pe, src)
                for t in range(TB):
                    mm = pe.transpose(out[:, P * t:P * t + P], sg[k % 2][:, P * t:P * t + P], ident[:, :])
                mm.then_inc(aux_done, 1)
            of_u()
            src = w.m - 1
            a, m = w.small()
            out = open_bank(m)
            wait_taken(pe, src)
            for t in range(TB):
                mm = pe.transpose(out[:, 48 * t:48 * t + 48], sg[0][0:48, P * t:P * t + P], ident[0:48, 0:48])
            mm.then_inc(aux_done, 1)
            for k in range(4 + KC):
                of_u()
            for side in range(2):
                w.loads += 5 if side == 0 else 2
                pe.wait_ge(small_in, 16 * w.loads)
                w.vec += 1
                pe.wait_ge(vec_ready, w.vec)
                hid = []
                for mh in range(2):
                    a, m = w.small()
                    out = open_bank(m)
                    for c in range(16):
                        mm = pe.matmul(out[:, 0:GROUPS * NCMP], w_c1[:, c, P * mh:P * mh + P],
                                       c_blk[:, c, :, :].rearrange("p g n -> p (g n)"), start=(c == 0),
                                       stop=(c == 15))
                    mm.then_inc(aux_done, 1)
                    hid.append(m)
                for m in hid:
                    wait_taken(pe, m)
                a, m = w.small()
                out = open_bank(m)
                if side == 0:
                    for mh in range(2):
                        mm = pe.matmul(out[0:HD, 0:GROUPS * NCMP], w_c2[:, mh, :], c_hid[:, mh, :],
                                       start=(mh == 0), stop=(mh == 1))
                    mm.then_inc(aux_done, 1)
                    rope_product(htmp[0][0:HD, 0:GROUPS * NCMP], HD, GROUPS * NCMP, m)
                else:
                    for g in range(GROUPS):
                        for mh in range(2):
                            mm = pe.matmul(out[0:NCMP, HD * g:HD * g + HD],
                                           c_hid[:, mh, NCMP * g:NCMP * g + NCMP], w_c2[:, mh, :],
                                           start=(mh == 0), stop=(mh == 1), skip_group_check=True)
                    mm.then_inc(aux_done, 1)
                    wait_taken(pe, m)
            pe.wait_ge(rope_done, w.rope)
            attention([dict(u, ptbuf=pt2) for u in nsa_units()])
            w.split += KC

            def project2(j, i):
                ready = u_arrives if i is None and j == 0 else None
                multiply(w.n + j, open_bank(w.m + j, i)[:, :], KC, lambda c: u_hi[:, c, :],
                         lambda c: u_lo[:, c, :], i, ready)

            looped(8, project2)
            norm(KC)
            ffn(PARTS2, 1)
            norm(KC, split=False)

        @block.scalar
        def _(act):
            w = Walk()

            def done(n, i=None):
                act.wait_ge(gemm_done, at_turn(n + 1, 4, i))

            def take(dst, src, m, func=ACT.Copy, **kw):
                return act.activation(dst, src, func, **kw).then_inc(taken[m % 4], 1)

            def small_load(dst, src):
                act.dma_start(dst, src).then_inc(small_in, 16)
                w.loads += 1

            def to_high(dst):
                act.wait_ge(u_full, w.full + 1)
                act.activation(dst, full[w.split % 3][:, 0:dst.shape[-1]], ACT.Copy).then_inc(u_hi_ready, 1)
                w.full += 1
                w.split += 1

            def norm(srcs, dim, ready, highs=None, size=T):
                for c, s in enumerate(srcs):
                    ready(c)
                    if w.sq >= 2:
                        act.wait_ge(sq_used, w.sq - 1)
                    act.activation(sq[w.sq % 2][:, 0:size], s, ACT.Square).then_inc(sq_ready, 1)
                    w.sq += 1
                m = w.bank()
                act.wait_ge(sq_used, w.sq)
                if w.norm:
                    act.wait_ge(rinv_ready, w.norm)
                take(std[:, 0:size], ring[m % 4][:, 0:size], m, ACT.Sqrt, scale=1.0 / dim, bias=col("eps", None, 0))
                w.norm += 1
                if highs is None:
                    w.full += len(srcs)
                else:
                    for dst in highs:
                        to_high(dst)

            def x_tiles():
                return [x[:, c, :] for c in range(KC)]

            def high_tiles(a=0, b=KC):
                return [u_hi[:, c, :] for c in range(a, b)]

            def x_updated(c):
                wait_taken(act, w.m - KC + c)

            def looped(count, per, body):
                body(None)
                with act.Fori(1, count // per) as i:
                    body(i)

            def ffn(parts, per):
                for part in parts:
                    def chunk(i, c):
                        if per == 2:
                            gate, up = 2 * c, 2 * c + 1
                            done(w.n + gate, i)
                            act.activation(sg[c % 2][:, :], ring[(w.m + gate) % 4][:, :], ACT.Silu)\
                               .then_inc(taken[(w.m + gate) % 4], 1)
                            m = w.m + up
                        else:
                            m = w.m + c
                            done(w.n + c, i)
                            act.activation(sg[c % 2][:, :], ring[m % 4][:, :], ACT.Relu)\
                               .then_inc(act_ready, 1)
                        wait_taken(act, m, i)
                        act.sem_inc(act_tick, 1)
                        dst = h_hi[:, c, :] if i is None else \
                            h_hi[:, bass.ds(i * (4 // per) + c, 1), :].rearrange("p o t -> p (o t)")
                        act.activation(dst, htmp[c % 2][:, :], ACT.Copy).then_inc(h_hi_ready, 1)

                    def turn(i):
                        for c in range(4 // per):
                            chunk(i, c)

                    looped(per * part, 4, turn)
                    w.n += per * part
                    w.m += per * part
                    w.hid += part
                    if per == 1:
                        w.act += part
                    w.n += 8
                    w.m += 8

            def attention(units):
                u0, g0 = w.unit, w.group
                ends = [s for s, u in enumerate(units) if u["last"]]
                for s in range(len(units) + 2):
                    if s < len(units):
                        u, k = units[s], u0 + s
                        act.wait_ge(s_max, k + 1)
                        if k >= 3:
                            act.wait_ge(t_full, k - 2)
                        j = k % 4
                        if u["kind"] == "window":
                            act.activation(e0[:, j:j + 1], nb[:, j:j + 1], ACT.Exp).then_inc(act_tick, 1)
                        act.activation(full[k % 3][:, 0:u["n"]], score[k % 2][:, 0:u["n"]], ACT.Exp,
                                       bias=nb[:, j:j + 1], scale=u["scale"],
                                       accum_out=sums[:, j:j + 1]).then_inc(exp_done, 1)
                    if 0 <= s - 2 < len(units):
                        u, k = units[s - 2], u0 + s - 2
                        group = g0 + sum(e < s - 2 for e in ends)
                        act.wait_ge(t_full, k + 1)
                        if group >= 2:
                            act.wait_ge(pv_done, group - 1)
                        nch = len(chunks(u["n"]))
                        rows = min(P, u["n"])
                        i = u["i"]
                        act.activation(u["ptbuf"][group % 2][0:rows, 0:nch, P * i:P * i + P],
                                       turned[k % 2][0:rows, 0:P * nch].rearrange("p (c q) -> p c q", q=P),
                                       ACT.Copy).then_inc(t_taken, 1)
                w.unit += len(units)
                w.group += len(ends)
                w.m += sum(u["last"] and u["closes"] for u in units)

            def small_done(a):
                act.wait_ge(aux_done, a + 1)

            def mixer(layer):
                norm(x_tiles(), D, x_updated, high_tiles())
                for k in range(14):
                    n, m = w.gemm()
                    if k < 4:
                        done(n)
                        take(hm_q[:, k, :], ring[m % 4][:, :], m)
                    elif 6 <= k < 8:
                        done(n)
                        take(g_sig[:, k - 6, :], ring[m % 4][:, :], m, ACT.Sigmoid)
                v0 = w.vec
                w.small()
                for t in range(2):
                    act.wait_ge(vec_ready, v0 + 3 + t)
                    if w.sq >= 2:
                        act.wait_ge(sq_used, w.sq - 1)
                    act.activation(sq[w.sq % 2][:, :], conv_c[:, t, :], ACT.Square).then_inc(sq_ready, 1)
                    w.sq += 1
                m = w.bank()
                act.wait_ge(sq_used, w.sq)
                act.wait_ge(rinv_ready, w.norm)
                take(std[:, :], ring[m % 4][:, :], m, ACT.Sqrt, scale=1.0 / CONVC, bias=col("eps", None, 0))
                w.norm += 1
                for t in range(2):
                    act.wait_ge(vec_ready, v0 + 5 + t)
                    act.activation(y_conv[:, t, :], conv_c[:, t, :], ACT.Silu,
                                   bias=col("ln_b", layer, t)).then_inc(act_ready, 1)
                w.vec += 6
                w.act += 2
                act.wait_ge(act_ready, w.act)
                small_load(f_w1[:, :], d["f_w1"][layer])
                small_load(f_w23[:, :, :], d["f_w23"][layer])
                small_load(f_w4[:, :], d["f_w4"][layer])
                small_load(f_z[:, :], d["f_z"])
                act.dma_start(decay[:, :, :], d["decay"]).then_inc(tables_in, 16)
                act.dma_start(dft[:, :, :, :], d["dft"]).then_inc(tables_in, 16)
                w.tables += 3
                for l in range(3):
                    w.small()
                    act.wait_ge(vec_ready, w.vec + l + 1)
                    act.activation(f_h[l % 2][:, :], f_a[0:HYF, :], ACT.Sin).then_inc(act_ready, 1)
                w.aux += 8
                w.m += 8
                w.vec += 3
                w.act += 3
                for o in range(2):
                    m = w.bank()
                    for t in range(TB):
                        if o == 0 and t == 0:
                            act.wait_ge(vec_ready, w.vec + 8)
                        if TB * o + t >= 2:
                            act.wait_ge(sq_used, w.sq - 1)
                        act.activation(f_abs[t % 2][:, :],
                                       filt[:, o, t, :, :].rearrange("p b c -> p (b c)"), ACT.Abs)\
                           .then_inc(sq_ready, 1)
                        w.sq += 1
                w.aux += 8
                w.m += 8
                w.vec += 10
                act.wait_ge(vec_ready, w.vec)
                act.dma_start(idft[:, :, :, :], d["idft"]).then_inc(tables_in, 16)
                for o in range(2):
                    for t in range(TB):
                        a, m = w.small()
                        small_done(a)
                        take(v_tok[:, t, :], ring[m % 4][:, 0:HYC], m)
                    w.aux += TB + 2
                    w.m += TB + 2
                    w.vec += TB + 2
                norm([hm_q[:, 0, :], hm_q[:, 1, :]], QRANK, lambda c: None)
                norm([hm_q[:, 2, :]], KVRANK, lambda c: None)
                act.wait_ge(vec_ready, w.vec)
                small_load(w_qb[:, :, :], d["w_qb"][layer])
                small_load(w_kvb[:, :, :], d["w_kvb"][layer])
                for t in range(TB):
                    a, m = w.small()
                    small_done(a)
                    take(v_all[:, t, :], ring[m % 4][:, :], m)
                for h in range(0, HEADS, 2):
                    a, m = w.small()
                    small_done(a)
                    act.activation(k_all[0:NOPE, h, :], ring[m % 4][0:NOPE, :], ACT.Copy)
                    take(k_all[0:NOPE, h + 1, :], ring[m % 4][NOPE:P, :], m)
                w.small()
                w.rope += 1
                for h in range(HEADS + 1):
                    if h < HEADS:
                        a, m = w.small()
                        small_done(a)
                        if h >= 2:
                            act.wait_ge(rope_done, w.rope)
                        take(htmp[h % 2][0:QK, :], ring[m % 4][0:QK, :], m)
                    if h >= 1:
                        w.small()
                        w.rope += 1
                w.vec += 1
                attention([dict(u, ptbuf=pt) for u in mla_units()])
                heads_at = w.m - HEADS
                norm([y_mla[:, c, :] for c in range(4)], 512, lambda c: wait_taken(act, heads_at + 2 * c + 1),
                     high_tiles(0, 4))
                norm([y_conv[:, c, :] for c in range(2)], 256, lambda c: None, high_tiles(4, 6))
                norm([hy[:, 4 + c, :] for c in range(2)], 256, lambda c: act.wait_ge(vec_ready, w.vec - 1),
                     high_tiles(6, 8))
                w.n += 8
                w.m += 8

            act.dma_start(rot[:, :], d["rot1"]).then_inc(small_in, 16)
            act.dma_start(cosq[0:QK, :].bitcast(I32), d["positions"]).then_inc(small_in, 16)
            w.loads += 2
            act.wait_ge(consts_in, 16 * 3)
            w.vec += 1
            for layer in range(DEPTH):
                norm(x_tiles(), D, (lambda c: None) if layer == 0 else x_updated, high_tiles())
                ffn(PARTS, 2)
                if layer == 0:
                    act.wait_ge(vec_ready, w.vec + 1)
                    act.activation(sinq[0:QK, :], f_a[0:QK, :], ACT.Sin).then_inc(act_ready, 1)
                    act.wait_ge(vec_ready, w.vec + 2)
                    act.activation(cosq[0:QK, :], f_n[0:QK, :], ACT.Sin).then_inc(act_ready, 1)
                    w.vec += 2
                    w.act += 2
                mixer(layer)
                norm(x_tiles(), D, x_updated, high_tiles())
                ffn(PARTS, 2)
            norm(x_tiles(), D, x_updated)

            u0 = w.full
            norm(x_tiles(), D, lambda c: act.wait_ge(u_full, u0 - KC + c + 1), high_tiles())
            small_load(w_ra[:, :, :, :], d["w_ra"])
            act.activation(lamt[:, 0, :], cols[:, places["lam"]:places["lam"] + KC], ACT.Abs)\
               .then_inc(act_ready, 1)
            act.wait_ge(act_ready, w.act + 1)
            act.activation(lamt[:, 1, :], lamt[:, 0, :], ACT.Exp, scale=-1.0).then_inc(act_ready, 1)
            w.act += 2
            w.vec += 1
            for t in range(KC):
                n, m = w.gemm()
                done(n)
                if t >= 2:
                    act.wait_ge(vec_ready, w.vec - 3)
                take(xpad[t % 2][:, 3:T + 3], ring[m % 4][:, :], m)
                n, m = w.gemm()
                done(n)
                act.wait_ge(vec_ready, w.vec)
                take(gel[:, :], ring[m % 4][:, :], m, ACT.Gelu_apprx_tanh)
                n, m = w.gemm()
                done(n)
                take(gm1[:, :], ring[m % 4][:, :], m, ACT.Sigmoid)
                w.vec += 1
                for k, (dst, b) in enumerate(((rs, "b_a"), (isg, "b_i"))):
                    a, m = w.small()
                    small_done(a)
                    take(dst[:, :], ring[m % 4][:, :], m, ACT.Sigmoid, bias=col(b, None, t))
                    if k == 0:
                        m_r = m
                wait_taken(act, m_r)
                act.activation(th[:, :], rs[:, :], ACT.Tanh, scale=lamt[:, 7, t:t + 1]).then_inc(act_ready, 1)
                act.wait_ge(act_ready, w.act + 1)
                act.activation(sqt[:, :], th[:, :], ACT.Sqrt).then_inc(act_ready, 1)
                w.act += 2
                w.vec += 1
            act.wait_ge(vec_ready, w.vec)
            small_load(mem_t[:, :, :], d["mem_t"])
            small_load(w_xo[:, :, :], d["w_xo"])
            act.wait_ge(small_in, 16 * w.loads)
            norm([mem_t[:, c, :] for c in range(KC)], D, lambda c: None, [mem_hi[:, c, :] for c in range(KC)],
                 size=MEM)
            for k in range(2):
                n, m = w.gemm()
                done(n)
                take(kx[:, k, :], ring[m % 4][:, 0:MEM], m)
            for k in range(2):
                n, m = w.gemm()
                done(n)
                take(vx[:, :, P * k:P * k + P], ring[m % 4][:, 0:MEM].rearrange("p (t c) -> p t c", c=P), m)
            for k in range(2):
                n, m = w.gemm()
                done(n)
                take(qx[:, k, :], ring[m % 4][:, :], m)
            attention([dict(u, ptbuf=ptx) for u in cross_units()])
            for t in range(KC):
                n, m = w.gemm()
                done(n)
                if t >= 2:
                    act.wait_ge(vec_ready, w.vec + t - 1)
                take(gm2[t % 2][:, :], ring[m % 4][:, :], m, ACT.Sigmoid)
                w.small()
            w.vec += KC
            small_load(rot[:, :], d["rot2"])
            small_load(cosq[:, :], d["cos2"])
            small_load(sinq[:, :], d["sin2"])
            act.wait_ge(vec_ready, w.vec)
            act.wait_ge(small_in, 16 * w.loads)
            for k in range(13):
                if k < 12:
                    n, m = w.gemm()
                    done(n)
                    if k >= 2:
                        act.wait_ge(rope_done, w.rope)
                    take(htmp[k % 2][:, :], ring[m % 4][:, :], m)
                if k >= 1:
                    w.small()
                    w.rope += 1
            for k in range(4):
                n, m = w.gemm()
                done(n)
                take(sg[k % 2][:, :], ring[m % 4][:, :], m)
                a, m = w.small()
                small_done(a)
                take(v2[:, k // 2, :, k % 2, :], ring[m % 4][:, :].rearrange("p (t c) -> p t c", c=P), m)
            n, m = w.gemm()
            done(n)
            take(sg[0][0:48, :], ring[m % 4][0:48, :], m, ACT.Sigmoid)
            a, m = w.small()
            small_done(a)
            take(gates[:, :, :], ring[m % 4][:, 0:48 * TB].rearrange("p (t c) -> p t c", c=48), m)
            for k in range(4):
                n, m = w.gemm()
                done(n)
                take(c_raw[:, k, :], ring[m % 4][:, :], m)
            for k in range(KC):
                n, m = w.gemm()
                done(n)
                take(gm0[:, k, :], ring[m % 4][:, :], m, ACT.Sigmoid)
            for side in range(2):
                if side == 1:
                    act.wait_ge(rope_done, w.rope)
                small_load(w_c1[:, :, :], d["w_c1"][side])
                small_load(w_c2[:, :, :], d["w_c2"][side])
                if side == 0:
                    act.dma_start(cos_c[:, :, :], d["cos_c"]).then_inc(small_in, 16)
                    act.dma_start(cmask[:, :, :], d["cmask"]).then_inc(small_in, 16)
                    act.dma_start(causal[:, :], d["causal"]).then_inc(small_in, 16)
                    w.loads += 3
                w.vec += 1
                for mh in range(2):
                    a, m = w.small()
                    small_done(a)
                    take(c_hid[:, mh, :], ring[m % 4][:, 0:GROUPS * NCMP], m, ACT.Gelu_apprx_tanh)
                a, m = w.small()
                small_done(a)
                if side == 0:
                    take(htmp[0][0:HD, 0:GROUPS * NCMP], ring[m % 4][0:HD, 0:GROUPS * NCMP], m)
                    w.small()
                    w.rope += 1
                else:
                    take(v_cmp[:, :, :], ring[m % 4][0:NCMP, 0:GROUPS * HD].rearrange("p (g c) -> p g c", c=HD), m)
            attention([dict(u, ptbuf=pt2) for u in nsa_units()])
            wait_taken(act, w.m - 1)
            for c in range(KC):
                act.activation(u_hi[:, c, :], y2[:, c, :], ACT.Copy).then_inc(u_hi_ready, 1)
            w.split += KC
            w.n += 8
            w.m += 8
            norm(x_tiles(), D, x_updated, high_tiles())
            ffn(PARTS2, 1)
            norm(x_tiles(), D, x_updated)

        @block.vector
        def _(dve):
            w = Walk()
            links = [0]

            def step(ins):
                links[0] += 1
                ins.then_inc(dve_link, 1)
                return links[0]

            def link(ins):
                dve.wait_ge(dve_link, step(ins))

            def done(n, i=None):
                dve.wait_ge(gemm_done, at_turn(n + 1, 4, i))

            def small_done(a):
                dve.wait_ge(aux_done, a + 1)

            def arrived(ins):
                w.vec += 1
                return ins.then_inc(vec_ready, 1)

            def norm(srcs, gains, outs=None, lows=None, highs=None, size=T, signal=None):
                m = w.bank()
                w.sq += len(srcs)
                wait_taken(dve, m)
                if w.full:
                    dve.wait_ge(u_full, w.full)
                dve.reciprocal(rinv[:, 0:size], std[:, 0:size]).then_inc(rinv_ready, 1)
                w.norm += 1
                dve.wait_ge(rinv_ready, w.norm)
                count = len(srcs)
                for c in range(count + 1):
                    if c < count:
                        if outs is not None:
                            out = outs[c]
                        else:
                            out = full[(w.split + c) % 3][:, 0:size]
                            if w.split + c >= 3:
                                dve.wait_ge(u_ready, w.split + c - 2)
                        dve.scalar_tensor_tensor(out, srcs[c], gains(c), rinv[:, 0:size], ALU.mult,
                                                 ALU.mult).then_inc(signal or u_full, 1)
                    if c >= 1 and outs is None:
                        dve.wait_ge(u_hi_ready, w.split + c)
                        dve.tensor_tensor(lows[c - 1], full[(w.split + c - 1) % 3][:, 0:size],
                                          highs[c - 1].bitcast(F32), ALU.subtract).then_inc(u_ready, 1)
                w.full += count
                if outs is None:
                    w.split += count

            def x_tiles():
                return [x[:, c, :] for c in range(KC)]

            def norm_x(name, layer):
                norm(x_tiles(), lambda c: col(name, layer, c), lows=[u_lo[:, c, :] for c in range(KC)],
                     highs=[u_hi[:, c, :] for c in range(KC)])

            def looped(turns, body):
                body(None)
                with dve.Fori(1, turns) as i:
                    body(i)

            def add_to_x(scale):
                def turn(i):
                    for j in range(4):
                        m = w.m + j
                        tile = x[:, j, :] if i is None else \
                            x[:, bass.ds(i * 4 + j, 1), :].rearrange("p o t -> p (o t)")
                        done(w.n + j, i)
                        dve.scalar_tensor_tensor(tile, ring[m % 4][:, :], scale, tile, ALU.mult,
                                                 ALU.add).then_inc(taken[m % 4], 1)
                looped(2, turn)
                w.n += 8
                w.m += 8

            def ffn(parts, per):
                for part in parts:
                    def chunk(i, c):
                        if per == 2:
                            gate, up = w.m + 2 * c, w.m + 2 * c + 1
                            wait_taken(dve, gate, i)
                            done(w.n + 2 * c + 1, i)
                            dve.tensor_tensor(htmp[c % 2][:, :], ring[up % 4][:, :], sg[c % 2][:, :],
                                              ALU.mult).then_inc(taken[up % 4], 1)
                        else:
                            m = w.m + c
                            dve.wait_ge(act_ready, at_turn(w.act + c + 1, 4, i))
                            dve.tensor_tensor(htmp[c % 2][:, :], sg[c % 2][:, :], sg[c % 2][:, :],
                                              ALU.mult).then_inc(taken[m % 4], 1)
                        turn_size = 4 // per
                        dst = h_lo[:, c, :] if i is None else \
                            h_lo[:, bass.ds(i * turn_size + c, 1), :].rearrange("p o t -> p (o t)")
                        high = h_hi[:, c, :] if i is None else \
                            h_hi[:, bass.ds(i * turn_size + c, 1), :].rearrange("p o t -> p (o t)")
                        dve.wait_ge(h_hi_ready, at_turn(w.hid + c + 1, turn_size, i))
                        dve.tensor_tensor(dst, htmp[c % 2][:, :], high.bitcast(F32),
                                          ALU.subtract).then_inc(h_ready, 1)

                    def turn(i):
                        for c in range(4 // per):
                            chunk(i, c)

                    looped(per * part // 4, turn)
                    w.n += per * part
                    w.m += per * part
                    w.hid += part
                    if per == 1:
                        w.act += part
                    add_to_x(0.5 if per == 2 else 1.0)

            def reduce_angle(a, n):
                link(dve.tensor_scalar(n, a, 1.0 / (2.0 * math.pi), MAGIC, ALU.mult, ALU.add))
                link(dve.tensor_scalar(n, n, MAGIC, None, ALU.subtract))
                for part in TWO_PI:
                    link(dve.scalar_tensor_tensor(a, n, -part, a, ALU.mult, ALU.add))

            def clamp_angle(a):
                return dve.tensor_scalar(a, a, 3.1415925, -3.1415925, ALU.min, ALU.max)

            def rotate(raw, outs, cos, sin, rows, cols_, m_raw):
                a, m = w.small()
                if m_raw is not None:
                    wait_taken(dve, m_raw)
                if w.rope:
                    dve.wait_ge(rope_done, w.rope)
                t1, t2 = sq[0][0:rows, 0:cols_], sq[1][0:rows, 0:cols_]
                step(dve.tensor_tensor(t1, raw, cos, ALU.mult))
                small_done(a)
                dve.tensor_tensor(t2, ring[m % 4][0:rows, 0:cols_], sin, ALU.mult)\
                   .then_inc(taken[m % 4], 1)
                dve.wait_ge(dve_link, links[0])
                wait_taken(dve, m)
                for k, (out, r0) in enumerate(outs):
                    r1 = r0 + out.shape[0]
                    ins = dve.tensor_tensor(out, sq[0][r0:r1, 0:cols_], sq[1][r0:r1, 0:cols_], ALU.add)
                    if k == len(outs) - 1:
                        ins.then_inc(rope_done, 1)
                w.rope += 1

            def attention(units, take_head):
                u0, g0 = w.unit, w.group
                ends = [s for s, u in enumerate(units) if u["last"]]
                for s in range(len(units) + 4):
                    if s < len(units):
                        u, k = units[s], u0 + s
                        j, n = k % 4, u["n"]
                        sc = score[k % 2]
                        dve.wait_ge(s_full, k + 1)
                        if u["kind"] in ("causal", "window"):
                            link(dve.tensor_tensor(sc[:, n - P:n], sc[:, n - P:n], causal[:, :], ALU.add))
                        elif u["kind"] == "cmp":
                            link(dve.tensor_tensor(sc[:, 0:n], sc[:, 0:n], cmask[:, u["i"], :], ALU.add))
                        link(dve.tensor_reduce(mx[:, j:j + 1], sc[:, 0:n], AX.X, ALU.max))
                        if u["kind"] == "window":
                            ins = dve.tensor_scalar(nb[:, j:j + 1], mx[:, j:j + 1], col("padfloor", None, u["i"]),
                                                    -u["scale"], ALU.max, ALU.mult)
                        elif u["kind"] == "cmp":
                            ins = dve.tensor_scalar(nb[:, j:j + 1], mx[:, j:j + 1], FLOOR, -u["scale"],
                                                    ALU.max, ALU.mult)
                        else:
                            ins = dve.tensor_scalar(nb[:, j:j + 1], mx[:, j:j + 1], -u["scale"], None, ALU.mult)
                        ins.then_inc(s_max, 1)
                    if 0 <= s - 1 < len(units):
                        u, k = units[s - 1], u0 + s - 1
                        j, n = k % 4, u["n"]
                        dve.wait_ge(exp_done, k + 1)
                        total = sums[:, j:j + 1]
                        if u["kind"] == "window":
                            link(dve.scalar_tensor_tensor(den[:, j:j + 1], e0[:, j:j + 1],
                                                          col("npad", None, u["i"]), total, ALU.mult, ALU.add))
                            total = den[:, j:j + 1]
                        elif u["kind"] == "cmp":
                            link(dve.tensor_scalar(den[:, j:j + 1], total, 1e-30, None, ALU.max))
                            total = den[:, j:j + 1]
                        link(dve.reciprocal(ri[:, j:j + 1], total))
                        prob = full[k % 3][:, 0:n]
                        if u["gate"] is None:
                            ins = dve.tensor_scalar(prob, prob, ri[:, j:j + 1], None, ALU.mult)
                        else:
                            ins = dve.tensor_scalar(prob, prob, ri[:, j:j + 1], u["gate"], ALU.mult, ALU.mult)
                        ins.then_inc(p_norm, 1)
                    if s - 4 in ends and units[s - 4]["closes"]:
                        u = units[s - 4]
                        m = w.bank()
                        dve.wait_ge(pv_done, g0 + ends.index(s - 4) + 1)
                        r0 = HD * (u["head"] % 2)
                        take_head(u["head"], ring[m % 4][r0:r0 + HD, :], r0, m)
                w.unit += len(units)
                w.group += len(ends)

            def mixer(layer):
                def c(name, k, rows=P):
                    return col(name, layer, k, rows)

                norm_x("g_mix", layer)
                w.n += 4
                w.m += 4
                for t in range(2):
                    n, m = w.gemm()
                    done(n)
                    dve.tensor_copy(a_in[:, t, :], ring[m % 4][:, :]).then_inc(taken[m % 4], 1)
                    m_a = m
                step(dve.memset(conv_pad[:, :, 0:TAPS // 2], 0.0))
                step(dve.memset(conv_pad[:, :, PADW - TAPS // 2:PADW], 0.0))
                wait_taken(dve, m_a)
                for t in range(2):
                    n, m = w.gemm()
                    wait_taken(dve, m)
                    step(dve.tensor_tensor(conv_pad[:, t, TAPS // 2:TAPS // 2 + T], a_in[:, t, :],
                                           g_sig[:, t, :], ALU.mult))
                for k in range(6):
                    n, m = w.gemm()
                    done(n)
                    src = ring[m % 4]
                    link(dve.tensor_scalar(hy[:, k, :], src[:, :], c("short_w", 3 * k + 1), c("short_b", k),
                                           ALU.mult, ALU.add))
                    link(dve.scalar_tensor_tensor(hy[:, k, 1:T], src[:, 0:T - 1], c("short_w", 3 * k),
                                                  hy[:, k, 1:T], ALU.mult, ALU.add))
                    dve.scalar_tensor_tensor(hy[:, k, 0:T - 1], src[:, 1:T], c("short_w", 3 * k + 2),
                                             hy[:, k, 0:T - 1], ALU.mult, ALU.add).then_inc(taken[m % 4], 1)
                for tap in range(TAPS):
                    for t in range(2):
                        dve.wait_ge(dve_link, links[0] - (1 if 0 < tap < TAPS - 1 else 0))
                        src = conv_pad[:, t, tap:tap + T]
                        if tap == 0:
                            ins = dve.tensor_scalar(conv_acc[:, t, :], src, c("conv_w", TAPS * t),
                                                    c("conv_b", t), ALU.mult, ALU.add)
                        else:
                            ins = dve.scalar_tensor_tensor(conv_acc[:, t, :], src, c("conv_w", TAPS * t + tap),
                                                           conv_acc[:, t, :], ALU.mult, ALU.add)
                        if tap < TAPS - 1:
                            step(ins)
                        else:
                            arrived(ins)
                a, m = w.small()
                small_done(a)
                dve.wait_ge(vec_ready, w.vec)
                for t in range(2):
                    ins = arrived(dve.scalar_tensor_tensor(conv_c[:, t, :], ring[m % 4][:, :], -1.0 / CONVC,
                                                           conv_acc[:, t, :], ALU.mult, ALU.add))
                dve.wait_ge(vec_ready, w.vec)
                dve.sem_inc(taken[m % 4], 1)
                m = w.bank()
                w.sq += 2
                wait_taken(dve, m)
                dve.wait_ge(u_full, w.full)
                dve.reciprocal(rinv[:, :], std[:, :]).then_inc(rinv_ready, 1)
                w.norm += 1
                dve.wait_ge(rinv_ready, w.norm)
                for t in range(2):
                    arrived(dve.scalar_tensor_tensor(conv_c[:, t, :], conv_c[:, t, :], c("ln_g", t), rinv[:, :],
                                                     ALU.mult, ALU.mult))
                w.act += 2
                for l in range(3):
                    a, m = w.small()
                    small_done(a)
                    arg, n_ = f_a[0:HYF, :], f_n[0:HYF, :]
                    if l:
                        dve.wait_ge(act_ready, w.act + l)
                    dve.tensor_scalar(arg, ring[m % 4][0:HYF, :], c("fb", l, HYF), c("freq", 0, HYF),
                                      ALU.add, ALU.mult).then_inc(taken[m % 4], 1)
                    wait_taken(dve, m)
                    reduce_angle(arg, n_)
                    arrived(clamp_angle(arg))
                w.act += 3
                dve.wait_ge(tables_in, 16 * (w.tables + 2))
                w.tables += 3
                v0 = w.vec
                for t in range(TB):
                    for o in range(2):
                        a, m = w.small()
                        small_done(a)
                        dve.tensor_tensor(filt[:, o, t, :, :].rearrange("p b c -> p (b c)"), ring[m % 4][:, :],
                                          decay[:, t, :], ALU.mult).then_inc(taken[m % 4], 1)
                    for m_ in (m - 1, m):
                        wait_taken(dve, m_)
                    step(dve.tensor_tensor(fsum[:, t, :, :], filt[:, :, t, 0, :], filt[:, :, t, 1, :], ALU.add))
                    dve.tensor_tensor(fdif[:, t, :, :], filt[:, :, t, 0, :], filt[:, :, t, 1, :], ALU.subtract)\
                       .then_inc(vec_ready, 2 if t < TB - 1 else 3)
                w.vec += 9
                for o in range(2):
                    m = w.bank()
                    w.sq += TB
                    dve.wait_ge(sq_used, w.sq)
                    dve.reciprocal(rinv[:, HYC * o:HYC * o + HYC], ring[m % 4][:, 0:HYC])\
                       .then_inc(taken[m % 4], 1)
                    wait_taken(dve, m)
                rk = rinv[:, :].rearrange("p (o c) -> p o c", o=2)
                for j in range(TB):
                    for part in range(2):
                        a, m = w.small()
                        small_done(a)
                        src = ring[m % 4][:, :].rearrange("p (o c) -> p o c", o=2)
                        if part == 0:
                            step(dve.tensor_tensor(spec[:, :, j, 2, :], src, rk, ALU.mult))
                        dve.tensor_tensor(spec[:, :, j, part, :], src, rk, ALU.mult).then_inc(taken[m % 4], 1)
                wait_taken(dve, m)
                dve.wait_ge(dve_link, links[0])
                w.vec += 1
                dve.sem_inc(vec_ready, 1)
                for o in range(2):
                    w.aux += TB
                    w.m += TB
                    for j in range(TB):
                        a, m = w.small()
                        small_done(a)
                        src = ring[m % 4][:, :].rearrange("p (h c) -> p h c", h=2)
                        if j:
                            dve.wait_ge(vec_ready, w.vec)
                        step(dve.tensor_tensor(prod[0][:, :, :], src, spec[:, o, j, 0:2, :], ALU.mult))
                        dve.tensor_tensor(prod[1][:, :, :], src, spec[:, o, j, 1:3, :], ALU.mult)\
                           .then_inc(taken[m % 4], 1)
                        dve.wait_ge(dve_link, links[0])
                        step(dve.tensor_tensor(y_spec[:, j, 0, :], prod[0][:, 0, :], prod[0][:, 1, :],
                                               ALU.subtract))
                        wait_taken(dve, m)
                        arrived(dve.tensor_tensor(y_spec[:, j, 1, :], prod[1][:, 0, :], prod[1][:, 1, :],
                                                  ALU.add))
                    dve.wait_ge(vec_ready, w.vec)
                    dve.wait_ge(dve_link, links[0])
                    for ch in range(2):
                        a, m = w.small()
                        small_done(a)
                        tmp = prod[ch][:, :, :].rearrange("p h c -> p (h c)")
                        dve.scalar_tensor_tensor(tmp, hy[:, 2 * o + ch, :], c("hy_d", 2 * o + ch),
                                                 ring[m % 4][:, :], ALU.mult, ALU.add).then_inc(taken[m % 4], 1)
                        wait_taken(dve, m)
                        arrived(dve.tensor_tensor(hy[:, 2 * o + 2 + ch, :], tmp, hy[:, 2 * o + 2 + ch, :],
                                                  ALU.mult))
                norm([hm_q[:, 0, :], hm_q[:, 1, :]], lambda k: c("g_q", k), outs=[qn[:, k, :] for k in range(2)])
                norm([hm_q[:, 2, :]], lambda k: c("g_kv", 0), outs=[kvn[:, 0, :]])
                w.loads += 2
                w.aux += TB + HEADS // 2
                w.m += TB + HEADS // 2
                cos, sin = cosq[0:QK, :], sinq[0:QK, :]
                rotate(hm_q[0:QK, 3, :], [(kpe_r[0:QK, :], 0)], cos, sin, QK, T, None)
                prev = None
                for h in range(HEADS + 1):
                    this = None
                    if h < HEADS:
                        this = w.small()[1]
                    if prev is not None:
                        rotate(htmp[(h - 1) % 2][0:QK, :], [(q_all[0:QK, h - 1, :], 0)], cos, sin, QK, T, prev)
                    prev = this
                dve.wait_ge(rope_done, w.rope)
                for h in range(HEADS):
                    ins = dve.tensor_copy(k_all[NOPE:QK, h, :], kpe_r[NOPE:QK, :])
                arrived(ins)

                def take_head(h, src, r0, m):
                    dve.tensor_copy(y_mla[r0:r0 + HD, h // 2, :], src).then_inc(taken[m % 4], 1)

                attention([dict(u, ptbuf=pt) for u in mla_units()], take_head)
                for srcs, a, b in (([y_mla[:, k, :] for k in range(4)], 0, 4),
                                   ([y_conv[:, k, :] for k in range(2)], 4, 6),
                                   ([hy[:, 4 + k, :] for k in range(2)], 6, 8)):
                    norm(srcs, lambda k: c("g_out", a + k), lows=[u_lo[:, k, :] for k in range(a, b)],
                         highs=[u_hi[:, k, :] for k in range(a, b)])
                add_to_x(1.0)

            arrived(dve.memset(ones[:, :], 1.0))
            dve.wait_ge(consts_in, 16 * 3)
            w.loads += 2
            for layer in range(DEPTH):
                norm_x("g_ffn1", layer)
                ffn(PARTS, 2)
                if layer == 0:
                    dve.wait_ge(small_in, 16 * w.loads)
                    ang, n_ = f_a[0:QK, :], f_n[0:QK, :]
                    for j in range(4):
                        wait_taken(dve, w.m - 4 + j)
                    link(dve.tensor_copy(ang, cosq[0:QK, :].bitcast(I32)))
                    link(dve.tensor_scalar(ang, ang, col("invf", None, 0, QK), None, ALU.mult))
                    reduce_angle(ang, n_)
                    arrived(clamp_angle(ang))
                    dve.wait_ge(vec_ready, w.vec)
                    link(dve.scalar_tensor_tensor(n_, ang, -1.0, ang, ALU.mult, ALU.max))
                    arrived(dve.tensor_scalar(n_, n_, -1.0, math.pi / 2, ALU.mult, ALU.add))
                    w.act += 2
                mixer(layer)
                norm_x("g_ffn2", layer)
                ffn(PARTS, 2)
            norm(x_tiles(), lambda c: col("g_final1", None, c), outs=x_tiles())

            norm_x("g_mix2", None)
            w.loads += 1
            w.act += 2
            dve.wait_ge(act_ready, w.act)
            lam = cols[:, places["lam"]:places["lam"] + KC]
            e, s, t_, z, p = (lamt[:, k, :] for k in (1, 2, 3, 4, 5))
            link(dve.tensor_scalar(t_, e, 2.0, None, ALU.add))
            link(dve.reciprocal(t_, t_))
            link(dve.tensor_tensor(s, e, t_, ALU.mult))
            link(dve.tensor_tensor(z, s, s, ALU.mult))
            link(dve.tensor_scalar(p, z, 1.0 / 17, 1.0 / 15, ALU.mult, ALU.add))
            for k in (13, 11, 9, 7, 5, 3, 1):
                link(dve.tensor_tensor(p, p, z, ALU.mult))
                link(dve.tensor_scalar(p, p, 1.0 / k, None, ALU.add))
            link(dve.tensor_tensor(p, p, s, ALU.mult))
            link(dve.tensor_scalar(t_, lam, -1.0, 0.0, ALU.mult, ALU.max))
            link(dve.scalar_tensor_tensor(t_, p, 2.0, t_, ALU.mult, ALU.add))
            link(dve.tensor_scalar(lamt[:, 7, :], t_, 4.0, None, ALU.mult))
            for k in range(2):
                link(dve.memset(xpad[k][:, 0:3], 0.0))
            w.vec += 1
            dve.sem_inc(vec_ready, 1)
            for t in range(KC):
                n, m = w.gemm()
                wait_taken(dve, m)
                src, acc = xpad[t % 2], xc[t % 2]
                link(dve.tensor_scalar(acc[:, :], src[:, 0:T], col("conv_w2", None, 4 * t),
                                       col("conv_b2", None, t), ALU.mult, ALU.add))
                for k in range(1, 4):
                    ins = dve.scalar_tensor_tensor(acc[:, :], src[:, k:k + T], col("conv_w2", None, 4 * t + k),
                                                   acc[:, :], ALU.mult, ALU.add)
                    if k < 3:
                        link(ins)
                    else:
                        arrived(ins)
                w.gemm()
                _, m_g = w.gemm()
                w.small()
                a, m_i = w.small()
                dve.wait_ge(act_ready, w.act + 1)
                link(dve.tensor_scalar(rw[:, :], th[:, :], 1.0, None, ALU.add))
                link(dve.reciprocal(rw[:, :], rw[:, :]))
                link(dve.tensor_scalar(ra[:, :], th[:, :], -1.0, 1.0, ALU.mult, ALU.add))
                link(dve.tensor_tensor(ra[:, :], ra[:, :], rw[:, :], ALU.mult))
                dve.wait_ge(act_ready, w.act + 2)
                link(dve.scalar_tensor_tensor(ru[:, :], sqt[:, :], 2.0, rw[:, :], ALU.mult, ALU.mult))
                wait_taken(dve, m_i)
                link(dve.tensor_tensor(ru[:, :], ru[:, :], isg[:, :], ALU.mult))
                link(dve.tensor_tensor(ru[:, :], ru[:, :], acc[:, :], ALU.mult))
                link(dve.tensor_tensor_scan(rh[:, :], ra[:, :], ru[:, :], 0.0, ALU.mult, ALU.add))
                link(dve.tensor_tensor(rh[:, :], rh[:, :], gel[:, :], ALU.mult))
                wait_taken(dve, m_g)
                arrived(dve.tensor_tensor(y2[:, t, :], rh[:, :], gm1[:, :], ALU.mult))
                w.act += 2
            w.loads += 2
            dve.wait_ge(small_in, 16 * w.loads)
            norm([mem_t[:, k, :] for k in range(KC)], lambda k: col("g_mem", None, k),
                 lows=[mem_lo[:, k, :] for k in range(KC)], highs=[mem_hi[:, k, :] for k in range(KC)], size=MEM)
            w.n += 6
            w.m += 6

            def take_cross(h, src, r0, m):
                dve.tensor_copy(ox[r0:r0 + HD, h // 2, :], src).then_inc(taken[m % 4], 1)

            attention([dict(u, ptbuf=ptx) for u in cross_units()], take_cross)
            for t in range(KC):
                _, m_g = w.gemm()
                a, m = w.small()
                wait_taken(dve, m_g)
                small_done(a)
                dve.tensor_tensor(sq[t % 2][:, :], ring[m % 4][:, :], gm2[t % 2][:, :], ALU.mult)\
                   .then_inc(taken[m % 4], 1)
                wait_taken(dve, m)
                arrived(dve.tensor_tensor(y2[:, t, :], y2[:, t, :], sq[t % 2][:, :], ALU.add))
            w.loads += 3
            dve.wait_ge(small_in, 16 * w.loads)
            prev = None
            for k in range(13):
                this = None
                if k < 12:
                    this = w.gemm()[1]
                if prev is not None:
                    item = k - 1
                    if item < 4:
                        outs = [(k2[HD * half:HD * half + HD, item // 2, 2 * (item % 2) + par, :], HD * par)
                                for par in range(2) for half in range(2)]
                    else:
                        outs = [(q2[:, item - 4, :], 0)]
                    rotate(htmp[item % 2][:, :], outs, cosq[:, :], sinq[:, :], P, T, prev)
                prev = this
            for k in range(5):
                w.gemm()
                w.small()
            w.n += 4 + KC
            w.m += 4 + KC
            gathered = w.m - KC - 1
            wait_taken(dve, w.m - 1)
            for side in range(2):
                w.loads += 5 if side == 0 else 2
                for g in range(GROUPS):
                    src = c_raw[HD * (g % 2):HD * (g % 2) + HD, 2 * side + g // 2, :]
                    step(dve.tensor_copy(c_dup[0:HD, g, :], src))
                    step(dve.tensor_copy(c_dup[HD:P, g, 0:T - 1], src[:, 1:T]))
                dve.wait_ge(dve_link, links[0])
                for i in range(16):
                    ins = dve.tensor_scalar(c_blk[:, i, :, :], c_dup[:, :, 2 * i:2 * i + 16 * (NCMP - 1) + 1:16],
                                            col(("pos_k", "pos_v")[side], None, i), None, ALU.add)
                arrived(ins)
                w.aux += 3
                w.m += 3
                m_raw = w.m - 1
                if side == 0:
                    dve.wait_ge(small_in, 16 * w.loads)
                    flat = GROUPS * NCMP
                    rotate(htmp[0][0:HD, 0:flat],
                           [(k_cmp[HD * half:HD * half + HD, :, :].rearrange("p g n -> p (g n)"), 0)
                            for half in range(2)], cos_c[:, 0, :], cos_c[:, 1, :], HD, flat, m_raw)
            wait_taken(dve, m_raw)

            def take_nsa(h, src, r0, m):
                tmp = sq[0][r0:r0 + HD, :]
                part = y2[r0:r0 + HD, h // 2, :]
                link(dve.tensor_tensor(tmp, src, gm0[r0:r0 + HD, h // 2, :], ALU.mult))
                dve.tensor_tensor(part, part, tmp, ALU.add).then_inc(taken[m % 4], 1)
                wait_taken(dve, m)

            attention([dict(u, ptbuf=pt2) for u in nsa_units()], take_nsa)
            for c in range(KC):
                dve.wait_ge(u_hi_ready, w.split + 1)
                dve.tensor_tensor(u_lo[:, c, :], y2[:, c, :], u_hi[:, c, :].bitcast(F32),
                                  ALU.subtract).then_inc(u_ready, 1)
                w.split += 1
            add_to_x(1.0)
            norm_x("g_mlp", None)
            ffn(PARTS2, 1)
            norm(x_tiles(), lambda c: col("g_final2", None, c), outs=[out_t[:, c, :] for c in range(KC)],
                 signal=out_ready)
    return nc


def _blocks(w, k):
    n = w.shape[1] // P
    return w.reshape(k, P, n, P).transpose(2, 1, 0, 3).reshape(n, P, k * P)


def _rows(v):
    return np.ascontiguousarray(v).reshape(-1, P).T


def _pad_rows(v):
    out = np.zeros((P, v.shape[1]), np.float32)
    out[:v.shape[0]] = v
    return out


def shape_constants():
    f = np.float32
    k = {"ident": np.eye(P, dtype=f)}
    rot1 = np.zeros((P, P), f)
    half = ROPE // 2
    for j in range(half):
        rot1[NOPE + half + j, NOPE + j] = -1
        rot1[NOPE + j, NOPE + half + j] = 1
    k["rot1"] = rot1
    rot2 = np.zeros((P, P), f)
    for h in range(2):
        for j in range(8):
            rot2[HD * h + 8 + j, HD * h + j] = -1
            rot2[HD * h + j, HD * h + 8 + j] = 1
    k["rot2"] = rot2
    inv2 = (f(1.0) / (f(500000.0) ** (np.arange(0, 16, 2, dtype=f) / f(16)))).astype(f)

    def tables(pos, rows):
        ang = (inv2[:, None] * pos[None, :].astype(f)).astype(f).astype(np.float64)
        c = np.ones((HD, len(pos)))
        s = np.zeros((HD, len(pos)))
        c[0:16] = np.tile(np.cos(ang), (2, 1))
        s[0:16] = np.tile(np.sin(ang), (2, 1))
        return np.tile(c, (rows // HD, 1)).astype(f), np.tile(s, (rows // HD, 1)).astype(f)

    k["cos2"], k["sin2"] = tables(np.arange(T), P)
    cc, sc = tables(np.arange(NCMP) * 16 + 31, HD)
    k["cos_c"] = np.stack([np.tile(cc, (1, GROUPS)), np.tile(sc, (1, GROUPS))], 1)
    ang = 2 * np.pi * np.outer(np.arange(T), np.arange(T) + 0.5) / (2 * T)
    cs = np.stack([np.cos(ang), np.sin(ang)])
    k["dft"] = cs.reshape(2, TB, P, T).transpose(2, 0, 1, 3).astype(f)
    k["idft"] = (cs.transpose(0, 2, 1) / T).reshape(2, TB, P, T).transpose(2, 0, 1, 3).astype(f)
    t = np.linspace(0.0, 1.0, T, dtype=f)[:, None]
    bands = (EMB - 1) // 2
    ang = (f(2.0 * math.pi) * np.arange(T, dtype=f)[:, None] / f(T)).astype(f)
    fb = np.linspace(1e-4, bands - 1, bands, dtype=f)[None, :]
    a = (fb * ang).astype(f).astype(np.float64)
    k["f_z"] = np.concatenate([t, np.cos(a), -np.sin(a)], 1).T.astype(f)
    deltas = np.linspace(math.log(1e-2) / 1.5, math.log(1e-2) / 0.3, HYC, dtype=f)
    win = np.exp((-t * np.abs(deltas)).astype(np.float64))
    back = win.copy()
    back[0] = 0.0
    k["decay"] = np.concatenate([win, back], 1).reshape(TB, P, T).transpose(1, 0, 2).astype(f)
    q = np.arange(T)
    end = np.arange(NCMP) * 16 + 31
    k["cmask"] = np.where(end[None, :] <= q[:, None], 0.0, NEG).reshape(TB, P, NCMP).transpose(1, 0, 2).astype(f)
    k["causal"] = np.where(np.arange(P)[None, :] <= np.arange(P)[:, None], 0.0, NEG).astype(f)
    return {n: np.ascontiguousarray(v) for n, v in k.items()}


def layout(a):
    k = shape_constants()
    w = {8: [], 10: [], 12: []}

    def ffn(i, name):
        gate, up, down = (a[f"{name}_w_{x}"][i] for x in ("gate", "up", "down"))
        first = 0
        for part in PARTS:
            c = slice(P * first, P * (first + part))
            pair = np.stack([_blocks(gate[:, c], KC), _blocks(up[:, c], KC)], 1)
            w[8].append(pair.reshape(2 * part, P, D))
            w[part].append(_blocks(down[c], part))
            first += part

    for i in range(DEPTH):
        ffn(i, "ffn1")
        w_in = a["w_in"][i]
        key = np.zeros((D, P), np.float32)
        key[:, NOPE:QK] = w_in[:, QRANK + KVRANK:QRANK + KVRANK + ROPE]
        w[8].append(_blocks(np.concatenate([w_in[:, 0:QRANK + KVRANK], key,
                                            w_in[:, QRANK + KVRANK + ROPE:]], 1), KC))
        w[8].append(_blocks(a["w_out"][i], KC))
        ffn(i, "ffn2")
    z = a["w_in_2"][0]
    ends = np.cumsum([0, 1024, 256, 256, 256, 256, 256, 256, 48, 1024, 1024, 256, 3072])
    q, kc, vc, ks, vs, kw, vw, ng, xr, gr, qx, mg = (z[:, s:e] for s, e in zip(ends[:-1], ends[1:]))
    trio = np.stack([_blocks(v, KC) for v in (xr, gr, mg[:, D:2 * D])], 1)
    w[8].append(trio.reshape(3 * KC, P, D))
    w[8].append(_blocks(a["w_mem_kv_2"][0], KC))
    w[8].append(_blocks(qx, KC))
    w[8].append(_blocks(mg[:, 2 * D:], KC))
    gate_cols = np.zeros((D, P), np.float32)
    gate_cols[:, 0:48] = ng
    for v in (ks, kw, q, vs, vw, gate_cols, kc, vc, mg[:, 0:D], a["w_o_2"][0]):
        w[8].append(_blocks(v, KC))
    first = 0
    for part in PARTS2:
        c = slice(P * first, P * (first + part))
        w[8].append(_blocks(a["w_up_2"][0][:, c], KC))
        w[part].append(_blocks(a["w_down_2"][0][c], part))
        first += part
    for n, v in w.items():
        k[f"w{n}"] = np.concatenate(v, 0)

    cols = []
    for i in range(DEPTH):
        conv = a["conv_dw_w"][i].reshape(TAPS, 2, P).transpose(2, 1, 0).reshape(P, 2 * TAPS)
        short = a["hy_short_w"][i].reshape(3, 6, P).transpose(2, 1, 0).reshape(P, 18)
        biases = np.stack([a[f"hy_filt_b{j}"][i] for j in (1, 2, 3)], 1)
        cols += [_rows(a["ffn1_norm"][i]), _rows(a["mix_norm"][i]), _rows(a["mla_q_norm"][i]),
                 _rows(a["mla_kv_norm"][i]), conv, _rows(a["conv_dw_b"][i]), _rows(a["conv_ln_g"][i]),
                 _rows(a["conv_ln_b"][i]), short, _rows(a["hy_short_b"][i]), _pad_rows(biases),
                 _pad_rows(a["hy_filt_freq"][i][:, None]), _rows(a["hy_bias_d"][i]), _rows(a["out_norm"][i]),
                 _rows(a["ffn2_norm"][i])]
    conv2 = a["conv_w_2"][0].reshape(4, KC, P).transpose(2, 1, 0).reshape(P, 4 * KC)
    tok = np.arange(T)
    invf = np.zeros((P, 1), np.float32)
    f = np.float32
    inv = f(1.0) / (f(10000.0) ** (np.arange(0, ROPE, 2, dtype=f) / f(ROPE)))
    invf[NOPE:QK, 0] = np.tile(inv, 2)
    cols += [_rows(a["final_norm"]), _rows(a["g_mix_2"][0]), conv2, _rows(a["conv_b_2"][0]),
             _rows(a["b_rg_a_2"][0]), _rows(a["b_rg_i_2"][0]), _rows(a["rg_lambda_2"][0]),
             _rows(a["g_mem_2"][0]), _rows(a["g_mlp_2"][0]), _rows(a["g_final_2"]),
             _rows(a["cmp_pos_k_2"][0]), _rows(a["cmp_pos_v_2"][0]), np.full((P, 1), EPS, f),
             (T - 1 - tok).reshape(TB, P).T.astype(f),
             np.where(tok < T - 1, 0.0, NEG).reshape(TB, P).T.astype(f), invf]
    k["cols"] = np.concatenate(cols, 1)

    k["xt"] = np.ascontiguousarray(a["x"][0].reshape(T, KC, P).transpose(2, 1, 0))
    k["positions"] = np.ascontiguousarray(np.broadcast_to(a["positions"], (QK, T)))
    k["f_w1"] = a["hy_filt_w1"]
    k["f_w23"] = np.stack([a["hy_filt_w2"], a["hy_filt_w3"]], 2)
    k["f_w4"] = a["hy_filt_w4"]
    k["w_qb"] = a["mla_w_qb"].reshape(DEPTH, 2, P, HEADS * QK).transpose(0, 2, 1, 3)
    k["w_kvb"] = a["mla_w_kvb"].reshape(DEPTH, P, HEADS, 2, VDIM).transpose(0, 1, 3, 2, 4).reshape(DEPTH, P, 2, T)
    ra = np.zeros((P, 2, KC, P), f)
    for j, name in enumerate(("w_rg_a_2", "w_rg_i_2")):
        for t in range(KC):
            for b in range(2):
                s = slice(64 * b, 64 * b + 64)
                ra[s, j, t, s] = a[name][0, 2 * t + b]
    k["w_ra"] = ra
    k["mem_t"] = a["mem_2"][0].reshape(MEM, KC, P).transpose(2, 1, 0)
    k["w_xo"] = a["w_xo_2"][0].reshape(2, P, D).transpose(1, 0, 2)
    k["w_c1"] = np.stack([a[f"w_cmp_{s}1_2"][0].reshape(16, P, 256).transpose(1, 0, 2) for s in "kv"])
    k["w_c2"] = np.stack([a[f"w_cmp_{s}2_2"][0].reshape(2, P, HD).transpose(1, 0, 2) for s in "kv"])
    return {n: np.ascontiguousarray(v) for n, v in k.items()}


def kernel(**inputs):
    import concourse.bacc as bacc
    from concourse.bass_utils import run_bass_kernel_spmd

    arrays = layout({n: np.asarray(v) for n, v in inputs.items()})
    nc = bacc.Bacc("TRN2", target_bir_lowering=False, num_devices=1)
    d = {n: nc.dram_tensor(f"in_{n}", v.shape, mybir.dt.from_np(v.dtype), kind="ExternalInput").ap()
         for n, v in arrays.items()}
    d["out"] = nc.dram_tensor("out", (P, KC, T), F32, kind="ExternalOutput").ap()
    build(nc, d)
    r = run_bass_kernel_spmd(nc, [{f"in_{n}": v for n, v in arrays.items()}], core_ids=[0])
    y = r.results[0]["out"]
    return np.ascontiguousarray(y.transpose(2, 1, 0)).reshape(1, T, D)
```

```python
import math
from contextlib import ExitStack

import numpy as np
import concourse.bass as bass
from concourse import mybir

F32 = mybir.dt.float32
F32R = mybir.dt.float32r
I32 = mybir.dt.int32
ALU = mybir.AluOpType
ACT = mybir.ActivationFunctionType
AX = mybir.AxisListType

P = 128
T = 512
TB = T // P
D = 1024
KC = D // P
F = 2816
PARTS = (12, 10)
DEPTH = 2
EPS = 1e-6

HEADS, NOPE, ROPE, VDIM = 8, 64, 32, 64
QK = NOPE + ROPE
QRANK, KVRANK = 256, 128
TAPS = 31
CONVC = 256
HYC = 256
HYF = 64
EMB = 33

MEM = 256
HEADS2, GROUPS = 16, 4
HD = 64
NCMP = (T - 32) // 16 + 1
CPAD = 32
XHEADS = 4
PARTS2 = (12, 12, 8)

RING = 4
SPLIT = 2
SLOT = 12 * P
MAGIC = 1.5 * 2.0 ** 23
TWO_PI = (6.28125, 1.93500518798828125e-3, 3.0199159819567e-7)
NEG = -1e30
FLOOR = -1e29

LAYER_COLS = [("g_ffn1", 8), ("g_mix", 8), ("g_q", 2), ("g_kv", 1), ("conv_w", 2 * TAPS), ("conv_b", 2),
              ("ln_g", 2), ("ln_b", 2), ("short_w", 18), ("short_b", 6), ("fb", 3), ("freq", 1),
              ("hy_d", 4), ("g_out", 8), ("g_ffn2", 8)]
LAST_COLS = [("g_final1", 8), ("g_mix2", 8), ("conv_w2", 32), ("conv_b2", 8), ("b_a", 8), ("b_i", 8),
             ("lam", 8), ("g_mem", 8), ("g_mlp", 8), ("g_final2", 8), ("pos_k", 16), ("pos_v", 16),
             ("eps", 1), ("npad", 4), ("padfloor", 4), ("invf", 1)]


def column_places():
    at, places = 0, {}
    for layer in range(DEPTH):
        for name, n in LAYER_COLS:
            places[name, layer] = at
            at += n
    for name, n in LAST_COLS:
        places[name] = at
        at += n
    return places, at


def stream():
    first = {8: 0, 10: 0, 12: 0}
    out = []

    def add(k, n):
        out.append((k, first[k], n))
        first[k] += n

    def ffn(parts, per):
        for part in parts:
            add(8, per * part)
            add(part, 8)

    for _ in range(DEPTH):
        ffn(PARTS, 2)
        add(8, 14)
        add(8, 8)
        ffn(PARTS, 2)
    add(8, 24)
    add(8, 6)
    add(8, 8)
    add(8, 21)
    add(8, 8)
    add(8, 8)
    ffn(PARTS2, 1)
    return out, first


class Walk:

    def __init__(self):
        self.n = self.m = self.aux = self.sq = self.norm = self.full = self.split = 0
        self.tables = self.hid = self.rope = self.unit = self.part = self.item = self.vec = self.act = self.loads = 0

    def gemm(self):
        self.n += 1
        self.m += 1
        return self.n - 1, self.m - 1

    def small(self):
        self.aux += 1
        self.m += 1
        return self.aux - 1, self.m - 1

    def bank(self):
        self.m += 1
        return self.m - 1


def at_turn(base, per, i):
    return base if i is None else i * per + base


def build(nc, d):
    places, ncols = column_places()
    plan, _ = stream()
    ctx = ExitStack()
    with ctx:
        base0 = (nc.sbuf_base + 31) // 32 * 32

        def place(name, shape, dt, at):
            return nc.alloc_sbuf_tensor_at(name, shape, dt, offset=base0 + at)

        K1 = 1024
        KB2 = T * 4
        X_AT, U_AT, RING_AT = 0, 16 * K1, 48 * K1
        H_AT = 96 * K1
        TMP_AT = 144 * K1
        ROPE_AT = 166 * K1
        SMALL_AT = 170 * K1
        x = place("x", [P, KC, T], F32, X_AT)
        u_hi = place("u_hi", [P, KC, T], F32R, U_AT)
        u_lo = place("u_lo", [P, KC, T], F32R, U_AT + 16 * K1)
        w_raw = [place(f"w_raw{i}", [P, SLOT], F32, RING_AT + i * SLOT * 4) for i in range(RING)]
        w_hi = [place(f"w_hi{i}", [P, SLOT], F32R, RING_AT + (4 + i) * SLOT * 4) for i in range(SPLIT)]
        w_lo = [place(f"w_lo{i}", [P, SLOT], F32R, RING_AT + (6 + i) * SLOT * 4) for i in range(SPLIT)]
        h_hi = place("h_hi", [P, 12, T], F32R, H_AT)
        h_lo = place("h_lo", [P, 12, T], F32R, H_AT + 24 * K1)
        sq = [place(f"sq{i}", [P, T], F32, TMP_AT + i * KB2) for i in range(2)]
        std = place("std", [P, T], F32, TMP_AT + 2 * KB2)
        rinv = place("rinv", [P, T], F32, TMP_AT + 3 * KB2)
        full = [place(f"full{i}", [P, T], F32, TMP_AT + (4 + i) * KB2) for i in range(3)]
        sg = [place(f"sg{i}", [P, T], F32, TMP_AT + (7 + i) * KB2) for i in range(2)]
        htmp = [place(f"htmp{i}", [P, T], F32, TMP_AT + (9 + i) * KB2) for i in range(2)]
        cosq = place("cosq", [P, T], F32, ROPE_AT)
        sinq = place("sinq", [P, T], F32, ROPE_AT + KB2)
        cols = place("cols", [P, ncols], F32, SMALL_AT)
        at = SMALL_AT + (ncols * 4 + 31) // 32 * 32
        ident = place("ident", [P, P], F32, at)
        ones = place("ones", [P, P], F32, at + 512)
        rot = place("rot", [P, P], F32, at + 1024)
        mx, nb, sums, e0, ri = (place(name, [P, 8, 8], F32, at + 1536 + 256 * k)
                                for k, name in enumerate(("mx", "nb", "sums", "e0", "ri")))
        assert at + 1536 + 5 * 256 <= 175 * K1
        R_AT = 175 * K1

        def mid(name, shape, at, dt=F32):
            return place(name, shape, dt, at)

        hm_q = mid("hm_q", [P, 4, T], R_AT)
        a_in = mid("a_in", [P, 2, T], R_AT + 8 * K1)
        g_sig = mid("g_sig", [P, 2, T], R_AT + 12 * K1)
        y_mla = mid("y_mla", [P, 4, T], R_AT + 8 * K1)
        hy = mid("hy", [P, 6, T], R_AT + 16 * K1)
        y_conv = mid("y_conv", [P, 2, T], R_AT + 28 * K1)
        PADW = T + TAPS - 1
        conv_pad = mid("conv_pad", [P, 2, PADW], H_AT)
        conv_acc = mid("conv_acc", [P, 2, T], H_AT + 5 * K1)
        conv_c = mid("conv_c", [P, 2, T], H_AT + 9 * K1)
        f_w1 = mid("f_w1", [EMB, HYF], H_AT)
        f_w23 = mid("f_w23", [HYF, 2, HYF], H_AT + 256)
        f_w4 = mid("f_w4", [HYF, 1024], H_AT + 1 * K1)
        f_z = mid("f_z", [EMB, T], H_AT + 5 * K1)
        f_h = [mid(f"f_h{i}", [HYF, T], H_AT + (7 + 2 * i) * K1) for i in range(2)]
        f_n = mid("f_n", [P, T], H_AT + 11 * K1)
        f_a = mid("f_a", [P, T], H_AT + 13 * K1)
        f_abs = [mid(f"f_abs{i}", [P, T], H_AT + (15 + 2 * i) * K1) for i in range(2)]
        spec = mid("spec", [P, 2, 4, 3, HYC], H_AT)
        dft = mid("dft", [P, 2, TB, T], H_AT + 24 * K1)
        decay = mid("decay", [P, TB, T], H_AT + 40 * K1)
        filt = mid("filt", [P, 2, TB, 2, HYC], U_AT)
        fsum = mid("fsum", [P, TB, 2, HYC], U_AT + 16 * K1)
        fdif = mid("fdif", [P, TB, 2, HYC], U_AT + 24 * K1)
        idft = mid("idft", [P, 2, TB, T], U_AT)
        v_tok = mid("v_tok", [P, TB, HYC], U_AT + 16 * K1)
        y_spec = mid("y_spec", [P, TB, 2, HYC], U_AT + 20 * K1)
        prod = [mid(f"prod{i}", [P, 2, HYC], U_AT + (28 + 2 * i) * K1) for i in range(2)]
        qn = mid("qn", [P, 2, T], H_AT)
        kvn = mid("kvn", [P, 1, T], H_AT + 4 * K1)
        q_all = mid("q_all", [P, HEADS, T], H_AT + 6 * K1)
        k_all = mid("k_all", [P, HEADS, T], H_AT + 22 * K1)
        v_all = mid("v_all", [P, TB, T], H_AT + 38 * K1)
        kpe_r = mid("kpe_r", [P, T], H_AT + 46 * K1)
        w_qb = mid("w_qb", [P, 2, HEADS * QK], U_AT)
        w_kvb = mid("w_kvb", [P, 2, T], U_AT + 6 * K1)
        pt = [mid(f"pt{i}", [P, 1, TB, P], U_AT + 2 * i * K1) for i in range(2)]
        y2 = mid("y2", [P, KC, T], R_AT)
        gm0 = mid("gm0", [P, KC, T], R_AT + 16 * K1)
        w_ra = mid("w_ra", [P, 2, KC, P], H_AT)
        xpad = [mid(f"xpad{i}", [P, T + 3], H_AT + 8 * K1 + i * 2080) for i in range(2)]
        xc = [mid(f"xc{i}", [P, T], H_AT + (13 + 2 * i) * K1) for i in range(2)]
        rs = mid("rs", [P, T], H_AT + 17 * K1)
        isg = mid("isg", [P, T], H_AT + 19 * K1)
        th = mid("th", [P, T], H_AT + 21 * K1)
        sqt = mid("sqt", [P, T], H_AT + 23 * K1)
        gel = mid("gel", [P, T], H_AT + 25 * K1)
        gm1 = mid("gm1", [P, T], H_AT + 27 * K1)
        rw = mid("rw", [P, T], H_AT + 29 * K1)
        ra = mid("ra", [P, T], H_AT + 31 * K1)
        ru = mid("ru", [P, T], H_AT + 33 * K1)
        rh = mid("rh", [P, T], H_AT + 35 * K1)
        lamt = mid("lamt", [P, 8, KC], H_AT + 37 * K1)
        mem_t = mid("mem_t", [P, KC, MEM], H_AT)
        mem_hi = mid("mem_hi", [P, KC, MEM], H_AT + 8 * K1, F32R)
        mem_lo = mid("mem_lo", [P, KC, MEM], H_AT + 16 * K1, F32R)
        kx = mid("kx", [P, 2, MEM], H_AT + 24 * K1)
        vx = mid("vx", [P, 2, MEM], H_AT + 26 * K1)
        qx = mid("qx", [P, 2, T], H_AT + 28 * K1)
        ox = mid("ox", [P, 2, T], H_AT + 32 * K1)
        w_xo = mid("w_xo", [P, 2, D], H_AT + 36 * K1)
        gm2 = [mid(f"gm2{i}", [P, T], H_AT + (44 + 2 * i) * K1) for i in range(2)]
        ptx = [mid(f"ptx{i}", [P, 1, TB, P], R_AT + (16 + 2 * i) * K1) for i in range(2)]
        q2 = mid("q2", [P, KC, T], H_AT)
        k2 = mid("k2", [P, 2, GROUPS, T], H_AT + 16 * K1)
        v2 = mid("v2", [P, 2, TB, 2, P], H_AT + 32 * K1)
        c_raw = mid("c_raw", [P, 4, T], H_AT + 40 * K1)
        w_c1 = mid("w_c1", [P, 16, 256], U_AT)
        c_dup = mid("c_dup", [P, GROUPS, T], U_AT + 16 * K1)
        c_blk = mid("c_blk", [P, 16, GROUPS, NCMP], U_AT + 24 * K1)
        c_hid = mid("c_hid", [P, 2, GROUPS * NCMP], TMP_AT + 7 * KB2)
        w_c2 = mid("w_c2", [P, 2, HD], TMP_AT + 8 * KB2)
        prob2 = [mid(f"prob2{i}", [P, 2, T], U_AT + 4 * i * K1) for i in range(4)]
        pt2 = [mid(f"pt2{i}", [P, 2, TB, P], H_AT + (40 + 4 * i) * K1) for i in range(2)]
        k_cmp = mid("k_cmp", [P, GROUPS, 2, CPAD], TMP_AT + 10 * KB2)
        v_cmp = mid("v_cmp", [2 * CPAD, GROUPS, 2, HD], TMP_AT + 2 * KB2)
        gates = mid("gates", [P, TB, 48], TMP_AT + 3 * KB2)
        cmask = mid("cmask", [P, TB, CPAD], TMP_AT + 3 * KB2 + 768)
        causal = mid("causal", [P, P], TMP_AT + 3 * KB2 + 1280)
        cos_c = mid("cos_c", [HD, 2, GROUPS * NCMP], TMP_AT + 8 * KB2 + 768)

        out_t = mid("out_t", [P, KC, T], H_AT)

        psum = ctx.enter_context(nc.psum_tensor("psum", [P, 8 * T], F32))
        banks = [psum[:, T * i:T * i + T] for i in range(8)]
        ring = banks[0:4]
        score = [psum[:, T * i:T * i + 2 * T].rearrange("p (b n) -> p b n", b=2) for i in (4, 2)]
        product = banks[0:2]
        turned = banks[6:8]

        def sem(name):
            return ctx.enter_context(nc.semaphore(name))

        w_loaded = [sem(f"w_loaded{i}") for i in range(RING)]
        w_hi_ready = sem("w_hi_ready")
        w_split = sem("w_split")
        gemm_done = sem("gemm_done")
        aux_done = sem("aux_done")
        taken = [sem(f"taken{i}") for i in range(4)]
        sq_ready = sem("sq_ready")
        sq_used = sem("sq_used")
        rinv_ready = sem("rinv_ready")
        u_full = sem("u_full")
        u_hi_ready = sem("u_hi_ready")
        u_ready = sem("u_ready")
        h_hi_ready = sem("h_hi_ready")
        h_ready = sem("h_ready")
        dve_link = sem("dve_link")
        vec_ready = sem("vec_ready")
        act_ready = sem("act_ready")
        rope_done = sem("rope_done")
        s_full = sem("s_full")
        s_max = sem("s_max")
        exp_done = sem("exp_done")
        p_norm = sem("p_norm")
        t_full = sem("t_full")
        t_taken = sem("t_taken")
        pv_done = sem("pv_done")
        o_taken = sem("o_taken")
        consts_in = sem("consts_in")
        small_in = sem("small_in")
        tables_in = sem("tables_in")
        out_ready = sem("out_ready")
        pool_tick = sem("pool_tick")
        act_tick = sem("act_tick")
        out_written = sem("out_written")

        block = ctx.enter_context(nc.Block())

        def col(name, layer, k, rows=P):
            c = places[(name, layer) if layer is not None else name] + k
            return cols[0:rows, c:c + 1]

        def wait_taken(eng, m, i=None):
            eng.wait_ge(taken[m % 4], at_turn(m // 4 + 1, 1, i))

        def weights(n, k):
            hi = w_hi[n % SPLIT][:, 0:k * P].rearrange("p (k n) -> p k n", n=P)
            lo = w_lo[n % SPLIT][:, 0:k * P].rearrange("p (k n) -> p k n", n=P)
            return hi, lo

        ORDER = range(TB)
        KEEP = [full[0], full[1], full[2], sg[0]]

        def unit(**kw):
            kw["rows"] = slice(0, P) if kw["kind"] == "cmp" else \
                slice(HD * (kw["head"] % 2), HD * (kw["head"] % 2) + HD)
            kw["closes"] = kw["kind"] == "cmp" or kw["head"] % 2 == 1 and kw["i"] == ORDER[-1]
            kw["opens"] = kw["kind"] == "cmp" or kw["head"] % 2 == 0 and kw["i"] == ORDER[0]
            kw["chunks"] = [(t, 2 * CPAD) for t in range(TB)] if kw["kind"] == "cmp" else \
                [(c, P) for c in range(kw["n"] // P)]
            return kw

        def mla_units():
            return [unit(head=h, i=i, kind="plain", scale=QK ** -0.5, n=T, keep=KEEP, pt=pt,
                         qk=[(0, q_all[0:QK, h, P * i:P * i + P], k_all[0:QK, h, :])],
                         v=[[v_all[:, j, VDIM * h:VDIM * h + VDIM] for j in range(TB)]])
                    for h in range(HEADS) for i in ORDER]

        def cross_units():
            return [unit(head=h, i=i, kind="plain", scale=HD ** -0.5, n=MEM, keep=KEEP, pt=ptx,
                         qk=[(0, qx[HD * (h % 2):HD * (h % 2) + HD, h // 2, P * i:P * i + P],
                              kx[HD * (h % 2):HD * (h % 2) + HD, h // 2, :])],
                         v=[[vx[:, j, HD * h:HD * h + HD] for j in range(MEM // P)]])
                    for h in range(XHEADS) for i in ORDER]

        def nsa_units(compressed):
            out = []
            for h in range(HEADS2):
                g = h // (HEADS2 // GROUPS)
                r = slice(HD * (h % 2), HD * (h % 2) + HD)
                q = [q2[r, h // 2, P * i:P * i + P] for i in range(TB)]
                if compressed:
                    if h % 2 == 0:
                        out.append(unit(head=h, i=None, kind="cmp", scale=HD ** -0.5, n=None, keep=prob2, pt=pt2,
                                        qk=[(i, q2[:, h // 2, P * i:P * i + P],
                                             k_cmp[:, g, :, :].rearrange("p e n -> p (e n)")) for i in range(TB)],
                                        v=[v_cmp[:, g, :, :].rearrange("p e c -> p (e c)")],
                                        gate=gates[:, :, 3 * h:3 * h + 6]
                                        .rearrange("p t (e k) -> p t e k", k=3)[:, :, :, 0]))
                    continue
                for i in ORDER:
                    n = P * (i + 1)
                    out.append(unit(head=h, i=i, kind="pair", scale=HD ** -0.5, n=n, keep=prob2, pt=pt2,
                                    qk=[(b, q[i], k2[r, b, g, 0:n]) for b in range(2)],
                                    v=[[v2[:, b, j, g // 2, HD * (g % 2):HD * (g % 2) + HD]
                                        for j in range(i + 1)] for b in range(2)],
                                    gate=gates[:, i, 3 * h + 1:3 * h + 3]))
            return out

        def parts_of(units, s):
            return sum(len(u["v"]) for u in units[0:max(s, 0)])

        TURN, VALUES = 3, 4

        @block.sync
        def _(sp):
            sp.dma_start(x[:, :, :], d["xt"]).then_inc(consts_in, 16)
            sp.dma_start(cols[:, :], d["cols"]).then_inc(consts_in, 16)
            sp.dma_start(ident[:, :], d["ident"]).then_inc(consts_in, 16)
            n = 0
            for k, first, count in plan:
                src = d[f"w{k}"]

                def load(j, i=None):
                    slot = (n + j) % RING
                    if i is not None or n + j >= RING:
                        sp.wait_ge(w_split, at_turn(n + j - RING + 1, RING, i))
                    index = first + j if i is None else i * RING + (first + j)
                    block_ = src[bass.ds(index, 1)].rearrange("o p f -> (o p) f")
                    sp.dma_start(w_raw[slot][:, 0:k * P], block_).then_inc(w_loaded[slot], 16)

                if count % RING:
                    for j in range(count):
                        load(j)
                else:
                    for j in range(RING):
                        load(j)
                    with sp.Fori(1, count // RING) as i:
                        for j in range(RING):
                            load(j, i)
                n += count
            for c in range(KC):
                sp.wait_ge(out_ready, c + 1)
                sp.dma_start(d["out"][:, c, :], out_t[:, c, :]).then_inc(out_written, 16)
            sp.wait_ge(out_written, 16 * KC)

        @block.gpsimd
        def _(pool):
            n = 0
            for k, first, count in plan:
                def split(j, i=None):
                    m = n + j
                    raw = w_raw[m % RING][:, 0:k * P]
                    hi = w_hi[m % SPLIT][:, 0:k * P]
                    lo = w_lo[m % SPLIT][:, 0:k * P]
                    pool.wait_ge(w_loaded[m % RING], at_turn(16 * (m // RING + 1), 16, i))
                    if i is not None:
                        pool.sem_inc(pool_tick, 1)
                    if i is not None or m >= SPLIT:
                        pool.wait_ge(gemm_done, at_turn(m - SPLIT + 1, RING, i))
                        if i is not None:
                            pool.sem_inc(pool_tick, 1)
                    pool.tensor_scalar(hi, raw, 1.0, 1.0, ALU.mult, ALU.mult).then_inc(w_hi_ready, 1)
                    pool.wait_ge(w_hi_ready, at_turn(m + 1, RING, i))
                    pool.tensor_tensor(lo, raw, hi.bitcast(F32), ALU.subtract).then_inc(w_split, 1)

                if count % RING:
                    for j in range(count):
                        split(j)
                else:
                    for j in range(RING):
                        split(j)
                    with pool.Fori(1, count // RING) as i:
                        for j in range(RING):
                            split(j, i)
                n += count

        @block.tensor
        def _(pe):
            w = Walk()

            def open_bank(m, i=None):
                if i is not None or m >= 4:
                    pe.wait_ge(taken[m % 4], at_turn(m // 4, 1, i))
                return ring[m % 4]

            def multiply(n, out, k, rhs_hi, rhs_lo, i=None, ready=None):
                pe.wait_ge(w_split, at_turn(n + 1, RING, i))
                hi, lo = weights(n, k)
                for c in range(k):
                    if ready is not None:
                        ready(c)
                    pe.matmul(out, hi[:, c, :], rhs_hi(c), start=(c == 0), stop=False)
                    pe.matmul(out, hi[:, c, :], rhs_lo(c), start=False, stop=False)
                    mm = pe.matmul(out, lo[:, c, :], rhs_hi(c), start=False, stop=(c == k - 1))
                mm.then_inc(gemm_done, 1)

            def of_u(ready=None):
                n, m = w.gemm()
                multiply(n, open_bank(m)[:, :], KC, lambda c: u_hi[:, c, :], lambda c: u_lo[:, c, :],
                         ready=ready)

            def u_arrives(c):
                pe.wait_ge(u_ready, w.split - KC + c + 1)

            def norm(tiles, size=T, split=True):
                m = w.bank()
                out = open_bank(m)
                for c in range(tiles):
                    pe.wait_ge(sq_ready, w.sq + 1)
                    pe.matmul(out[:, 0:size], ones[:, :], sq[w.sq % 2][:, 0:size], start=(c == 0),
                              stop=(c == tiles - 1)).then_inc(sq_used, 1)
                    w.sq += 1
                w.full += tiles
                w.norm += 1
                if split:
                    w.split += tiles

            def looped(count, body):
                for j in range(4):
                    body(j, None)
                with pe.Fori(1, count // 4) as i:
                    for j in range(4):
                        body(j, i)
                w.n += count
                w.m += count

            def ffn(parts, per):
                for p, part in enumerate(parts):
                    def up(j, i):
                        ready = u_arrives if i is None and j == 0 and p == 0 else None
                        multiply(w.n + j, open_bank(w.m + j, i)[:, :], KC, lambda c: u_hi[:, c, :],
                                 lambda c: u_lo[:, c, :], i, ready)

                    looped(per * part, up)

                    def down(j, i):
                        ready = (lambda c: pe.wait_ge(h_ready, w.hid + c + 1)) if i is None and j == 0 else None
                        multiply(w.n + j, open_bank(w.m + j, i)[:, :], part, lambda c: h_hi[:, c, :],
                                 lambda c: h_lo[:, c, :], i, ready)

                    looped(8, down)
                    w.hid += part

            def attention(units):
                u0, p0 = w.unit, w.part
                for m in range(w.m - 4, w.m):
                    wait_taken(pe, m)
                for s in range(len(units) + VALUES):
                    if s < len(units):
                        u = units[s]
                        if s >= 2:
                            pe.wait_ge(exp_done, p0 + parts_of(units, s - 1))
                        for b, q, key in u["qk"]:
                            out = score[s % 2][:, 0, 2 * CPAD * b:2 * CPAD * (b + 1)] if u["kind"] == "cmp" else \
                                score[s % 2][:, b, 0:u["n"]]
                            mm = pe.matmul(out, q, key, start=True, stop=True, skip_group_check=True)
                        mm.then_inc(s_full, 1)
                    if 0 <= s - TURN < len(units):
                        u, k = units[s - TURN], u0 + s - TURN
                        p = p0 + parts_of(units, s - TURN)
                        keep = u["keep"][k % 4]
                        for b in range(len(u["v"])):
                            pe.wait_ge(p_norm, p + b + 1)
                            if p + b >= 2:
                                pe.wait_ge(t_taken, p + b - 1)
                            for c, rows in u["chunks"]:
                                if u["kind"] == "plain":
                                    src = keep[:, P * c:P * c + P]
                                elif u["kind"] == "pair":
                                    src = keep[:, b, P * c:P * c + P]
                                else:
                                    src = keep[:, 0, rows * c:rows * c + rows]
                                mm = pe.transpose(turned[(p + b) % 2][0:rows, P * c:P * c + P], src, ident[:, :])
                            mm.then_inc(t_full, 1)
                    if s >= VALUES:
                        u, k = units[s - VALUES], u0 + s - VALUES
                        buf = u["pt"][k % 2]
                        out = product[w.item % 2][u["rows"], :]
                        pe.wait_ge(t_taken, p0 + parts_of(units, s - VALUES + 1))
                        if u["opens"] and w.item >= 2:
                            pe.wait_ge(o_taken, w.item - 1)
                        if u["kind"] == "cmp":
                            mm = pe.matmul(out, u["v"][0], buf[0:2 * CPAD, 0, :, :].rearrange("p c q -> p (c q)"),
                                           start=True, stop=True, skip_group_check=True)
                        else:
                            for b, values in enumerate(u["v"]):
                                for c, rows in u["chunks"]:
                                    mm = pe.matmul(out[:, P * u["i"]:P * u["i"] + P], values[c], buf[:, b, c, :],
                                                   start=(b == 0 and c == 0),
                                                   stop=(b == len(u["v"]) - 1 and c == len(values) - 1),
                                                   skip_group_check=True)
                        mm.then_inc(pv_done, 1)
                        if u["closes"]:
                            w.item += 1
                w.unit += len(units)
                w.part += parts_of(units, len(units))
                pe.wait_ge(o_taken, w.item)

            def rope_product(raw, rows, cols_, m_raw):
                a, m = w.small()
                out = open_bank(m)
                if m_raw is not None:
                    wait_taken(pe, m_raw)
                pe.matmul(out[0:rows, 0:cols_], rot[0:rows, 0:rows], raw, start=True,
                          stop=True).then_inc(aux_done, 1)
                w.rope += 1

            def mixer(layer):
                norm(KC)
                for k in range(14):
                    of_u(u_arrives if k == 0 else None)
                v0 = w.vec
                a, m = w.small()
                out = open_bank(m)
                for t in range(2):
                    pe.wait_ge(vec_ready, v0 + 1 + t)
                    mm = pe.matmul(out[:, :], ones[:, :], conv_acc[:, t, :], start=(t == 0), stop=(t == 1))
                mm.then_inc(aux_done, 1)
                m = w.bank()
                out = open_bank(m)
                for t in range(2):
                    pe.wait_ge(sq_ready, w.sq + 1)
                    pe.matmul(out[:, :], ones[:, :], sq[w.sq % 2][:, :], start=(t == 0),
                              stop=(t == 1)).then_inc(sq_used, 1)
                    w.sq += 1
                w.norm += 1
                w.vec += 6
                w.act += 2
                w.loads += 4
                pe.wait_ge(small_in, 16 * w.loads)
                for l in range(3):
                    a, m = w.small()
                    if l == 0:
                        lhs, rhs = f_w1[:, :], f_z[:, :]
                    else:
                        pe.wait_ge(act_ready, w.act + l)
                        lhs, rhs = f_w23[:, l - 1, :], f_h[(l - 1) % 2][:, :]
                    pe.matmul(open_bank(m)[0:HYF, :], lhs, rhs, start=True, stop=True).then_inc(aux_done, 1)
                pe.wait_ge(act_ready, w.act + 3)
                for t in range(TB):
                    for o in range(2):
                        a, m = w.small()
                        pe.matmul(open_bank(m)[:, :], f_h[0][:, P * t:P * t + P],
                                  f_w4[:, T * o:T * o + T], start=True, stop=True).then_inc(aux_done, 1)
                w.vec += 3
                w.act += 3
                for o in range(2):
                    m = w.bank()
                    out = open_bank(m)
                    for t in range(TB):
                        pe.wait_ge(sq_ready, w.sq + 1)
                        for b in range(2):
                            mm = pe.matmul(out[:, 0:HYC], ones[:, :],
                                           f_abs[t % 2][:, HYC * b:HYC * b + HYC],
                                           start=(t == 0 and b == 0), stop=(t == TB - 1 and b == 1))
                        mm.then_inc(sq_used, 1)
                        w.sq += 1
                w.tables += 2
                pe.wait_ge(tables_in, 16 * w.tables)
                pe.wait_ge(vec_ready, w.vec + 9)
                for j in range(TB):
                    for part, src in ((0, fsum), (1, fdif)):
                        a, m = w.small()
                        out = open_bank(m)
                        for t in range(TB):
                            mm = pe.matmul(out[:, :], dft[:, part, t, P * j:P * j + P],
                                           src[:, t, :, :].rearrange("p o c -> p (o c)"),
                                           start=(t == 0), stop=(t == TB - 1))
                        mm.then_inc(aux_done, 1)
                w.vec += 10
                w.tables += 1
                for o in range(2):
                    v0 = w.vec
                    if o == 1:
                        pe.wait_ge(vec_ready, v0)
                    jobs = []
                    for t in range(TB):
                        a, m = w.small()
                        out = open_bank(m)
                        for c in range(2):
                            mm = pe.transpose(out[:, P * c:P * c + P], hy[:, 2 * o + c, P * t:P * t + P],
                                              ident[:, :])
                        mm.then_inc(aux_done, 1)
                        jobs.append(m)
                    for m in jobs:
                        wait_taken(pe, m)
                    for j in range(TB):
                        a, m = w.small()
                        out = open_bank(m)
                        for part in range(2):
                            for t in range(TB):
                                mm = pe.matmul(out[:, HYC * part:HYC * part + HYC],
                                               dft[:, part, t, P * j:P * j + P], v_tok[:, t, :],
                                               start=(t == 0), stop=(t == TB - 1), skip_group_check=True)
                        mm.then_inc(aux_done, 1)
                    if o == 0:
                        pe.wait_ge(tables_in, 16 * w.tables)
                    for c in range(2):
                        a, m = w.small()
                        out = open_bank(m)
                        for j in range(TB):
                            if c == 0:
                                pe.wait_ge(vec_ready, v0 + j + 1)
                            for part in range(2):
                                mm = pe.matmul(out[:, :], y_spec[:, j, part, P * c:P * c + P],
                                               idft[:, part, j, :], start=(j == 0 and part == 0),
                                               stop=(j == TB - 1 and part == 1))
                        mm.then_inc(aux_done, 1)
                    w.vec += TB + 2
                norm(2, split=False)
                norm(1, split=False)
                w.loads += 2
                pe.wait_ge(small_in, 16 * w.loads)
                pe.wait_ge(u_full, w.full)
                for t in range(TB):
                    a, m = w.small()
                    pe.matmul(open_bank(m)[:, :], kvn[:, 0, P * t:P * t + P], w_kvb[:, 1, :], start=True,
                              stop=True).then_inc(aux_done, 1)
                for h in range(0, HEADS, 2):
                    a, m = w.small()
                    pe.matmul(open_bank(m)[:, :], w_kvb[:, 0, NOPE * h:NOPE * h + P], kvn[:, 0, :],
                              start=True, stop=True).then_inc(aux_done, 1)
                rope_product(hm_q[0:QK, 3, :], QK, T, None)
                prev = None
                for h in range(HEADS + 1):
                    this = None
                    if h < HEADS:
                        a, m = w.small()
                        out = open_bank(m)
                        for c in range(2):
                            mm = pe.matmul(out[0:QK, :], w_qb[:, c, QK * h:QK * h + QK], qn[:, c, :],
                                           start=(c == 0), stop=(c == 1))
                        mm.then_inc(aux_done, 1)
                        this = m
                    if prev is not None:
                        rope_product(htmp[(h - 1) % 2][0:QK, :], QK, T, prev)
                    prev = this
                pe.wait_ge(rope_done, w.rope)
                w.vec += 1
                pe.wait_ge(vec_ready, w.vec)
                attention(mla_units())
                norm(4)
                norm(2)
                norm(2)

                def project(j, i):
                    ready = u_arrives if i is None and j == 0 else None
                    multiply(w.n + j, open_bank(w.m + j, i)[:, :], KC, lambda c: u_hi[:, c, :],
                             lambda c: u_lo[:, c, :], i, ready)

                looped(8, project)

            pe.wait_ge(consts_in, 16 * 3)
            pe.wait_ge(vec_ready, 1)
            w.vec += 1
            w.loads += 2
            for layer in range(DEPTH):
                norm(KC)
                ffn(PARTS, 2)
                if layer == 0:
                    w.vec += 2
                    w.act += 2
                mixer(layer)
                norm(KC)
                ffn(PARTS, 2)
            norm(KC, split=False)

            norm(KC)
            w.loads += 1
            pe.wait_ge(small_in, 16 * w.loads)
            w.vec += 1
            w.act += 2
            for t in range(KC):
                for k in range(3):
                    of_u(u_arrives if t == 0 and k == 0 else None)
                w.vec += 1
                pe.wait_ge(vec_ready, w.vec)
                for k in range(2):
                    a, m = w.small()
                    pe.matmul(open_bank(m)[:, :], w_ra[:, k, t, :], xc[t % 2][:, :], start=True,
                              stop=True).then_inc(aux_done, 1)
                w.act += 2
                w.vec += 1
            w.loads += 2
            norm(KC, size=MEM)
            for k in range(2):
                n, m = w.gemm()
                multiply(n, open_bank(m)[:, 0:MEM], KC, lambda c: mem_hi[:, c, :],
                         lambda c: mem_lo[:, c, :], ready=u_arrives if k == 0 else None)
            for k in range(2):
                n, m = w.gemm()
                out = open_bank(m)
                pe.wait_ge(w_split, n + 1)
                hi, lo = weights(n, KC)
                for tc in range(2):
                    for c in range(KC):
                        for q, (a_, b_) in enumerate(((mem_hi, hi), (mem_lo, hi), (mem_hi, lo))):
                            mm = pe.matmul(out[:, P * tc:P * tc + P], a_[:, c, P * tc:P * tc + P], b_[:, c, :],
                                           start=(c == 0 and q == 0), stop=(c == KC - 1 and q == 2),
                                           skip_group_check=True)
                mm.then_inc(gemm_done, 1)
            for k in range(2):
                of_u()
            attention(cross_units())
            pe.wait_ge(small_in, 16 * w.loads)
            for t in range(KC):
                of_u()
                a, m = w.small()
                out = open_bank(m)
                for c in range(2):
                    mm = pe.matmul(out[:, :], w_xo[:, c, P * t:P * t + P], ox[:, c, :], start=(c == 0),
                                   stop=(c == 1))
                mm.then_inc(aux_done, 1)
            w.vec += KC
            w.loads += 3
            pe.wait_ge(small_in, 16 * w.loads)
            prev = None
            for k in range(13):
                this = None
                if k < 12:
                    of_u()
                    this = w.m - 1
                if prev is not None:
                    rope_product(htmp[(k - 1) % 2][:, :], P, T, prev)
                prev = this
            for k in range(4):
                of_u()
                src = w.m - 1
                a, m = w.small()
                out = open_bank(m)
                wait_taken(pe, src)
                for t in range(TB):
                    mm = pe.transpose(out[:, P * t:P * t + P], sg[k % 2][:, P * t:P * t + P], ident[:, :])
                mm.then_inc(aux_done, 1)
            of_u()
            src = w.m - 1
            a, m = w.small()
            out = open_bank(m)
            wait_taken(pe, src)
            for t in range(TB):
                mm = pe.transpose(out[:, 48 * t:48 * t + 48], sg[0][0:48, P * t:P * t + P], ident[0:48, 0:48])
            mm.then_inc(aux_done, 1)
            for k in range(4 + KC):
                of_u()
            for side in range(2):
                w.loads += 5 if side == 0 else 2
                pe.wait_ge(small_in, 16 * w.loads)
                w.vec += 1
                pe.wait_ge(vec_ready, w.vec)
                hid = []
                for mh in range(2):
                    a, m = w.small()
                    out = open_bank(m)
                    for c in range(16):
                        mm = pe.matmul(out[:, 0:GROUPS * NCMP], w_c1[:, c, P * mh:P * mh + P],
                                       c_blk[:, c, :, :].rearrange("p g n -> p (g n)"), start=(c == 0),
                                       stop=(c == 15))
                    mm.then_inc(aux_done, 1)
                    hid.append(m)
                for m in hid:
                    wait_taken(pe, m)
                a, m = w.small()
                out = open_bank(m)
                if side == 0:
                    for mh in range(2):
                        mm = pe.matmul(out[0:HD, 0:GROUPS * NCMP], w_c2[:, mh, :], c_hid[:, mh, :],
                                       start=(mh == 0), stop=(mh == 1))
                    mm.then_inc(aux_done, 1)
                    rope_product(htmp[0][0:HD, 0:GROUPS * NCMP], HD, GROUPS * NCMP, m)
                else:
                    for r in (0, CPAD):
                        for g in range(GROUPS):
                            for mh in range(2):
                                mm = pe.matmul(out[r:r + NCMP, HD * g:HD * g + HD],
                                               c_hid[:, mh, NCMP * g:NCMP * g + NCMP], w_c2[:, mh, :],
                                               start=(mh == 0), stop=(mh == 1), skip_group_check=True)
                    mm.then_inc(aux_done, 1)
                    wait_taken(pe, m)
            pe.wait_ge(rope_done, w.rope)
            attention(nsa_units(True))
            attention(nsa_units(False))
            w.split += KC

            def project2(j, i):
                ready = u_arrives if i is None and j == 0 else None
                multiply(w.n + j, open_bank(w.m + j, i)[:, :], KC, lambda c: u_hi[:, c, :],
                         lambda c: u_lo[:, c, :], i, ready)

            looped(8, project2)
            norm(KC)
            ffn(PARTS2, 1)
            norm(KC, split=False)

        @block.scalar
        def _(act):
            w = Walk()

            def done(n, i=None):
                act.wait_ge(gemm_done, at_turn(n + 1, 4, i))

            def take(dst, src, m, func=ACT.Copy, **kw):
                return act.activation(dst, src, func, **kw).then_inc(taken[m % 4], 1)

            def small_load(dst, src):
                act.dma_start(dst, src).then_inc(small_in, 16)
                w.loads += 1

            def to_high(dst):
                act.wait_ge(u_full, w.full + 1)
                act.activation(dst, full[w.split % 3][:, 0:dst.shape[-1]], ACT.Copy).then_inc(u_hi_ready, 1)
                w.full += 1
                w.split += 1

            def norm(srcs, dim, ready, highs=None, size=T):
                for c, s in enumerate(srcs):
                    ready(c)
                    if w.sq >= 2:
                        act.wait_ge(sq_used, w.sq - 1)
                    act.activation(sq[w.sq % 2][:, 0:size], s, ACT.Square).then_inc(sq_ready, 1)
                    w.sq += 1
                m = w.bank()
                act.wait_ge(sq_used, w.sq)
                if w.norm:
                    act.wait_ge(rinv_ready, w.norm)
                take(std[:, 0:size], ring[m % 4][:, 0:size], m, ACT.Sqrt, scale=1.0 / dim, bias=col("eps", None, 0))
                w.norm += 1
                if highs is None:
                    w.full += len(srcs)
                else:
                    for dst in highs:
                        to_high(dst)

            def x_tiles():
                return [x[:, c, :] for c in range(KC)]

            def high_tiles(a=0, b=KC):
                return [u_hi[:, c, :] for c in range(a, b)]

            def x_updated(c):
                wait_taken(act, w.m - KC + c)

            def looped(count, per, body):
                body(None)
                with act.Fori(1, count // per) as i:
                    body(i)

            def ffn(parts, per):
                for part in parts:
                    def chunk(i, c):
                        if per == 2:
                            gate, up = 2 * c, 2 * c + 1
                            done(w.n + gate, i)
                            act.activation(sg[c % 2][:, :], ring[(w.m + gate) % 4][:, :], ACT.Silu)\
                               .then_inc(taken[(w.m + gate) % 4], 1)
                            m = w.m + up
                        else:
                            m = w.m + c
                            done(w.n + c, i)
                            act.activation(sg[c % 2][:, :], ring[m % 4][:, :], ACT.Relu)\
                               .then_inc(act_ready, 1)
                        wait_taken(act, m, i)
                        act.sem_inc(act_tick, 1)
                        dst = h_hi[:, c, :] if i is None else \
                            h_hi[:, bass.ds(i * (4 // per) + c, 1), :].rearrange("p o t -> p (o t)")
                        act.activation(dst, htmp[c % 2][:, :], ACT.Copy).then_inc(h_hi_ready, 1)

                    def turn(i):
                        for c in range(4 // per):
                            chunk(i, c)

                    looped(per * part, 4, turn)
                    w.n += per * part
                    w.m += per * part
                    w.hid += part
                    if per == 1:
                        w.act += part
                    w.n += 8
                    w.m += 8

            def attention(units):
                u0, p0 = w.unit, w.part
                for s in range(len(units) + TURN):
                    if s < len(units):
                        u, k = units[s], u0 + s
                        n, j = u["n"], k % 8
                        keep, sc = u["keep"][k % 4], score[s % 2]
                        act.wait_ge(s_max, k + 1)
                        if s >= 4:
                            act.wait_ge(t_full, p0 + parts_of(units, s - 3))
                        if u["kind"] == "cmp":
                            flat = keep[:, 0, 0:2 * TB * CPAD]
                            act.activation(flat, flat, ACT.Exp, scale=u["scale"]).then_inc(exp_done, 1)
                        elif u["kind"] == "pair":
                            act.activation(e0[:, j, 0:1], nb[:, j, 1:2], ACT.Exp).then_inc(act_tick, 1)
                            for b in range(2):
                                act.activation(keep[:, b, 0:n], sc[:, b, 0:n], ACT.Exp, bias=nb[:, j, b:b + 1],
                                               scale=u["scale"], accum_out=sums[:, j, b:b + 1])\
                                   .then_inc(exp_done, 1)
                        else:
                            act.activation(keep[:, 0:n], sc[:, 0, 0:n], ACT.Exp, bias=nb[:, j, 0:1],
                                           scale=u["scale"], accum_out=sums[:, j, 0:1]).then_inc(exp_done, 1)
                    if s >= TURN:
                        u, k = units[s - TURN], u0 + s - TURN
                        p = p0 + parts_of(units, s - TURN)
                        if k >= 2:
                            act.wait_ge(pv_done, k - 1)
                        for b in range(len(u["v"])):
                            act.wait_ge(t_full, p + b + 1)
                            nch, rows = len(u["chunks"]), u["chunks"][0][1]
                            act.activation(u["pt"][k % 2][0:rows, b, 0:nch, :],
                                           turned[(p + b) % 2][0:rows, 0:P * nch]
                                           .rearrange("p (c q) -> p c q", q=P), ACT.Copy).then_inc(t_taken, 1)
                w.unit += len(units)
                w.part += parts_of(units, len(units))
                w.item += sum(u["closes"] for u in units)

            def small_done(a):
                act.wait_ge(aux_done, a + 1)

            def mixer(layer):
                norm(x_tiles(), D, x_updated, high_tiles())
                for k in range(14):
                    n, m = w.gemm()
                    if k < 4:
                        done(n)
                        take(hm_q[:, k, :], ring[m % 4][:, :], m)
                    elif 6 <= k < 8:
                        done(n)
                        take(g_sig[:, k - 6, :], ring[m % 4][:, :], m, ACT.Sigmoid)
                v0 = w.vec
                w.small()
                for t in range(2):
                    act.wait_ge(vec_ready, v0 + 3 + t)
                    if w.sq >= 2:
                        act.wait_ge(sq_used, w.sq - 1)
                    act.activation(sq[w.sq % 2][:, :], conv_c[:, t, :], ACT.Square).then_inc(sq_ready, 1)
                    w.sq += 1
                m = w.bank()
                act.wait_ge(sq_used, w.sq)
                act.wait_ge(rinv_ready, w.norm)
                take(std[:, :], ring[m % 4][:, :], m, ACT.Sqrt, scale=1.0 / CONVC, bias=col("eps", None, 0))
                w.norm += 1
                for t in range(2):
                    act.wait_ge(vec_ready, v0 + 5 + t)
                    act.activation(y_conv[:, t, :], conv_c[:, t, :], ACT.Silu,
                                   bias=col("ln_b", layer, t)).then_inc(act_ready, 1)
                w.vec += 6
                w.act += 2
                act.wait_ge(act_ready, w.act)
                small_load(f_w1[:, :], d["f_w1"][layer])
                small_load(f_w23[:, :, :], d["f_w23"][layer])
                small_load(f_w4[:, :], d["f_w4"][layer])
                small_load(f_z[:, :], d["f_z"])
                act.dma_start(decay[:, :, :], d["decay"]).then_inc(tables_in, 16)
                act.dma_start(dft[:, :, :, :], d["dft"]).then_inc(tables_in, 16)
                w.tables += 3
                for l in range(3):
                    w.small()
                    act.wait_ge(vec_ready, w.vec + l + 1)
                    act.activation(f_h[l % 2][:, :], f_a[0:HYF, :], ACT.Sin).then_inc(act_ready, 1)
                w.aux += 8
                w.m += 8
                w.vec += 3
                w.act += 3
                for o in range(2):
                    m = w.bank()
                    for t in range(TB):
                        if o == 0 and t == 0:
                            act.wait_ge(vec_ready, w.vec + 8)
                        if TB * o + t >= 2:
                            act.wait_ge(sq_used, w.sq - 1)
                        act.activation(f_abs[t % 2][:, :],
                                       filt[:, o, t, :, :].rearrange("p b c -> p (b c)"), ACT.Abs)\
                           .then_inc(sq_ready, 1)
                        w.sq += 1
                w.aux += 8
                w.m += 8
                w.vec += 10
                act.wait_ge(vec_ready, w.vec)
                act.dma_start(idft[:, :, :, :], d["idft"]).then_inc(tables_in, 16)
                for o in range(2):
                    for t in range(TB):
                        a, m = w.small()
                        small_done(a)
                        take(v_tok[:, t, :], ring[m % 4][:, 0:HYC], m)
                    w.aux += TB + 2
                    w.m += TB + 2
                    w.vec += TB + 2
                norm([hm_q[:, 0, :], hm_q[:, 1, :]], QRANK, lambda c: None)
                norm([hm_q[:, 2, :]], KVRANK, lambda c: None)
                act.wait_ge(vec_ready, w.vec)
                small_load(w_qb[:, :, :], d["w_qb"][layer])
                small_load(w_kvb[:, :, :], d["w_kvb"][layer])
                for t in range(TB):
                    a, m = w.small()
                    small_done(a)
                    take(v_all[:, t, :], ring[m % 4][:, :], m)
                for h in range(0, HEADS, 2):
                    a, m = w.small()
                    small_done(a)
                    act.activation(k_all[0:NOPE, h, :], ring[m % 4][0:NOPE, :], ACT.Copy)
                    take(k_all[0:NOPE, h + 1, :], ring[m % 4][NOPE:P, :], m)
                w.small()
                w.rope += 1
                for h in range(HEADS + 1):
                    if h < HEADS:
                        a, m = w.small()
                        small_done(a)
                        if h >= 2:
                            act.wait_ge(rope_done, w.rope)
                        take(htmp[h % 2][0:QK, :], ring[m % 4][0:QK, :], m)
                    if h >= 1:
                        w.small()
                        w.rope += 1
                w.vec += 1
                attention(mla_units())
                act.wait_ge(o_taken, w.item)
                norm([y_mla[:, c, :] for c in range(4)], 512, lambda c: None, high_tiles(0, 4))
                norm([y_conv[:, c, :] for c in range(2)], 256, lambda c: None, high_tiles(4, 6))
                norm([hy[:, 4 + c, :] for c in range(2)], 256, lambda c: act.wait_ge(vec_ready, w.vec - 1),
                     high_tiles(6, 8))
                w.n += 8
                w.m += 8

            act.dma_start(rot[:, :], d["rot1"]).then_inc(small_in, 16)
            act.dma_start(cosq[0:QK, :].bitcast(I32), d["positions"]).then_inc(small_in, 16)
            w.loads += 2
            act.wait_ge(consts_in, 16 * 3)
            w.vec += 1
            for layer in range(DEPTH):
                norm(x_tiles(), D, (lambda c: None) if layer == 0 else x_updated, high_tiles())
                ffn(PARTS, 2)
                if layer == 0:
                    act.wait_ge(vec_ready, w.vec + 1)
                    act.activation(sinq[0:QK, :], f_a[0:QK, :], ACT.Sin).then_inc(act_ready, 1)
                    act.wait_ge(vec_ready, w.vec + 2)
                    act.activation(cosq[0:QK, :], f_n[0:QK, :], ACT.Sin).then_inc(act_ready, 1)
                    w.vec += 2
                    w.act += 2
                mixer(layer)
                norm(x_tiles(), D, x_updated, high_tiles())
                ffn(PARTS, 2)
            norm(x_tiles(), D, x_updated)

            u0 = w.full
            norm(x_tiles(), D, lambda c: act.wait_ge(u_full, u0 - KC + c + 1), high_tiles())
            small_load(w_ra[:, :, :, :], d["w_ra"])
            act.activation(lamt[:, 0, :], cols[:, places["lam"]:places["lam"] + KC], ACT.Abs)\
               .then_inc(act_ready, 1)
            act.wait_ge(act_ready, w.act + 1)
            act.activation(lamt[:, 1, :], lamt[:, 0, :], ACT.Exp, scale=-1.0).then_inc(act_ready, 1)
            w.act += 2
            w.vec += 1
            for t in range(KC):
                n, m = w.gemm()
                done(n)
                if t >= 2:
                    act.wait_ge(vec_ready, w.vec - 3)
                take(xpad[t % 2][:, 3:T + 3], ring[m % 4][:, :], m)
                n, m = w.gemm()
                done(n)
                act.wait_ge(vec_ready, w.vec)
                take(gel[:, :], ring[m % 4][:, :], m, ACT.Gelu_apprx_tanh)
                n, m = w.gemm()
                done(n)
                take(gm1[:, :], ring[m % 4][:, :], m, ACT.Sigmoid)
                w.vec += 1
                for k, (dst, b) in enumerate(((rs, "b_a"), (isg, "b_i"))):
                    a, m = w.small()
                    small_done(a)
                    take(dst[:, :], ring[m % 4][:, :], m, ACT.Sigmoid, bias=col(b, None, t))
                    if k == 0:
                        m_r = m
                wait_taken(act, m_r)
                act.activation(th[:, :], rs[:, :], ACT.Tanh, scale=lamt[:, 7, t:t + 1]).then_inc(act_ready, 1)
                act.wait_ge(act_ready, w.act + 1)
                act.activation(sqt[:, :], th[:, :], ACT.Sqrt).then_inc(act_ready, 1)
                w.act += 2
                w.vec += 1
            act.wait_ge(vec_ready, w.vec)
            small_load(mem_t[:, :, :], d["mem_t"])
            small_load(w_xo[:, :, :], d["w_xo"])
            act.wait_ge(small_in, 16 * w.loads)
            norm([mem_t[:, c, :] for c in range(KC)], D, lambda c: None, [mem_hi[:, c, :] for c in range(KC)],
                 size=MEM)
            for k in range(2):
                n, m = w.gemm()
                done(n)
                take(kx[:, k, :], ring[m % 4][:, 0:MEM], m)
            for k in range(2):
                n, m = w.gemm()
                done(n)
                take(vx[:, :, P * k:P * k + P], ring[m % 4][:, 0:MEM].rearrange("p (t c) -> p t c", c=P), m)
            for k in range(2):
                n, m = w.gemm()
                done(n)
                take(qx[:, k, :], ring[m % 4][:, :], m)
            attention(cross_units())
            for t in range(KC):
                n, m = w.gemm()
                done(n)
                if t >= 2:
                    act.wait_ge(vec_ready, w.vec + t - 1)
                take(gm2[t % 2][:, :], ring[m % 4][:, :], m, ACT.Sigmoid)
                w.small()
            w.vec += KC
            small_load(rot[:, :], d["rot2"])
            small_load(cosq[:, :], d["cos2"])
            small_load(sinq[:, :], d["sin2"])
            act.wait_ge(vec_ready, w.vec)
            act.wait_ge(small_in, 16 * w.loads)
            for k in range(13):
                if k < 12:
                    n, m = w.gemm()
                    done(n)
                    if k >= 2:
                        act.wait_ge(rope_done, w.rope)
                    take(htmp[k % 2][:, :], ring[m % 4][:, :], m)
                if k >= 1:
                    w.small()
                    w.rope += 1
            for k in range(4):
                n, m = w.gemm()
                done(n)
                take(sg[k % 2][:, :], ring[m % 4][:, :], m)
                a, m = w.small()
                small_done(a)
                take(v2[:, k // 2, :, k % 2, :], ring[m % 4][:, :].rearrange("p (t c) -> p t c", c=P), m)
            n, m = w.gemm()
            done(n)
            take(sg[0][0:48, :], ring[m % 4][0:48, :], m, ACT.Sigmoid)
            a, m = w.small()
            small_done(a)
            take(gates[:, :, :], ring[m % 4][:, 0:48 * TB].rearrange("p (t c) -> p t c", c=48), m)
            for k in range(4):
                n, m = w.gemm()
                done(n)
                take(c_raw[:, k, :], ring[m % 4][:, :], m)
            for k in range(KC):
                n, m = w.gemm()
                done(n)
                take(gm0[:, k, :], ring[m % 4][:, :], m, ACT.Sigmoid)
            for side in range(2):
                if side == 1:
                    act.wait_ge(rope_done, w.rope)
                small_load(w_c1[:, :, :], d["w_c1"][side])
                small_load(w_c2[:, :, :], d["w_c2"][side])
                if side == 0:
                    act.dma_start(cos_c[:, :, :], d["cos_c"]).then_inc(small_in, 16)
                    act.dma_start(cmask[:, :, :], d["cmask"]).then_inc(small_in, 16)
                    act.dma_start(causal[:, :], d["causal"]).then_inc(small_in, 16)
                    w.loads += 3
                w.vec += 1
                for mh in range(2):
                    a, m = w.small()
                    small_done(a)
                    take(c_hid[:, mh, :], ring[m % 4][:, 0:GROUPS * NCMP], m, ACT.Gelu_apprx_tanh)
                a, m = w.small()
                small_done(a)
                if side == 0:
                    take(htmp[0][0:HD, 0:GROUPS * NCMP], ring[m % 4][0:HD, 0:GROUPS * NCMP], m)
                    w.small()
                    w.rope += 1
                else:
                    for e in range(2):
                        dst = v_cmp[CPAD * e:CPAD * e + NCMP, :, e, :]
                        src = ring[m % 4][CPAD * e:CPAD * e + NCMP, 0:GROUPS * HD]\
                            .rearrange("p (g c) -> p g c", c=HD)
                        if e == 0:
                            act.activation(dst, src, ACT.Copy)
                        else:
                            take(dst, src, m)
            attention(nsa_units(True))
            attention(nsa_units(False))
            act.wait_ge(o_taken, w.item)
            for c in range(KC):
                act.activation(u_hi[:, c, :], y2[:, c, :], ACT.Copy).then_inc(u_hi_ready, 1)
            w.split += KC
            w.n += 8
            w.m += 8
            norm(x_tiles(), D, x_updated, high_tiles())
            ffn(PARTS2, 1)
            norm(x_tiles(), D, x_updated)

        @block.vector
        def _(dve):
            w = Walk()
            links = [0]

            def step(ins):
                links[0] += 1
                ins.then_inc(dve_link, 1)
                return links[0]

            def link(ins):
                dve.wait_ge(dve_link, step(ins))

            def done(n, i=None):
                dve.wait_ge(gemm_done, at_turn(n + 1, 4, i))

            def small_done(a):
                dve.wait_ge(aux_done, a + 1)

            def arrived(ins):
                w.vec += 1
                return ins.then_inc(vec_ready, 1)

            def norm(srcs, gains, outs=None, lows=None, highs=None, size=T, signal=None):
                m = w.bank()
                w.sq += len(srcs)
                wait_taken(dve, m)
                if w.full:
                    dve.wait_ge(u_full, w.full)
                dve.reciprocal(rinv[:, 0:size], std[:, 0:size]).then_inc(rinv_ready, 1)
                w.norm += 1
                dve.wait_ge(rinv_ready, w.norm)
                count = len(srcs)
                for c in range(count + 1):
                    if c < count:
                        if outs is not None:
                            out = outs[c]
                        else:
                            out = full[(w.split + c) % 3][:, 0:size]
                            if w.split + c >= 3:
                                dve.wait_ge(u_ready, w.split + c - 2)
                        dve.scalar_tensor_tensor(out, srcs[c], gains(c), rinv[:, 0:size], ALU.mult,
                                                 ALU.mult).then_inc(signal or u_full, 1)
                    if c >= 1 and outs is None:
                        dve.wait_ge(u_hi_ready, w.split + c)
                        dve.tensor_tensor(lows[c - 1], full[(w.split + c - 1) % 3][:, 0:size],
                                          highs[c - 1].bitcast(F32), ALU.subtract).then_inc(u_ready, 1)
                w.full += count
                if outs is None:
                    w.split += count

            def x_tiles():
                return [x[:, c, :] for c in range(KC)]

            def norm_x(name, layer):
                norm(x_tiles(), lambda c: col(name, layer, c), lows=[u_lo[:, c, :] for c in range(KC)],
                     highs=[u_hi[:, c, :] for c in range(KC)])

            def looped(turns, body):
                body(None)
                with dve.Fori(1, turns) as i:
                    body(i)

            def add_to_x(scale):
                def turn(i):
                    for j in range(4):
                        m = w.m + j
                        tile = x[:, j, :] if i is None else \
                            x[:, bass.ds(i * 4 + j, 1), :].rearrange("p o t -> p (o t)")
                        done(w.n + j, i)
                        dve.scalar_tensor_tensor(tile, ring[m % 4][:, :], scale, tile, ALU.mult,
                                                 ALU.add).then_inc(taken[m % 4], 1)
                looped(2, turn)
                w.n += 8
                w.m += 8

            def ffn(parts, per):
                for part in parts:
                    def chunk(i, c):
                        if per == 2:
                            gate, up = w.m + 2 * c, w.m + 2 * c + 1
                            wait_taken(dve, gate, i)
                            done(w.n + 2 * c + 1, i)
                            dve.tensor_tensor(htmp[c % 2][:, :], ring[up % 4][:, :], sg[c % 2][:, :],
                                              ALU.mult).then_inc(taken[up % 4], 1)
                        else:
                            m = w.m + c
                            dve.wait_ge(act_ready, at_turn(w.act + c + 1, 4, i))
                            dve.tensor_tensor(htmp[c % 2][:, :], sg[c % 2][:, :], sg[c % 2][:, :],
                                              ALU.mult).then_inc(taken[m % 4], 1)
                        turn_size = 4 // per
                        dst = h_lo[:, c, :] if i is None else \
                            h_lo[:, bass.ds(i * turn_size + c, 1), :].rearrange("p o t -> p (o t)")
                        high = h_hi[:, c, :] if i is None else \
                            h_hi[:, bass.ds(i * turn_size + c, 1), :].rearrange("p o t -> p (o t)")
                        dve.wait_ge(h_hi_ready, at_turn(w.hid + c + 1, turn_size, i))
                        dve.tensor_tensor(dst, htmp[c % 2][:, :], high.bitcast(F32),
                                          ALU.subtract).then_inc(h_ready, 1)

                    def turn(i):
                        for c in range(4 // per):
                            chunk(i, c)

                    looped(per * part // 4, turn)
                    w.n += per * part
                    w.m += per * part
                    w.hid += part
                    if per == 1:
                        w.act += part
                    add_to_x(0.5 if per == 2 else 1.0)

            def reduce_angle(a, n):
                link(dve.tensor_scalar(n, a, 1.0 / (2.0 * math.pi), MAGIC, ALU.mult, ALU.add))
                link(dve.tensor_scalar(n, n, MAGIC, None, ALU.subtract))
                for part in TWO_PI:
                    link(dve.scalar_tensor_tensor(a, n, -part, a, ALU.mult, ALU.add))

            def clamp_angle(a):
                return dve.tensor_scalar(a, a, 3.1415925, -3.1415925, ALU.min, ALU.max)

            def rotate(raw, outs, cos, sin, rows, cols_, m_raw):
                a, m = w.small()
                if m_raw is not None:
                    wait_taken(dve, m_raw)
                if w.rope:
                    dve.wait_ge(rope_done, w.rope)
                t1, t2 = sq[0][0:rows, 0:cols_], sq[1][0:rows, 0:cols_]
                step(dve.tensor_tensor(t1, raw, cos, ALU.mult))
                small_done(a)
                dve.tensor_tensor(t2, ring[m % 4][0:rows, 0:cols_], sin, ALU.mult)\
                   .then_inc(taken[m % 4], 1)
                dve.wait_ge(dve_link, links[0])
                wait_taken(dve, m)
                for k, (out, r0) in enumerate(outs):
                    r1 = r0 + out.shape[0]
                    a_, b_ = (s_[r0:r1, 0:cols_] for s_ in sq)
                    if len(out.shape) == 3:
                        a_, b_ = (s_.rearrange("p (g n) -> p g n", n=NCMP) for s_ in (a_, b_))
                    ins = dve.tensor_tensor(out, a_, b_, ALU.add)
                    if k == len(outs) - 1:
                        ins.then_inc(rope_done, 1)
                w.rope += 1

            def attention(units, take_tile):
                u0, p0, i0 = w.unit, w.part, w.item
                for s in range(len(units) + VALUES + 1):
                    if s < len(units):
                        u, k = units[s], u0 + s
                        j, n = k % 8, u["n"]
                        sc = score[s % 2]
                        dve.wait_ge(s_full, k + 1)
                        if u["kind"] == "plain":
                            link(dve.tensor_reduce(mx[:, j, 0:1], sc[:, 0, 0:n], AX.X, ALU.max))
                            dve.tensor_scalar(nb[:, j, 0:1], mx[:, j, 0:1], -u["scale"], None, ALU.mult)\
                               .then_inc(s_max, 1)
                        elif u["kind"] == "pair":
                            edge = sc[:, :, n - P:n]
                            link(dve.tensor_tensor(edge, edge, causal[:, :].unsqueeze(1).broadcast_to([P, 2, P]),
                                                   ALU.add))
                            link(dve.tensor_reduce(mx[:, j, 0:2], sc[:, :, 0:n], AX.X, ALU.max))
                            step(dve.tensor_scalar(nb[:, j, 0:1], mx[:, j, 0:1], -u["scale"], None, ALU.mult))
                            dve.tensor_scalar(nb[:, j, 1:2], mx[:, j, 1:2], col("padfloor", None, u["i"]),
                                              -u["scale"], ALU.max, ALU.mult).then_inc(s_max, 1)
                        else:
                            rows_ = sc[:, 0, 0:2 * TB * CPAD].rearrange("p (t n) -> p t n", n=CPAD)
                            each = sc[:, 0, 0:2 * TB * CPAD].rearrange("p (t e n) -> p t e n", e=2, n=CPAD)
                            mask = cmask[:, :, :].unsqueeze(2).broadcast_to([P, TB, 2, CPAD])
                            link(dve.tensor_tensor(each, each, mask, ALU.add))
                            link(dve.tensor_reduce(mx[:, j, :], rows_, AX.X, ALU.max))
                            link(dve.tensor_scalar(mx[:, j, :], mx[:, j, :], FLOOR, None, ALU.max))
                            if s >= 4:
                                dve.wait_ge(t_full, p0 + parts_of(units, s - 3))
                            dve.tensor_tensor(u["keep"][k % 4][:, 0, 0:2 * TB * CPAD]
                                              .rearrange("p (t n) -> p t n", n=CPAD), rows_,
                                              mx[:, j, :].unsqueeze(2).broadcast_to([P, 2 * TB, CPAD]),
                                              ALU.subtract).then_inc(s_max, 1)
                    if 0 <= s - 1 < len(units):
                        u, k = units[s - 1], u0 + s - 1
                        j, n = k % 8, u["n"]
                        keep = u["keep"][k % 4]
                        dve.wait_ge(exp_done, p0 + parts_of(units, s))
                        if u["kind"] == "plain":
                            link(dve.reciprocal(ri[:, j, 0:1], sums[:, j, 0:1]))
                            dve.tensor_scalar(keep[:, 0:n], keep[:, 0:n], ri[:, j, 0:1], None, ALU.mult)\
                               .then_inc(p_norm, 1)
                        elif u["kind"] == "pair":
                            link(dve.scalar_tensor_tensor(sums[:, j, 1:2], e0[:, j, 0:1],
                                                          col("npad", None, u["i"]), sums[:, j, 1:2],
                                                          ALU.mult, ALU.add))
                            link(dve.reciprocal(ri[:, j, 0:2], sums[:, j, 0:2]))
                            for b in range(2):
                                dve.tensor_scalar(keep[:, b, 0:n], keep[:, b, 0:n], ri[:, j, b:b + 1],
                                                  u["gate"][:, b:b + 1], ALU.mult, ALU.mult).then_inc(p_norm, 1)
                        else:
                            rows_ = keep[:, 0, 0:2 * TB * CPAD].rearrange("p (t n) -> p t n", n=CPAD)
                            link(dve.tensor_reduce(sums[:, j, :], rows_, AX.X, ALU.add))
                            link(dve.tensor_scalar(sums[:, j, :], sums[:, j, :], 1e-30, None, ALU.max))
                            link(dve.reciprocal(ri[:, j, :], sums[:, j, :]))
                            inv = ri[:, j, :].rearrange("p (t e) -> p t e", e=2)
                            link(dve.tensor_tensor(inv, inv, u["gate"], ALU.mult))
                            dve.tensor_tensor(rows_, rows_,
                                              ri[:, j, :].unsqueeze(2).broadcast_to([P, 2 * TB, CPAD]),
                                              ALU.mult).then_inc(p_norm, 1)
                    if s > VALUES and units[s - VALUES - 1]["closes"]:
                        dve.wait_ge(pv_done, u0 + s - VALUES)
                        if w.item:
                            dve.wait_ge(o_taken, w.item)
                        take_tile(w.item - i0, product[w.item % 2][:, :]).then_inc(o_taken, 1)
                        w.item += 1
                w.unit += len(units)
                w.part += parts_of(units, len(units))

            def mixer(layer):
                def c(name, k, rows=P):
                    return col(name, layer, k, rows)

                norm_x("g_mix", layer)
                w.n += 4
                w.m += 4
                for t in range(2):
                    n, m = w.gemm()
                    done(n)
                    dve.tensor_copy(a_in[:, t, :], ring[m % 4][:, :]).then_inc(taken[m % 4], 1)
                    m_a = m
                step(dve.memset(conv_pad[:, :, 0:TAPS // 2], 0.0))
                step(dve.memset(conv_pad[:, :, PADW - TAPS // 2:PADW], 0.0))
                wait_taken(dve, m_a)
                for t in range(2):
                    n, m = w.gemm()
                    wait_taken(dve, m)
                    step(dve.tensor_tensor(conv_pad[:, t, TAPS // 2:TAPS // 2 + T], a_in[:, t, :],
                                           g_sig[:, t, :], ALU.mult))
                for k in range(6):
                    n, m = w.gemm()
                    done(n)
                    src = ring[m % 4]
                    link(dve.tensor_scalar(hy[:, k, :], src[:, :], c("short_w", 3 * k + 1), c("short_b", k),
                                           ALU.mult, ALU.add))
                    link(dve.scalar_tensor_tensor(hy[:, k, 1:T], src[:, 0:T - 1], c("short_w", 3 * k),
                                                  hy[:, k, 1:T], ALU.mult, ALU.add))
                    dve.scalar_tensor_tensor(hy[:, k, 0:T - 1], src[:, 1:T], c("short_w", 3 * k + 2),
                                             hy[:, k, 0:T - 1], ALU.mult, ALU.add).then_inc(taken[m % 4], 1)
                for tap in range(TAPS):
                    for t in range(2):
                        dve.wait_ge(dve_link, links[0] - (1 if 0 < tap < TAPS - 1 else 0))
                        src = conv_pad[:, t, tap:tap + T]
                        if tap == 0:
                            ins = dve.tensor_scalar(conv_acc[:, t, :], src, c("conv_w", TAPS * t),
                                                    c("conv_b", t), ALU.mult, ALU.add)
                        else:
                            ins = dve.scalar_tensor_tensor(conv_acc[:, t, :], src, c("conv_w", TAPS * t + tap),
                                                           conv_acc[:, t, :], ALU.mult, ALU.add)
                        if tap < TAPS - 1:
                            step(ins)
                        else:
                            arrived(ins)
                a, m = w.small()
                small_done(a)
                dve.wait_ge(vec_ready, w.vec)
                for t in range(2):
                    ins = arrived(dve.scalar_tensor_tensor(conv_c[:, t, :], ring[m % 4][:, :], -1.0 / CONVC,
                                                           conv_acc[:, t, :], ALU.mult, ALU.add))
                dve.wait_ge(vec_ready, w.vec)
                dve.sem_inc(taken[m % 4], 1)
                m = w.bank()
                w.sq += 2
                wait_taken(dve, m)
                dve.wait_ge(u_full, w.full)
                dve.reciprocal(rinv[:, :], std[:, :]).then_inc(rinv_ready, 1)
                w.norm += 1
                dve.wait_ge(rinv_ready, w.norm)
                for t in range(2):
                    arrived(dve.scalar_tensor_tensor(conv_c[:, t, :], conv_c[:, t, :], c("ln_g", t), rinv[:, :],
                                                     ALU.mult, ALU.mult))
                w.act += 2
                for l in range(3):
                    a, m = w.small()
                    small_done(a)
                    arg, n_ = f_a[0:HYF, :], f_n[0:HYF, :]
                    if l:
                        dve.wait_ge(act_ready, w.act + l)
                    dve.tensor_scalar(arg, ring[m % 4][0:HYF, :], c("fb", l, HYF), c("freq", 0, HYF),
                                      ALU.add, ALU.mult).then_inc(taken[m % 4], 1)
                    wait_taken(dve, m)
                    reduce_angle(arg, n_)
                    arrived(clamp_angle(arg))
                w.act += 3
                dve.wait_ge(tables_in, 16 * (w.tables + 2))
                w.tables += 3
                v0 = w.vec
                for t in range(TB):
                    for o in range(2):
                        a, m = w.small()
                        small_done(a)
                        dve.tensor_tensor(filt[:, o, t, :, :].rearrange("p b c -> p (b c)"), ring[m % 4][:, :],
                                          decay[:, t, :], ALU.mult).then_inc(taken[m % 4], 1)
                    for m_ in (m - 1, m):
                        wait_taken(dve, m_)
                    step(dve.tensor_tensor(fsum[:, t, :, :], filt[:, :, t, 0, :], filt[:, :, t, 1, :], ALU.add))
                    dve.tensor_tensor(fdif[:, t, :, :], filt[:, :, t, 0, :], filt[:, :, t, 1, :], ALU.subtract)\
                       .then_inc(vec_ready, 2 if t < TB - 1 else 3)
                w.vec += 9
                for o in range(2):
                    m = w.bank()
                    w.sq += TB
                    dve.wait_ge(sq_used, w.sq)
                    dve.reciprocal(rinv[:, HYC * o:HYC * o + HYC], ring[m % 4][:, 0:HYC])\
                       .then_inc(taken[m % 4], 1)
                    wait_taken(dve, m)
                rk = rinv[:, :].rearrange("p (o c) -> p o c", o=2)
                for j in range(TB):
                    for part in range(2):
                        a, m = w.small()
                        small_done(a)
                        src = ring[m % 4][:, :].rearrange("p (o c) -> p o c", o=2)
                        if part == 0:
                            step(dve.tensor_tensor(spec[:, :, j, 2, :], src, rk, ALU.mult))
                        dve.tensor_tensor(spec[:, :, j, part, :], src, rk, ALU.mult).then_inc(taken[m % 4], 1)
                wait_taken(dve, m)
                dve.wait_ge(dve_link, links[0])
                w.vec += 1
                dve.sem_inc(vec_ready, 1)
                for o in range(2):
                    w.aux += TB
                    w.m += TB
                    for j in range(TB):
                        a, m = w.small()
                        small_done(a)
                        src = ring[m % 4][:, :].rearrange("p (h c) -> p h c", h=2)
                        if j:
                            dve.wait_ge(vec_ready, w.vec)
                        step(dve.tensor_tensor(prod[0][:, :, :], src, spec[:, o, j, 0:2, :], ALU.mult))
                        dve.tensor_tensor(prod[1][:, :, :], src, spec[:, o, j, 1:3, :], ALU.mult)\
                           .then_inc(taken[m % 4], 1)
                        dve.wait_ge(dve_link, links[0])
                        step(dve.tensor_tensor(y_spec[:, j, 0, :], prod[0][:, 0, :], prod[0][:, 1, :],
                                               ALU.subtract))
                        wait_taken(dve, m)
                        arrived(dve.tensor_tensor(y_spec[:, j, 1, :], prod[1][:, 0, :], prod[1][:, 1, :],
                                                  ALU.add))
                    dve.wait_ge(vec_ready, w.vec)
                    dve.wait_ge(dve_link, links[0])
                    for ch in range(2):
                        a, m = w.small()
                        small_done(a)
                        tmp = prod[ch][:, :, :].rearrange("p h c -> p (h c)")
                        dve.scalar_tensor_tensor(tmp, hy[:, 2 * o + ch, :], c("hy_d", 2 * o + ch),
                                                 ring[m % 4][:, :], ALU.mult, ALU.add).then_inc(taken[m % 4], 1)
                        wait_taken(dve, m)
                        arrived(dve.tensor_tensor(hy[:, 2 * o + 2 + ch, :], tmp, hy[:, 2 * o + 2 + ch, :],
                                                  ALU.mult))
                norm([hm_q[:, 0, :], hm_q[:, 1, :]], lambda k: c("g_q", k), outs=[qn[:, k, :] for k in range(2)])
                norm([hm_q[:, 2, :]], lambda k: c("g_kv", 0), outs=[kvn[:, 0, :]])
                w.loads += 2
                w.aux += TB + HEADS // 2
                w.m += TB + HEADS // 2
                cos, sin = cosq[0:QK, :], sinq[0:QK, :]
                rotate(hm_q[0:QK, 3, :], [(kpe_r[0:QK, :], 0)], cos, sin, QK, T, None)
                prev = None
                for h in range(HEADS + 1):
                    this = None
                    if h < HEADS:
                        this = w.small()[1]
                    if prev is not None:
                        rotate(htmp[(h - 1) % 2][0:QK, :], [(q_all[0:QK, h - 1, :], 0)], cos, sin, QK, T, prev)
                    prev = this
                dve.wait_ge(rope_done, w.rope)
                for h in range(HEADS):
                    ins = dve.tensor_copy(k_all[NOPE:QK, h, :], kpe_r[NOPE:QK, :])
                arrived(ins)

                attention(mla_units(), lambda tile, src: dve.tensor_copy(y_mla[:, tile, :], src))
                for srcs, a, b in (([y_mla[:, k, :] for k in range(4)], 0, 4),
                                   ([y_conv[:, k, :] for k in range(2)], 4, 6),
                                   ([hy[:, 4 + k, :] for k in range(2)], 6, 8)):
                    norm(srcs, lambda k: c("g_out", a + k), lows=[u_lo[:, k, :] for k in range(a, b)],
                         highs=[u_hi[:, k, :] for k in range(a, b)])
                add_to_x(1.0)

            arrived(dve.memset(ones[:, :], 1.0))
            dve.wait_ge(consts_in, 16 * 3)
            w.loads += 2
            for layer in range(DEPTH):
                norm_x("g_ffn1", layer)
                ffn(PARTS, 2)
                if layer == 0:
                    dve.wait_ge(small_in, 16 * w.loads)
                    ang, n_ = f_a[0:QK, :], f_n[0:QK, :]
                    for j in range(4):
                        wait_taken(dve, w.m - 4 + j)
                    link(dve.tensor_copy(ang, cosq[0:QK, :].bitcast(I32)))
                    link(dve.tensor_scalar(ang, ang, col("invf", None, 0, QK), None, ALU.mult))
                    reduce_angle(ang, n_)
                    arrived(clamp_angle(ang))
                    dve.wait_ge(vec_ready, w.vec)
                    link(dve.scalar_tensor_tensor(n_, ang, -1.0, ang, ALU.mult, ALU.max))
                    arrived(dve.tensor_scalar(n_, n_, -1.0, math.pi / 2, ALU.mult, ALU.add))
                    w.act += 2
                mixer(layer)
                norm_x("g_ffn2", layer)
                ffn(PARTS, 2)
            norm(x_tiles(), lambda c: col("g_final1", None, c), outs=x_tiles())

            norm_x("g_mix2", None)
            w.loads += 1
            w.act += 2
            dve.wait_ge(act_ready, w.act)
            lam = cols[:, places["lam"]:places["lam"] + KC]
            e, s, t_, z, p = (lamt[:, k, :] for k in (1, 2, 3, 4, 5))
            link(dve.tensor_scalar(t_, e, 2.0, None, ALU.add))
            link(dve.reciprocal(t_, t_))
            link(dve.tensor_tensor(s, e, t_, ALU.mult))
            link(dve.tensor_tensor(z, s, s, ALU.mult))
            link(dve.tensor_scalar(p, z, 1.0 / 17, 1.0 / 15, ALU.mult, ALU.add))
            for k in (13, 11, 9, 7, 5, 3, 1):
                link(dve.tensor_tensor(p, p, z, ALU.mult))
                link(dve.tensor_scalar(p, p, 1.0 / k, None, ALU.add))
            link(dve.tensor_tensor(p, p, s, ALU.mult))
            link(dve.tensor_scalar(t_, lam, -1.0, 0.0, ALU.mult, ALU.max))
            link(dve.scalar_tensor_tensor(t_, p, 2.0, t_, ALU.mult, ALU.add))
            link(dve.tensor_scalar(lamt[:, 7, :], t_, 4.0, None, ALU.mult))
            for k in range(2):
                link(dve.memset(xpad[k][:, 0:3], 0.0))
            w.vec += 1
            dve.sem_inc(vec_ready, 1)
            for t in range(KC):
                n, m = w.gemm()
                wait_taken(dve, m)
                src, acc = xpad[t % 2], xc[t % 2]
                link(dve.tensor_scalar(acc[:, :], src[:, 0:T], col("conv_w2", None, 4 * t),
                                       col("conv_b2", None, t), ALU.mult, ALU.add))
                for k in range(1, 4):
                    ins = dve.scalar_tensor_tensor(acc[:, :], src[:, k:k + T], col("conv_w2", None, 4 * t + k),
                                                   acc[:, :], ALU.mult, ALU.add)
                    if k < 3:
                        link(ins)
                    else:
                        arrived(ins)
                w.gemm()
                _, m_g = w.gemm()
                w.small()
                a, m_i = w.small()
                dve.wait_ge(act_ready, w.act + 1)
                link(dve.tensor_scalar(rw[:, :], th[:, :], 1.0, None, ALU.add))
                link(dve.reciprocal(rw[:, :], rw[:, :]))
                link(dve.tensor_scalar(ra[:, :], th[:, :], -1.0, 1.0, ALU.mult, ALU.add))
                link(dve.tensor_tensor(ra[:, :], ra[:, :], rw[:, :], ALU.mult))
                dve.wait_ge(act_ready, w.act + 2)
                link(dve.scalar_tensor_tensor(ru[:, :], sqt[:, :], 2.0, rw[:, :], ALU.mult, ALU.mult))
                wait_taken(dve, m_i)
                link(dve.tensor_tensor(ru[:, :], ru[:, :], isg[:, :], ALU.mult))
                link(dve.tensor_tensor(ru[:, :], ru[:, :], acc[:, :], ALU.mult))
                link(dve.tensor_tensor_scan(rh[:, :], ra[:, :], ru[:, :], 0.0, ALU.mult, ALU.add))
                link(dve.tensor_tensor(rh[:, :], rh[:, :], gel[:, :], ALU.mult))
                wait_taken(dve, m_g)
                arrived(dve.tensor_tensor(y2[:, t, :], rh[:, :], gm1[:, :], ALU.mult))
                w.act += 2
            w.loads += 2
            dve.wait_ge(small_in, 16 * w.loads)
            norm([mem_t[:, k, :] for k in range(KC)], lambda k: col("g_mem", None, k),
                 lows=[mem_lo[:, k, :] for k in range(KC)], highs=[mem_hi[:, k, :] for k in range(KC)], size=MEM)
            w.n += 6
            w.m += 6

            attention(cross_units(), lambda tile, src: dve.tensor_copy(ox[:, tile, :], src))
            for t in range(KC):
                _, m_g = w.gemm()
                a, m = w.small()
                wait_taken(dve, m_g)
                small_done(a)
                dve.tensor_tensor(sq[t % 2][:, :], ring[m % 4][:, :], gm2[t % 2][:, :], ALU.mult)\
                   .then_inc(taken[m % 4], 1)
                wait_taken(dve, m)
                arrived(dve.tensor_tensor(y2[:, t, :], y2[:, t, :], sq[t % 2][:, :], ALU.add))
            w.loads += 3
            dve.wait_ge(small_in, 16 * w.loads)
            prev = None
            for k in range(13):
                this = None
                if k < 12:
                    this = w.gemm()[1]
                if prev is not None:
                    item = k - 1
                    if item < 4:
                        outs = [(k2[HD * half:HD * half + HD, item // 2, 2 * (item % 2) + par, :], HD * par)
                                for par in range(2) for half in range(2)]
                    else:
                        outs = [(q2[:, item - 4, :], 0)]
                    rotate(htmp[item % 2][:, :], outs, cosq[:, :], sinq[:, :], P, T, prev)
                prev = this
            for k in range(5):
                w.gemm()
                w.small()
            w.n += 4 + KC
            w.m += 4 + KC
            gathered = w.m - KC - 1
            wait_taken(dve, w.m - 1)
            dve.wait_ge(rope_done, w.rope)
            step(dve.memset(k_cmp[:, :, :, :], 0.0))
            step(dve.memset(v_cmp[:, :, :, :], 0.0))
            for side in range(2):
                w.loads += 5 if side == 0 else 2
                for g in range(GROUPS):
                    src = c_raw[HD * (g % 2):HD * (g % 2) + HD, 2 * side + g // 2, :]
                    step(dve.tensor_copy(c_dup[0:HD, g, :], src))
                    step(dve.tensor_copy(c_dup[HD:P, g, 0:T - 1], src[:, 1:T]))
                dve.wait_ge(dve_link, links[0])
                for i in range(16):
                    ins = dve.tensor_scalar(c_blk[:, i, :, :], c_dup[:, :, 2 * i:2 * i + 16 * (NCMP - 1) + 1:16],
                                            col(("pos_k", "pos_v")[side], None, i), None, ALU.add)
                arrived(ins)
                w.aux += 3
                w.m += 3
                m_raw = w.m - 1
                if side == 0:
                    dve.wait_ge(small_in, 16 * w.loads)
                    flat = GROUPS * NCMP
                    rotate(htmp[0][0:HD, 0:flat],
                           [(k_cmp[HD * half:HD * half + HD, :, half, 0:NCMP], 0)
                            for half in range(2)], cos_c[:, 0, :], cos_c[:, 1, :], HD, flat, m_raw)
            wait_taken(dve, m_raw)

            def merge(tile, src):
                link(dve.tensor_tensor(sq[0][:, :], src, gm0[:, tile, :], ALU.mult))
                return dve.tensor_tensor(y2[:, tile, :], y2[:, tile, :], sq[0][:, :], ALU.add)

            attention(nsa_units(True), merge)
            attention(nsa_units(False), merge)
            dve.wait_ge(o_taken, w.item)
            for c in range(KC):
                dve.wait_ge(u_hi_ready, w.split + 1)
                dve.tensor_tensor(u_lo[:, c, :], y2[:, c, :], u_hi[:, c, :].bitcast(F32),
                                  ALU.subtract).then_inc(u_ready, 1)
                w.split += 1
            add_to_x(1.0)
            norm_x("g_mlp", None)
            ffn(PARTS2, 1)
            norm(x_tiles(), lambda c: col("g_final2", None, c), outs=[out_t[:, c, :] for c in range(KC)],
                 signal=out_ready)
    return nc


def _blocks(w, k):
    n = w.shape[1] // P
    return w.reshape(k, P, n, P).transpose(2, 1, 0, 3).reshape(n, P, k * P)


def _rows(v):
    return np.ascontiguousarray(v).reshape(-1, P).T


def _pad_rows(v):
    out = np.zeros((P, v.shape[1]), np.float32)
    out[:v.shape[0]] = v
    return out


def shape_constants():
    f = np.float32
    k = {"ident": np.eye(P, dtype=f)}
    rot1 = np.zeros((P, P), f)
    half = ROPE // 2
    for j in range(half):
        rot1[NOPE + half + j, NOPE + j] = -1
        rot1[NOPE + j, NOPE + half + j] = 1
    k["rot1"] = rot1
    rot2 = np.zeros((P, P), f)
    for h in range(2):
        for j in range(8):
            rot2[HD * h + 8 + j, HD * h + j] = -1
            rot2[HD * h + j, HD * h + 8 + j] = 1
    k["rot2"] = rot2
    inv2 = (f(1.0) / (f(500000.0) ** (np.arange(0, 16, 2, dtype=f) / f(16)))).astype(f)

    def tables(pos, rows):
        ang = (inv2[:, None] * pos[None, :].astype(f)).astype(f).astype(np.float64)
        c = np.ones((HD, len(pos)))
        s = np.zeros((HD, len(pos)))
        c[0:16] = np.tile(np.cos(ang), (2, 1))
        s[0:16] = np.tile(np.sin(ang), (2, 1))
        return np.tile(c, (rows // HD, 1)).astype(f), np.tile(s, (rows // HD, 1)).astype(f)

    k["cos2"], k["sin2"] = tables(np.arange(T), P)
    cc, sc = tables(np.arange(NCMP) * 16 + 31, HD)
    k["cos_c"] = np.stack([np.tile(cc, (1, GROUPS)), np.tile(sc, (1, GROUPS))], 1)
    ang = 2 * np.pi * np.outer(np.arange(T), np.arange(T) + 0.5) / (2 * T)
    cs = np.stack([np.cos(ang), np.sin(ang)])
    k["dft"] = cs.reshape(2, TB, P, T).transpose(2, 0, 1, 3).astype(f)
    k["idft"] = (cs.transpose(0, 2, 1) / T).reshape(2, TB, P, T).transpose(2, 0, 1, 3).astype(f)
    t = np.linspace(0.0, 1.0, T, dtype=f)[:, None]
    bands = (EMB - 1) // 2
    ang = (f(2.0 * math.pi) * np.arange(T, dtype=f)[:, None] / f(T)).astype(f)
    fb = np.linspace(1e-4, bands - 1, bands, dtype=f)[None, :]
    a = (fb * ang).astype(f).astype(np.float64)
    k["f_z"] = np.concatenate([t, np.cos(a), -np.sin(a)], 1).T.astype(f)
    deltas = np.linspace(math.log(1e-2) / 1.5, math.log(1e-2) / 0.3, HYC, dtype=f)
    win = np.exp((-t * np.abs(deltas)).astype(np.float64))
    back = win.copy()
    back[0] = 0.0
    k["decay"] = np.concatenate([win, back], 1).reshape(TB, P, T).transpose(1, 0, 2).astype(f)
    q = np.arange(T)
    end = np.arange(NCMP) * 16 + 31
    cmask = np.full((T, CPAD), NEG)
    cmask[:, 0:NCMP] = np.where(end[None, :] <= q[:, None], 0.0, NEG)
    k["cmask"] = cmask.reshape(TB, P, CPAD).transpose(1, 0, 2).astype(f)
    k["causal"] = np.where(np.arange(P)[None, :] <= np.arange(P)[:, None], 0.0, NEG).astype(f)
    return {n: np.ascontiguousarray(v) for n, v in k.items()}


def layout(a):
    k = shape_constants()
    w = {8: [], 10: [], 12: []}

    def ffn(i, name):
        gate, up, down = (a[f"{name}_w_{x}"][i] for x in ("gate", "up", "down"))
        first = 0
        for part in PARTS:
            c = slice(P * first, P * (first + part))
            pair = np.stack([_blocks(gate[:, c], KC), _blocks(up[:, c], KC)], 1)
            w[8].append(pair.reshape(2 * part, P, D))
            w[part].append(_blocks(down[c], part))
            first += part

    for i in range(DEPTH):
        ffn(i, "ffn1")
        w_in = a["w_in"][i]
        key = np.zeros((D, P), np.float32)
        key[:, NOPE:QK] = w_in[:, QRANK + KVRANK:QRANK + KVRANK + ROPE]
        w[8].append(_blocks(np.concatenate([w_in[:, 0:QRANK + KVRANK], key,
                                            w_in[:, QRANK + KVRANK + ROPE:]], 1), KC))
        w[8].append(_blocks(a["w_out"][i], KC))
        ffn(i, "ffn2")
    z = a["w_in_2"][0]
    ends = np.cumsum([0, 1024, 256, 256, 256, 256, 256, 256, 48, 1024, 1024, 256, 3072])
    q, kc, vc, ks, vs, kw, vw, ng, xr, gr, qx, mg = (z[:, s:e] for s, e in zip(ends[:-1], ends[1:]))
    trio = np.stack([_blocks(v, KC) for v in (xr, gr, mg[:, D:2 * D])], 1)
    w[8].append(trio.reshape(3 * KC, P, D))
    w[8].append(_blocks(a["w_mem_kv_2"][0], KC))
    w[8].append(_blocks(qx, KC))
    w[8].append(_blocks(mg[:, 2 * D:], KC))
    gate_cols = np.zeros((D, P), np.float32)
    gate_cols[:, 0:48] = ng
    for v in (ks, kw, q, vs, vw, gate_cols, kc, vc, mg[:, 0:D], a["w_o_2"][0]):
        w[8].append(_blocks(v, KC))
    first = 0
    for part in PARTS2:
        c = slice(P * first, P * (first + part))
        w[8].append(_blocks(a["w_up_2"][0][:, c], KC))
        w[part].append(_blocks(a["w_down_2"][0][c], part))
        first += part
    for n, v in w.items():
        k[f"w{n}"] = np.concatenate(v, 0)

    cols = []
    for i in range(DEPTH):
        conv = a["conv_dw_w"][i].reshape(TAPS, 2, P).transpose(2, 1, 0).reshape(P, 2 * TAPS)
        short = a["hy_short_w"][i].reshape(3, 6, P).transpose(2, 1, 0).reshape(P, 18)
        biases = np.stack([a[f"hy_filt_b{j}"][i] for j in (1, 2, 3)], 1)
        cols += [_rows(a["ffn1_norm"][i]), _rows(a["mix_norm"][i]), _rows(a["mla_q_norm"][i]),
                 _rows(a["mla_kv_norm"][i]), conv, _rows(a["conv_dw_b"][i]), _rows(a["conv_ln_g"][i]),
                 _rows(a["conv_ln_b"][i]), short, _rows(a["hy_short_b"][i]), _pad_rows(biases),
                 _pad_rows(a["hy_filt_freq"][i][:, None]), _rows(a["hy_bias_d"][i]), _rows(a["out_norm"][i]),
                 _rows(a["ffn2_norm"][i])]
    conv2 = a["conv_w_2"][0].reshape(4, KC, P).transpose(2, 1, 0).reshape(P, 4 * KC)
    tok = np.arange(T)
    invf = np.zeros((P, 1), np.float32)
    f = np.float32
    inv = f(1.0) / (f(10000.0) ** (np.arange(0, ROPE, 2, dtype=f) / f(ROPE)))
    invf[NOPE:QK, 0] = np.tile(inv, 2)
    cols += [_rows(a["final_norm"]), _rows(a["g_mix_2"][0]), conv2, _rows(a["conv_b_2"][0]),
             _rows(a["b_rg_a_2"][0]), _rows(a["b_rg_i_2"][0]), _rows(a["rg_lambda_2"][0]),
             _rows(a["g_mem_2"][0]), _rows(a["g_mlp_2"][0]), _rows(a["g_final_2"]),
             _rows(a["cmp_pos_k_2"][0]), _rows(a["cmp_pos_v_2"][0]), np.full((P, 1), EPS, f),
             (T - 1 - tok).reshape(TB, P).T.astype(f),
             np.where(tok < T - 1, 0.0, NEG).reshape(TB, P).T.astype(f), invf]
    k["cols"] = np.concatenate(cols, 1)

    k["xt"] = np.ascontiguousarray(a["x"][0].reshape(T, KC, P).transpose(2, 1, 0))
    k["positions"] = np.ascontiguousarray(np.broadcast_to(a["positions"], (QK, T)))
    k["f_w1"] = a["hy_filt_w1"]
    k["f_w23"] = np.stack([a["hy_filt_w2"], a["hy_filt_w3"]], 2)
    k["f_w4"] = a["hy_filt_w4"]
    k["w_qb"] = a["mla_w_qb"].reshape(DEPTH, 2, P, HEADS * QK).transpose(0, 2, 1, 3)
    k["w_kvb"] = a["mla_w_kvb"].reshape(DEPTH, P, HEADS, 2, VDIM).transpose(0, 1, 3, 2, 4).reshape(DEPTH, P, 2, T)
    ra = np.zeros((P, 2, KC, P), f)
    for j, name in enumerate(("w_rg_a_2", "w_rg_i_2")):
        for t in range(KC):
            for b in range(2):
                s = slice(64 * b, 64 * b + 64)
                ra[s, j, t, s] = a[name][0, 2 * t + b]
    k["w_ra"] = ra
    k["mem_t"] = a["mem_2"][0].reshape(MEM, KC, P).transpose(2, 1, 0)
    k["w_xo"] = a["w_xo_2"][0].reshape(2, P, D).transpose(1, 0, 2)
    k["w_c1"] = np.stack([a[f"w_cmp_{s}1_2"][0].reshape(16, P, 256).transpose(1, 0, 2) for s in "kv"])
    k["w_c2"] = np.stack([a[f"w_cmp_{s}2_2"][0].reshape(2, P, HD).transpose(1, 0, 2) for s in "kv"])
    return {n: np.ascontiguousarray(v) for n, v in k.items()}


def kernel(**inputs):
    import concourse.bacc as bacc
    from concourse.bass_utils import run_bass_kernel_spmd

    arrays = layout({n: np.asarray(v) for n, v in inputs.items()})
    nc = bacc.Bacc("TRN2", target_bir_lowering=False, num_devices=1)
    d = {n: nc.dram_tensor(f"in_{n}", v.shape, mybir.dt.from_np(v.dtype), kind="ExternalInput").ap()
         for n, v in arrays.items()}
    d["out"] = nc.dram_tensor("out", (P, KC, T), F32, kind="ExternalOutput").ap()
    build(nc, d)
    r = run_bass_kernel_spmd(nc, [{f"in_{n}": v for n, v in arrays.items()}], core_ids=[0])
    y = r.results[0]["out"]
    return np.ascontiguousarray(y.transpose(2, 1, 0)).reshape(1, T, D)
```

```python
import math
from contextlib import ExitStack

import numpy as np
import concourse.bass as bass
from concourse import mybir

F32 = mybir.dt.float32
F32R = mybir.dt.float32r
I32 = mybir.dt.int32
ALU = mybir.AluOpType
ACT = mybir.ActivationFunctionType
AX = mybir.AxisListType

P = 128
T = 512
TB = T // P
D = 1024
KC = D // P
F = 2816
PARTS = (12, 10)
DEPTH = 2
EPS = 1e-6

HEADS, NOPE, ROPE, VDIM = 8, 64, 32, 64
QK = NOPE + ROPE
QRANK, KVRANK = 256, 128
TAPS = 31
CONVC = 256
HYC = 256
HYF = 64
EMB = 33

MEM = 256
HEADS2, GROUPS = 16, 4
HD = 64
NCMP = (T - 32) // 16 + 1
CPAD = 32
XHEADS = 4
PARTS2 = (12, 12, 8)

RING = 4
SPLIT = 2
SLOT = 12 * P
MAGIC = 1.5 * 2.0 ** 23
TWO_PI = (6.28125, 1.93500518798828125e-3, 3.0199159819567e-7)
NEG = -1e30
FLOOR = -1e29

LAYER_COLS = [("g_ffn1", 8), ("g_mix", 8), ("g_q", 2), ("g_kv", 1), ("conv_w", 2 * TAPS), ("conv_b", 2),
              ("ln_g", 2), ("ln_b", 2), ("short_w", 18), ("short_b", 6), ("fb", 3), ("freq", 1),
              ("hy_d", 4), ("g_out", 8), ("g_ffn2", 8)]
LAST_COLS = [("g_final1", 8), ("g_mix2", 8), ("conv_w2", 32), ("conv_b2", 8), ("b_a", 8), ("b_i", 8),
             ("lam", 8), ("g_mem", 8), ("g_mlp", 8), ("g_final2", 8), ("pos_k", 16), ("pos_v", 16),
             ("eps", 1), ("npad", 4), ("padfloor", 4), ("invf", 1)]


def column_places():
    at, places = 0, {}
    for layer in range(DEPTH):
        for name, n in LAYER_COLS:
            places[name, layer] = at
            at += n
    for name, n in LAST_COLS:
        places[name] = at
        at += n
    return places, at


def stream():
    first = {8: 0, 10: 0, 12: 0}
    out = []

    def add(k, n):
        out.append((k, first[k], n))
        first[k] += n

    def ffn(parts, per):
        for part in parts:
            add(8, per * part)
            add(part, 8)

    for _ in range(DEPTH):
        ffn(PARTS, 2)
        add(8, 14)
        add(8, 8)
        ffn(PARTS, 2)
    add(8, 24)
    add(8, 6)
    add(8, 8)
    add(8, 21)
    add(8, 8)
    add(8, 8)
    ffn(PARTS2, 1)
    return out, first


class Walk:

    def __init__(self):
        self.n = self.m = self.aux = self.sq = self.norm = self.full = self.split = 0
        self.tables = self.hid = self.rope = self.unit = self.part = self.item = self.vec = self.act = self.loads = self.sums = self.gate = 0

    def gemm(self):
        self.n += 1
        self.m += 1
        return self.n - 1, self.m - 1

    def small(self):
        self.aux += 1
        self.m += 1
        return self.aux - 1, self.m - 1

    def bank(self):
        self.m += 1
        return self.m - 1


def at_turn(base, per, i):
    return base if i is None else i * per + base


def build(nc, d):
    places, ncols = column_places()
    plan, _ = stream()
    ctx = ExitStack()
    with ctx:
        base0 = (nc.sbuf_base + 31) // 32 * 32

        def place(name, shape, dt, at):
            return nc.alloc_sbuf_tensor_at(name, shape, dt, offset=base0 + at)

        K1 = 1024
        KB2 = T * 4
        X_AT, U_AT, RING_AT = 0, 16 * K1, 48 * K1
        H_AT = 96 * K1
        TMP_AT = 144 * K1
        ROPE_AT = 166 * K1
        SMALL_AT = 170 * K1
        x = place("x", [P, KC, T], F32, X_AT)
        u_hi = place("u_hi", [P, KC, T], F32R, U_AT)
        u_lo = place("u_lo", [P, KC, T], F32R, U_AT + 16 * K1)
        w_raw = [place(f"w_raw{i}", [P, SLOT], F32, RING_AT + i * SLOT * 4) for i in range(RING)]
        w_hi = [place(f"w_hi{i}", [P, SLOT], F32R, RING_AT + (4 + i) * SLOT * 4) for i in range(SPLIT)]
        w_lo = [place(f"w_lo{i}", [P, SLOT], F32R, RING_AT + (6 + i) * SLOT * 4) for i in range(SPLIT)]
        h_hi = place("h_hi", [P, 12, T], F32R, H_AT)
        h_lo = place("h_lo", [P, 12, T], F32R, H_AT + 24 * K1)
        sq = [place(f"sq{i}", [P, T], F32, TMP_AT + i * KB2) for i in range(2)]
        std = place("std", [P, T], F32, TMP_AT + 2 * KB2)
        rinv = place("rinv", [P, T], F32, TMP_AT + 3 * KB2)
        full = [place(f"full{i}", [P, T], F32, TMP_AT + (4 + i) * KB2) for i in range(3)]
        sg = [place(f"sg{i}", [P, T], F32, TMP_AT + (7 + i) * KB2) for i in range(2)]
        htmp = [place(f"htmp{i}", [P, T], F32, TMP_AT + (9 + i) * KB2) for i in range(2)]
        cosq = place("cosq", [P, T], F32, ROPE_AT)
        sinq = place("sinq", [P, T], F32, ROPE_AT + KB2)
        cols = place("cols", [P, ncols], F32, SMALL_AT)
        at = SMALL_AT + (ncols * 4 + 31) // 32 * 32
        ident = place("ident", [P, P], F32, at)
        ones = place("ones", [P, P], F32, at + 512)
        rot = place("rot", [P, P], F32, at + 1024)
        mx, nb, sums, e0, ri = (place(name, [P, 8, 8], F32, at + 1536 + 256 * k)
                                for k, name in enumerate(("mx", "nb", "sums", "e0", "ri")))
        assert at + 1536 + 5 * 256 <= 175 * K1
        R_AT = 175 * K1

        def mid(name, shape, at, dt=F32):
            return place(name, shape, dt, at)

        hm_q = mid("hm_q", [P, 4, T], R_AT)
        a_in = mid("a_in", [P, 2, T], R_AT + 8 * K1)
        g_sig = mid("g_sig", [P, 2, T], R_AT + 12 * K1)
        y_mla = mid("y_mla", [P, 4, T], R_AT + 8 * K1)
        hy = mid("hy", [P, 6, T], R_AT + 16 * K1)
        y_conv = mid("y_conv", [P, 2, T], R_AT + 28 * K1)
        PADW = T + TAPS - 1
        conv_pad = mid("conv_pad", [P, 2, PADW], H_AT + 19 * K1)
        f_w1 = mid("f_w1", [EMB, HYF], H_AT)
        f_w23 = mid("f_w23", [HYF, 2, HYF], H_AT + 256)
        f_w4 = mid("f_w4", [HYF, 1024], H_AT + 1 * K1)
        f_z = mid("f_z", [EMB, T], H_AT + 5 * K1)
        f_h = [mid(f"f_h{i}", [HYF, T], H_AT + (7 + 2 * i) * K1) for i in range(2)]
        f_n = mid("f_n", [P, T], H_AT + 11 * K1)
        f_a = mid("f_a", [P, T], H_AT + 13 * K1)
        f_abs = [mid(f"f_abs{i}", [P, T], H_AT + (15 + 2 * i) * K1) for i in range(2)]
        spec = mid("spec", [P, 2, 4, 3, HYC], H_AT)
        dft = mid("dft", [P, 2, TB, T], H_AT + 24 * K1)
        decay = mid("decay", [P, TB, T], H_AT + 40 * K1)
        filt = mid("filt", [P, 2, TB, 2, HYC], U_AT)
        fsum = mid("fsum", [P, TB, 2, HYC], U_AT + 16 * K1)
        fdif = mid("fdif", [P, TB, 2, HYC], U_AT + 24 * K1)
        idft = mid("idft", [P, 2, TB, T], U_AT)
        v_tok = mid("v_tok", [P, TB, HYC], U_AT + 16 * K1)
        y_spec = mid("y_spec", [P, TB, 2, HYC], U_AT + 20 * K1)
        prod = [mid(f"prod{i}", [P, 2, HYC], U_AT + (28 + 2 * i) * K1) for i in range(2)]
        qn, kvn = hm_q[:, 0:2, :], hm_q[:, 2:3, :]
        q_all = mid("q_all", [P, HEADS, T], H_AT + 6 * K1)
        k_all = mid("k_all", [P, HEADS, T], H_AT + 22 * K1)
        v_all = mid("v_all", [P, TB, T], H_AT + 38 * K1)
        kpe_r = mid("kpe_r", [P, T], H_AT + 46 * K1)
        w_qb = mid("w_qb", [P, 2, HEADS * QK], R_AT + 8 * K1)
        w_kvb = mid("w_kvb", [P, 2, T], R_AT + 16 * K1)
        pt = [mid(f"pt{i}", [P, 1, TB, P], U_AT + 2 * i * K1) for i in range(2)]
        y2 = mid("y2", [P, KC, T], R_AT)
        gm0 = mid("gm0", [P, KC, T], R_AT + 16 * K1)
        w_ra = mid("w_ra", [P, 2, KC, P], H_AT)
        xpad = [mid(f"xpad{i}", [P, T + 3], H_AT + 8 * K1 + i * 2080) for i in range(2)]
        xc = [mid(f"xc{i}", [P, T], H_AT + (13 + 2 * i) * K1) for i in range(2)]
        rs = mid("rs", [P, T], H_AT + 17 * K1)
        isg = mid("isg", [P, T], H_AT + 19 * K1)
        th = mid("th", [P, T], H_AT + 21 * K1)
        sqt = mid("sqt", [P, T], H_AT + 23 * K1)
        gel = mid("gel", [P, T], H_AT + 25 * K1)
        gm1 = mid("gm1", [P, T], H_AT + 27 * K1)
        rw = mid("rw", [P, T], H_AT + 29 * K1)
        ra = mid("ra", [P, T], H_AT + 31 * K1)
        ru = mid("ru", [P, T], H_AT + 33 * K1)
        rh = mid("rh", [P, T], H_AT + 35 * K1)
        lamt = mid("lamt", [P, 8, KC], H_AT + 37 * K1)
        mem_t = mid("mem_t", [P, KC, MEM], R_AT + 20 * K1)
        mem_hi = mid("mem_hi", [P, KC, MEM], H_AT + 8 * K1, F32R)
        mem_lo = mid("mem_lo", [P, KC, MEM], H_AT + 16 * K1, F32R)
        kx = mid("kx", [P, 2, MEM], H_AT + 24 * K1)
        vx = mid("vx", [P, 2, MEM], H_AT + 26 * K1)
        qx = mid("qx", [P, 2, T], H_AT + 28 * K1)
        ox = mid("ox", [P, 2, T], H_AT + 32 * K1)
        w_xo = mid("w_xo", [P, 2, D], H_AT + 36 * K1)
        gm2 = [mid(f"gm2{i}", [P, T], H_AT + (44 + 2 * i) * K1) for i in range(2)]
        ptx = [mid(f"ptx{i}", [P, 1, TB, P], R_AT + (16 + 2 * i) * K1) for i in range(2)]
        q2 = mid("q2", [P, KC, T], H_AT)
        k2 = mid("k2", [P, 2, GROUPS, T], H_AT + 16 * K1)
        v2 = mid("v2", [P, 2, TB, 2, P], H_AT + 32 * K1)
        c_raw = mid("c_raw", [P, 4, T], H_AT + 40 * K1)
        w_c1 = mid("w_c1", [P, 16, 256], U_AT)
        c_dup = mid("c_dup", [P, GROUPS, T], U_AT + 16 * K1)
        c_blk = mid("c_blk", [P, 16, GROUPS, NCMP], U_AT + 24 * K1)
        c_hid = mid("c_hid", [P, 2, GROUPS * NCMP], TMP_AT + 7 * KB2)
        w_c2 = mid("w_c2", [P, 2, HD], TMP_AT + 8 * KB2)
        prob2 = [mid(f"prob2{i}", [P, 2, T], U_AT + 4 * i * K1) for i in range(4)]
        pt2 = [mid(f"pt2{i}", [P, 2, TB, P], H_AT + (40 + 4 * i) * K1) for i in range(2)]
        k_cmp = mid("k_cmp", [P, GROUPS, 2, CPAD], TMP_AT + 10 * KB2)
        v_cmp = mid("v_cmp", [2 * CPAD, GROUPS, 2, HD], TMP_AT + 2 * KB2)
        gates = mid("gates", [P, TB, 48], TMP_AT + 3 * KB2)
        cmask = mid("cmask", [P, TB, CPAD], TMP_AT + 3 * KB2 + 768)
        causal = mid("causal", [P, P], TMP_AT + 3 * KB2 + 1280)
        cos_c = mid("cos_c", [HD, 2, GROUPS * NCMP], TMP_AT + 8 * KB2 + 768)

        out_t = mid("out_t", [P, KC, T], H_AT)

        psum = ctx.enter_context(nc.psum_tensor("psum", [P, 8 * T], F32))
        banks = [psum[:, T * i:T * i + T] for i in range(8)]
        ring = banks[0:4]
        score = [psum[:, T * i:T * i + 2 * T].rearrange("p (b n) -> p b n", b=2) for i in (4, 2)]
        product = banks[0:2]
        turned = banks[6:8]

        def sem(name):
            return ctx.enter_context(nc.semaphore(name))

        w_loaded = [sem(f"w_loaded{i}") for i in range(RING)]
        w_hi_ready = sem("w_hi_ready")
        w_split = sem("w_split")
        gemm_done = sem("gemm_done")
        aux_done = sem("aux_done")
        taken = [sem(f"taken{i}") for i in range(4)]
        sq_ready = sem("sq_ready")
        sq_used = sem("sq_used")
        sum_done = sem("sum_done")
        rinv_ready = sem("rinv_ready")
        gate_ready = sem("gate_ready")
        hid_full = sem("hid_full")
        u_full = sem("u_full")
        u_hi_ready = sem("u_hi_ready")
        u_ready = sem("u_ready")
        h_hi_ready = sem("h_hi_ready")
        h_ready = sem("h_ready")
        dve_link = sem("dve_link")
        vec_ready = sem("vec_ready")
        act_ready = sem("act_ready")
        rope_done = sem("rope_done")
        s_full = sem("s_full")
        s_max = sem("s_max")
        exp_done = sem("exp_done")
        p_norm = sem("p_norm")
        t_full = sem("t_full")
        t_taken = sem("t_taken")
        pv_done = sem("pv_done")
        o_taken = sem("o_taken")
        consts_in = sem("consts_in")
        small_in = sem("small_in")
        tables_in = sem("tables_in")
        out_ready = sem("out_ready")
        pool_tick = sem("pool_tick")
        act_tick = sem("act_tick")
        out_written = sem("out_written")

        block = ctx.enter_context(nc.Block())

        def col(name, layer, k, rows=P):
            c = places[(name, layer) if layer is not None else name] + k
            return cols[0:rows, c:c + 1]

        def wait_taken(eng, m, i=None):
            eng.wait_ge(taken[m % 4], at_turn(m // 4 + 1, 1, i))

        def weights(n, k):
            hi = w_hi[n % SPLIT][:, 0:k * P].rearrange("p (k n) -> p k n", n=P)
            lo = w_lo[n % SPLIT][:, 0:k * P].rearrange("p (k n) -> p k n", n=P)
            return hi, lo

        SINES = (5, 7, 9)

        ORDER = range(TB)
        KEEP = [full[0], full[1], full[2], sg[0]]

        def unit(**kw):
            kw["rows"] = slice(0, P) if kw["kind"] == "cmp" else \
                slice(HD * (kw["head"] % 2), HD * (kw["head"] % 2) + HD)
            kw["closes"] = kw["kind"] == "cmp" or kw["head"] % 2 == 1 and kw["i"] == ORDER[-1]
            kw["opens"] = kw["kind"] == "cmp" or kw["head"] % 2 == 0 and kw["i"] == ORDER[0]
            kw["chunks"] = [(t, 2 * CPAD) for t in range(TB)] if kw["kind"] == "cmp" else \
                [(c, P) for c in range(kw["n"] // P)]
            return kw

        def mla_units():
            return [unit(head=h, i=i, kind="plain", scale=QK ** -0.5, n=T, keep=KEEP, pt=pt,
                         qk=[(0, q_all[0:QK, h, P * i:P * i + P], k_all[0:QK, h, :])],
                         v=[[v_all[:, j, VDIM * h:VDIM * h + VDIM] for j in range(TB)]])
                    for h in range(HEADS) for i in ORDER]

        def cross_units():
            return [unit(head=h, i=i, kind="plain", scale=HD ** -0.5, n=MEM, keep=KEEP, pt=ptx,
                         qk=[(0, qx[HD * (h % 2):HD * (h % 2) + HD, h // 2, P * i:P * i + P],
                              kx[HD * (h % 2):HD * (h % 2) + HD, h // 2, :])],
                         v=[[vx[:, j, HD * h:HD * h + HD] for j in range(MEM // P)]])
                    for h in range(XHEADS) for i in ORDER]

        def nsa_units(compressed):
            out = []
            for h in range(HEADS2):
                g = h // (HEADS2 // GROUPS)
                r = slice(HD * (h % 2), HD * (h % 2) + HD)
                q = [q2[r, h // 2, P * i:P * i + P] for i in range(TB)]
                if compressed:
                    if h % 2 == 0:
                        out.append(unit(head=h, i=None, kind="cmp", scale=HD ** -0.5, n=None, keep=prob2, pt=pt2,
                                        qk=[(i, q2[:, h // 2, P * i:P * i + P],
                                             k_cmp[:, g, :, :].rearrange("p e n -> p (e n)")) for i in range(TB)],
                                        v=[v_cmp[:, g, :, :].rearrange("p e c -> p (e c)")],
                                        gate=gates[:, :, 3 * h:3 * h + 6]
                                        .rearrange("p t (e k) -> p t e k", k=3)[:, :, :, 0]))
                    continue
                for i in ORDER:
                    n = P * (i + 1)
                    out.append(unit(head=h, i=i, kind="pair", scale=HD ** -0.5, n=n, keep=prob2, pt=pt2,
                                    qk=[(b, q[i], k2[r, b, g, 0:n]) for b in range(2)],
                                    v=[[v2[:, b, j, g // 2, HD * (g % 2):HD * (g % 2) + HD]
                                        for j in range(i + 1)] for b in range(2)],
                                    gate=gates[:, i, 3 * h + 1:3 * h + 3]))
            return out

        def parts_of(units, s):
            return sum(len(u["v"]) for u in units[0:max(s, 0)])

        TURN, VALUES = 3, 4

        @block.sync
        def _(sp):
            sp.dma_start(x[:, :, :], d["xt"]).then_inc(consts_in, 16)
            sp.dma_start(cols[:, :], d["cols"]).then_inc(consts_in, 16)
            sp.dma_start(ident[:, :], d["ident"]).then_inc(consts_in, 16)
            n = 0
            for k, first, count in plan:
                src = d[f"w{k}"]

                def load(j, i=None):
                    slot = (n + j) % RING
                    if i is not None or n + j >= RING:
                        sp.wait_ge(w_split, at_turn(n + j - RING + 1, RING, i))
                    index = first + j if i is None else i * RING + (first + j)
                    block_ = src[bass.ds(index, 1)].rearrange("o p f -> (o p) f")
                    sp.dma_start(w_raw[slot][:, 0:k * P], block_).then_inc(w_loaded[slot], 16)

                if count % RING:
                    for j in range(count):
                        load(j)
                else:
                    for j in range(RING):
                        load(j)
                    with sp.Fori(1, count // RING) as i:
                        for j in range(RING):
                            load(j, i)
                n += count
            for c in range(KC):
                sp.wait_ge(out_ready, c + 1)
                sp.dma_start(d["out"][:, c, :], out_t[:, c, :]).then_inc(out_written, 16)
            sp.wait_ge(out_written, 16 * KC)

        @block.gpsimd
        def _(pool):
            n = 0
            for k, first, count in plan:
                def split(j, i=None):
                    m = n + j
                    raw = w_raw[m % RING][:, 0:k * P]
                    hi = w_hi[m % SPLIT][:, 0:k * P]
                    lo = w_lo[m % SPLIT][:, 0:k * P]
                    pool.wait_ge(w_loaded[m % RING], at_turn(16 * (m // RING + 1), 16, i))
                    if i is not None:
                        pool.sem_inc(pool_tick, 1)
                    if i is not None or m >= SPLIT:
                        pool.wait_ge(gemm_done, at_turn(m - SPLIT + 1, RING, i))
                        if i is not None:
                            pool.sem_inc(pool_tick, 1)
                    pool.tensor_scalar(hi, raw, 1.0, 1.0, ALU.mult, ALU.mult).then_inc(w_hi_ready, 1)
                    pool.wait_ge(w_hi_ready, at_turn(m + 1, RING, i))
                    pool.tensor_tensor(lo, raw, hi.bitcast(F32), ALU.subtract).then_inc(w_split, 1)

                if count % RING:
                    for j in range(count):
                        split(j)
                else:
                    for j in range(RING):
                        split(j)
                    with pool.Fori(1, count // RING) as i:
                        for j in range(RING):
                            split(j, i)
                n += count

        @block.tensor
        def _(pe):
            w = Walk()

            def open_bank(m, i=None):
                if i is not None or m >= 4:
                    pe.wait_ge(taken[m % 4], at_turn(m // 4, 1, i))
                return ring[m % 4]

            def multiply(n, out, k, rhs_hi, rhs_lo, i=None, ready=None, order=None):
                pe.wait_ge(w_split, at_turn(n + 1, RING, i))
                hi, lo = weights(n, k)
                for s, c in enumerate(order or range(k)):
                    if ready is not None:
                        ready(s)
                    pe.matmul(out, hi[:, c, :], rhs_hi(c), start=(s == 0), stop=False)
                    pe.matmul(out, hi[:, c, :], rhs_lo(c), start=False, stop=False)
                    mm = pe.matmul(out, lo[:, c, :], rhs_hi(c), start=False, stop=(s == k - 1))
                mm.then_inc(gemm_done, 1)

            def of_u(ready=None):
                n, m = w.gemm()
                multiply(n, open_bank(m)[:, :], KC, lambda c: u_hi[:, c, :], lambda c: u_lo[:, c, :],
                         ready=ready)

            def u_arrives(c):
                pe.wait_ge(u_ready, w.split - KC + c + 1)

            def norm(tiles, size=T, split=True):
                m = w.bank()
                out = open_bank(m)
                for c in range(tiles):
                    pe.wait_ge(sq_ready, w.sq + 1)
                    pe.matmul(out[:, 0:size], ones[:, :], sq[w.sq % 2][:, 0:size], start=(c == 0),
                              stop=(c == tiles - 1)).then_inc(sq_used, 1)
                    w.sq += 1
                w.full += tiles
                w.norm += 1
                if split:
                    w.split += tiles

            def norm_x(split=True):
                m = w.bank()
                out = open_bank(m)
                w.sq += KC
                pe.wait_ge(sq_used, w.sq)
                pe.matmul(out[:, :], ones[:, :], std[:, :], start=True, stop=True).then_inc(sum_done, 1)
                w.full += KC
                w.norm += 1
                if split:
                    w.split += KC

            def looped(count, body):
                for j in range(4):
                    body(j, None)
                with pe.Fori(1, count // 4) as i:
                    for j in range(4):
                        body(j, i)
                w.n += count
                w.m += count

            def ffn(parts, per):
                for p, part in enumerate(parts):
                    def up(j, i):
                        ready = u_arrives if i is None and j == 0 and p == 0 else None
                        multiply(w.n + j, open_bank(w.m + j, i)[:, :], KC, lambda c: u_hi[:, c, :],
                                 lambda c: u_lo[:, c, :], i, ready)

                    looped(per * part, up)

                    def down(j, i):
                        ready = (lambda c: pe.wait_ge(h_ready, w.hid + c + 1)) if i is None and j == 0 else None
                        multiply(w.n + j, open_bank(w.m + j, i)[:, :], part, lambda c: h_hi[:, c, :],
                                 lambda c: h_lo[:, c, :], i, ready)

                    looped(8, down)
                    w.hid += part

            def attention(units):
                u0, p0 = w.unit, w.part
                for m in range(w.m - 4, w.m):
                    wait_taken(pe, m)
                for s in range(len(units) + VALUES):
                    if s < len(units):
                        u = units[s]
                        if s >= 2:
                            pe.wait_ge(exp_done, p0 + parts_of(units, s - 1))
                        for b, q, key in u["qk"]:
                            out = score[s % 2][:, 0, 2 * CPAD * b:2 * CPAD * (b + 1)] if u["kind"] == "cmp" else \
                                score[s % 2][:, b, 0:u["n"]]
                            mm = pe.matmul(out, q, key, start=True, stop=True, skip_group_check=True)
                        mm.then_inc(s_full, 1)
                    if 0 <= s - TURN < len(units):
                        u, k = units[s - TURN], u0 + s - TURN
                        p = p0 + parts_of(units, s - TURN)
                        keep = u["keep"][k % 4]
                        for b in range(len(u["v"])):
                            pe.wait_ge(p_norm, p + b + 1)
                            if p + b >= 2:
                                pe.wait_ge(t_taken, p + b - 1)
                            for c, rows in u["chunks"]:
                                if u["kind"] == "plain":
                                    src = keep[:, P * c:P * c + P]
                                elif u["kind"] == "pair":
                                    src = keep[:, b, P * c:P * c + P]
                                else:
                                    src = keep[:, 0, rows * c:rows * c + rows]
                                mm = pe.transpose(turned[(p + b) % 2][0:rows, P * c:P * c + P], src, ident[:, :])
                            mm.then_inc(t_full, 1)
                    if s >= VALUES:
                        u, k = units[s - VALUES], u0 + s - VALUES
                        buf = u["pt"][k % 2]
                        out = product[w.item % 2][u["rows"], :]
                        pe.wait_ge(t_taken, p0 + parts_of(units, s - VALUES + 1))
                        if u["opens"] and w.item >= 2:
                            pe.wait_ge(o_taken, w.item - 1)
                        if u["kind"] == "cmp":
                            mm = pe.matmul(out, u["v"][0], buf[0:2 * CPAD, 0, :, :].rearrange("p c q -> p (c q)"),
                                           start=True, stop=True, skip_group_check=True)
                        else:
                            for b, values in enumerate(u["v"]):
                                for c, rows in u["chunks"]:
                                    mm = pe.matmul(out[:, P * u["i"]:P * u["i"] + P], values[c], buf[:, b, c, :],
                                                   start=(b == 0 and c == 0),
                                                   stop=(b == len(u["v"]) - 1 and c == len(values) - 1),
                                                   skip_group_check=True)
                        mm.then_inc(pv_done, 1)
                        if u["closes"]:
                            w.item += 1
                w.unit += len(units)
                w.part += parts_of(units, len(units))
                pe.wait_ge(o_taken, w.item)

            def rope_product(raw, rows, cols_, m_raw):
                a, m = w.small()
                out = open_bank(m)
                if m_raw is not None:
                    wait_taken(pe, m_raw)
                pe.matmul(out[0:rows, 0:cols_], rot[0:rows, 0:rows], raw, start=True,
                          stop=True).then_inc(aux_done, 1)
                w.rope += 1

            def mixer(layer):
                norm_x()
                w.loads += 4
                for k in range(14):
                    of_u(u_arrives if k == 0 else None)
                    if k in SINES:
                        l = SINES.index(k)
                        pe.wait_ge(small_in, 16 * w.loads)
                        a, m = w.small()
                        if l == 0:
                            lhs, rhs = f_w1[:, :], f_z[:, :]
                        else:
                            pe.wait_ge(act_ready, w.act + l)
                            lhs, rhs = f_w23[:, l - 1, :], f_h[(l - 1) % 2][:, :]
                        pe.matmul(open_bank(m)[0:HYF, :], lhs, rhs, start=True, stop=True).then_inc(aux_done, 1)
                w.act += 3
                w.vec += 3
                pe.wait_ge(act_ready, w.act)
                for t in range(TB):
                    for o in range(2):
                        a, m = w.small()
                        pe.matmul(open_bank(m)[:, :], f_h[0][:, P * t:P * t + P],
                                  f_w4[:, T * o:T * o + T], start=True, stop=True).then_inc(aux_done, 1)
                outs = [open_bank(w.bank()) for _ in range(2)]
                for t in range(TB):
                    for o in range(2):
                        pe.wait_ge(sq_ready, w.sq + 1)
                        for b in range(2):
                            mm = pe.matmul(outs[o][:, 0:HYC], ones[:, :],
                                           f_abs[o][:, HYC * b:HYC * b + HYC],
                                           start=(t == 0 and b == 0), stop=(t == TB - 1 and b == 1))
                        mm.then_inc(sq_used, 1)
                        w.sq += 1
                w.tables += 3
                pe.wait_ge(tables_in, 16 * (w.tables - 1))
                pe.wait_ge(vec_ready, w.vec + 9)
                for j in range(TB):
                    for part, src in ((0, fsum), (1, fdif)):
                        a, m = w.small()
                        out = open_bank(m)
                        for t in range(TB):
                            mm = pe.matmul(out[:, :], dft[:, part, t, P * j:P * j + P],
                                           src[:, t, :, :].rearrange("p o c -> p (o c)"),
                                           start=(t == 0), stop=(t == TB - 1))
                        mm.then_inc(aux_done, 1)
                    if j == 0:
                        pe.wait_ge(vec_ready, w.vec + 11)
                        a, m = w.small()
                        out = open_bank(m)
                        for t in range(2):
                            mm = pe.matmul(out[:, :], ones[:, :], y_conv[:, t, :], start=(t == 0), stop=(t == 1))
                        mm.then_inc(aux_done, 1)
                    elif j == 1:
                        norm(2, split=False)
                        w.full -= 2
                    elif j == 2:
                        norm(2, split=False)
                    else:
                        norm(1, split=False)
                w.vec += 16
                w.act += 2
                for o in range(2):
                    v0 = w.vec
                    if o == 1:
                        pe.wait_ge(vec_ready, v0)
                    jobs = []
                    for t in range(TB):
                        a, m = w.small()
                        out = open_bank(m)
                        for c in range(2):
                            mm = pe.transpose(out[:, P * c:P * c + P], hy[:, 2 * o + c, P * t:P * t + P],
                                              ident[:, :])
                        mm.then_inc(aux_done, 1)
                        jobs.append(m)
                    for m in jobs:
                        wait_taken(pe, m)
                    for j in range(TB):
                        a, m = w.small()
                        out = open_bank(m)
                        for part in range(2):
                            for t in range(TB):
                                mm = pe.matmul(out[:, HYC * part:HYC * part + HYC],
                                               dft[:, part, t, P * j:P * j + P], v_tok[:, t, :],
                                               start=(t == 0), stop=(t == TB - 1), skip_group_check=True)
                        mm.then_inc(aux_done, 1)
                    if o == 0:
                        norm(2, split=False)
                        pe.wait_ge(tables_in, 16 * w.tables)
                    for c in range(2):
                        a, m = w.small()
                        out = open_bank(m)
                        for j in range(TB):
                            if c == 0:
                                pe.wait_ge(vec_ready, v0 + j + 1)
                            for part in range(2):
                                mm = pe.matmul(out[:, :], y_spec[:, j, part, P * c:P * c + P],
                                               idft[:, part, j, :], start=(j == 0 and part == 0),
                                               stop=(j == TB - 1 and part == 1))
                        mm.then_inc(aux_done, 1)
                    w.vec += TB + 2
                w.loads += 2
                pe.wait_ge(small_in, 16 * w.loads)
                pe.wait_ge(u_full, w.full)
                for t in range(TB):
                    a, m = w.small()
                    pe.matmul(open_bank(m)[:, :], kvn[:, 0, P * t:P * t + P], w_kvb[:, 1, :], start=True,
                              stop=True).then_inc(aux_done, 1)
                norm(2, split=False)
                for h in range(0, HEADS, 2):
                    a, m = w.small()
                    pe.matmul(open_bank(m)[:, :], w_kvb[:, 0, NOPE * h:NOPE * h + P], kvn[:, 0, :],
                              start=True, stop=True).then_inc(aux_done, 1)
                rope_product(hm_q[0:QK, 3, :], QK, T, None)
                prev = None
                for h in range(HEADS + 1):
                    this = None
                    if h < HEADS:
                        a, m = w.small()
                        out = open_bank(m)
                        for c in range(2):
                            mm = pe.matmul(out[0:QK, :], w_qb[:, c, QK * h:QK * h + QK], qn[:, c, :],
                                           start=(c == 0), stop=(c == 1))
                        mm.then_inc(aux_done, 1)
                        this = m
                    if prev is not None:
                        rope_product(htmp[(h - 1) % 2][0:QK, :], QK, T, prev)
                    prev = this
                pe.wait_ge(rope_done, w.rope)
                w.vec += 1
                pe.wait_ge(vec_ready, w.vec)
                attention(mla_units())
                norm(4)
                w.split += 4

                def project(j, i):
                    ready = u_arrives if i is None and j == 0 else None
                    multiply(w.n + j, open_bank(w.m + j, i)[:, :], KC, lambda c: u_hi[:, c, :],
                             lambda c: u_lo[:, c, :], i, ready, order=(4, 5, 6, 7, 0, 1, 2, 3))

                looped(8, project)

            pe.wait_ge(consts_in, 16 * 3)
            pe.wait_ge(vec_ready, 1)
            w.vec += 1
            w.loads += 2
            for layer in range(DEPTH):
                norm_x()
                ffn(PARTS, 2)
                if layer == 0:
                    w.vec += 2
                    w.act += 2
                mixer(layer)
                norm_x()
                ffn(PARTS, 2)
            norm_x(split=False)

            norm(KC)
            w.loads += 2
            w.vec += 1
            w.act += 2
            for t in range(KC):
                for k in range(3):
                    of_u(u_arrives if t == 0 and k == 0 else None)
                w.vec += 1
                if t == 0:
                    pe.wait_ge(small_in, 16 * w.loads)
                pe.wait_ge(vec_ready, w.vec)
                for k in range(2):
                    a, m = w.small()
                    pe.matmul(open_bank(m)[:, :], w_ra[:, k, t, :], xc[t % 2][:, :], start=True,
                              stop=True).then_inc(aux_done, 1)
                w.act += 2
                w.vec += 1
            w.loads += 1
            for k in range(2):
                of_u()
            norm(KC, size=MEM)
            for k in range(2):
                n, m = w.gemm()
                multiply(n, open_bank(m)[:, 0:MEM], KC, lambda c: mem_hi[:, c, :],
                         lambda c: mem_lo[:, c, :], ready=u_arrives if k == 0 else None)
            for k in range(2):
                n, m = w.gemm()
                out = open_bank(m)
                pe.wait_ge(w_split, n + 1)
                hi, lo = weights(n, KC)
                for tc in range(2):
                    for c in range(KC):
                        for q, (a_, b_) in enumerate(((mem_hi, hi), (mem_lo, hi), (mem_hi, lo))):
                            mm = pe.matmul(out[:, P * tc:P * tc + P], a_[:, c, P * tc:P * tc + P], b_[:, c, :],
                                           start=(c == 0 and q == 0), stop=(c == KC - 1 and q == 2),
                                           skip_group_check=True)
                mm.then_inc(gemm_done, 1)
            attention(cross_units())
            pe.wait_ge(small_in, 16 * w.loads)
            for t in range(KC):
                of_u()
                a, m = w.small()
                out = open_bank(m)
                for c in range(2):
                    mm = pe.matmul(out[:, :], w_xo[:, c, P * t:P * t + P], ox[:, c, :], start=(c == 0),
                                   stop=(c == 1))
                mm.then_inc(aux_done, 1)
            w.vec += KC
            w.loads += 3
            pe.wait_ge(small_in, 16 * w.loads)
            prev = None
            for k in range(13):
                this = None
                if k < 12:
                    of_u()
                    this = w.m - 1
                if prev is not None:
                    rope_product(htmp[(k - 1) % 2][:, :], P, T, prev)
                prev = this
            for k in range(4):
                of_u()
                src = w.m - 1
                a, m = w.small()
                out = open_bank(m)
                wait_taken(pe, src)
                for t in range(TB):
                    mm = pe.transpose(out[:, P * t:P * t + P], sg[k % 2][:, P * t:P * t + P], ident[:, :])
                mm.then_inc(aux_done, 1)
            of_u()
            src = w.m - 1
            a, m = w.small()
            out = open_bank(m)
            wait_taken(pe, src)
            for t in range(TB):
                mm = pe.transpose(out[:, 48 * t:48 * t + 48], sg[0][0:48, P * t:P * t + P], ident[0:48, 0:48])
            mm.then_inc(aux_done, 1)
            for k in range(4 + KC):
                of_u()
            for side in range(2):
                w.loads += 5 if side == 0 else 2
                pe.wait_ge(small_in, 16 * w.loads)
                w.vec += 1
                pe.wait_ge(vec_ready, w.vec)
                hid = []
                for mh in range(2):
                    a, m = w.small()
                    out = open_bank(m)
                    for c in range(16):
                        mm = pe.matmul(out[:, 0:GROUPS * NCMP], w_c1[:, c, P * mh:P * mh + P],
                                       c_blk[:, c, :, :].rearrange("p g n -> p (g n)"), start=(c == 0),
                                       stop=(c == 15))
                    mm.then_inc(aux_done, 1)
                    hid.append(m)
                for m in hid:
                    wait_taken(pe, m)
                a, m = w.small()
                out = open_bank(m)
                if side == 0:
                    for mh in range(2):
                        mm = pe.matmul(out[0:HD, 0:GROUPS * NCMP], w_c2[:, mh, :], c_hid[:, mh, :],
                                       start=(mh == 0), stop=(mh == 1))
                    mm.then_inc(aux_done, 1)
                    rope_product(htmp[0][0:HD, 0:GROUPS * NCMP], HD, GROUPS * NCMP, m)
                else:
                    for r in (0, CPAD):
                        for g in range(GROUPS):
                            for mh in range(2):
                                mm = pe.matmul(out[r:r + NCMP, HD * g:HD * g + HD],
                                               c_hid[:, mh, NCMP * g:NCMP * g + NCMP], w_c2[:, mh, :],
                                               start=(mh == 0), stop=(mh == 1), skip_group_check=True)
                    mm.then_inc(aux_done, 1)
                    wait_taken(pe, m)
            pe.wait_ge(rope_done, w.rope)
            attention(nsa_units(True))
            attention(nsa_units(False))
            w.split += KC

            def project2(j, i):
                ready = u_arrives if i is None and j == 0 else None
                multiply(w.n + j, open_bank(w.m + j, i)[:, :], KC, lambda c: u_hi[:, c, :],
                         lambda c: u_lo[:, c, :], i, ready)

            looped(8, project2)
            norm_x()
            ffn(PARTS2, 1)
            norm_x(split=False)

        @block.scalar
        def _(act):
            w = Walk()

            def done(n, i=None):
                act.wait_ge(gemm_done, at_turn(n + 1, 4, i))

            def take(dst, src, m, func=ACT.Copy, **kw):
                return act.activation(dst, src, func, **kw).then_inc(taken[m % 4], 1)

            def small_load(dst, src):
                act.dma_start(dst, src).then_inc(small_in, 16)
                w.loads += 1

            def to_high(dst):
                act.wait_ge(u_full, w.full + 1)
                act.activation(dst, full[w.split % 3][:, 0:dst.shape[-1]], ACT.Copy).then_inc(u_hi_ready, 1)
                w.full += 1
                w.split += 1

            def norm(srcs, dim, ready, highs=None, size=T, between=None):
                for c, s in enumerate(srcs):
                    ready(c)
                    if w.sq >= 2:
                        act.wait_ge(sq_used, w.sq - 1)
                    act.activation(sq[w.sq % 2][:, 0:size], s, ACT.Square).then_inc(sq_ready, 1)
                    w.sq += 1
                if between is not None:
                    between()
                m = w.bank()
                act.wait_ge(sq_used, w.sq)
                if w.norm:
                    act.wait_ge(rinv_ready, w.norm)
                take(std[:, 0:size], ring[m % 4][:, 0:size], m, ACT.Sqrt, scale=1.0 / dim, bias=col("eps", None, 0))
                w.norm += 1
                if highs is None:
                    w.full += len(srcs)
                else:
                    for dst in highs:
                        to_high(dst)

            def norm_x(ready, scaled_later=False, split=True, over_operands=False):
                for c in range(KC):
                    ready(c)
                    if w.sq >= 2:
                        act.wait_ge(sq_used, w.sq - 1)
                    act.activation(sq[w.sq % 2][:, :], x[:, c, :], ACT.Square).then_inc(sq_ready, 1)
                    w.sq += 1
                    if scaled_later and not over_operands:
                        to_high(u_hi[:, c, :])
                if over_operands:
                    for c in range(KC):
                        to_high(u_hi[:, c, :])
                m = w.bank()
                w.sums += 1
                act.wait_ge(sum_done, w.sums)
                if w.norm:
                    act.wait_ge(rinv_ready, w.norm)
                take(std[:, :], ring[m % 4][:, :], m, ACT.Sqrt, scale=1.0 / D, bias=col("eps", None, 0))
                w.norm += 1
                if not split:
                    w.full += KC
                elif not scaled_later:
                    for c in range(KC):
                        to_high(u_hi[:, c, :])

            def high_tiles(a=0, b=KC):
                return [u_hi[:, c, :] for c in range(a, b)]

            def x_updated(c):
                wait_taken(act, w.m - KC + c)

            def looped(count, per, body):
                body(None)
                with act.Fori(1, count // per) as i:
                    body(i)

            def ffn(parts, per):
                for part in parts:
                    def chunk(i, c):
                        if per == 2:
                            wait_taken(act, w.m + 2 * c, i)
                            act.activation(sg[c % 2][:, :], full[c % 2][:, :], ACT.Silu).then_inc(gate_ready, 1)
                        else:
                            m = w.m + c
                            done(w.n + c, i)
                            act.activation(sg[c % 2][:, :], ring[m % 4][:, :], ACT.Relu)\
                               .then_inc(act_ready, 1)
                        act.wait_ge(hid_full, at_turn(w.hid + c + 1, 4 // per, i))
                        act.sem_inc(act_tick, 1)
                        dst = h_hi[:, c, :] if i is None else \
                            h_hi[:, bass.ds(i * (4 // per) + c, 1), :].rearrange("p o t -> p (o t)")
                        act.activation(dst, htmp[c % 2][:, :], ACT.Copy).then_inc(h_hi_ready, 1)

                    def turn(i):
                        for c in range(4 // per):
                            chunk(i, c)

                    looped(per * part, 4, turn)
                    w.n += per * part
                    w.m += per * part
                    w.hid += part
                    if per == 1:
                        w.act += part
                    w.n += 8
                    w.m += 8

            def attention(units):
                u0, p0 = w.unit, w.part
                for s in range(len(units) + TURN):
                    if s < len(units):
                        u, k = units[s], u0 + s
                        n, j = u["n"], k % 8
                        keep, sc = u["keep"][k % 4], score[s % 2]
                        act.wait_ge(s_max, k + 1)
                        if s >= 4:
                            act.wait_ge(t_full, p0 + parts_of(units, s - 3))
                        if u["kind"] == "cmp":
                            flat = keep[:, 0, 0:2 * TB * CPAD]
                            act.activation(flat, flat, ACT.Exp, scale=u["scale"]).then_inc(exp_done, 1)
                        elif u["kind"] == "pair":
                            act.activation(e0[:, j, 0:1], nb[:, j, 1:2], ACT.Exp).then_inc(act_tick, 1)
                            for b in range(2):
                                act.activation(keep[:, b, 0:n], sc[:, b, 0:n], ACT.Exp, bias=nb[:, j, b:b + 1],
                                               scale=u["scale"], accum_out=sums[:, j, b:b + 1])\
                                   .then_inc(exp_done, 1)
                        else:
                            act.activation(keep[:, 0:n], sc[:, 0, 0:n], ACT.Exp, bias=nb[:, j, 0:1],
                                           scale=u["scale"], accum_out=sums[:, j, 0:1]).then_inc(exp_done, 1)
                    if s >= TURN:
                        u, k = units[s - TURN], u0 + s - TURN
                        p = p0 + parts_of(units, s - TURN)
                        if k >= 2:
                            act.wait_ge(pv_done, k - 1)
                        for b in range(len(u["v"])):
                            act.wait_ge(t_full, p + b + 1)
                            nch, rows = len(u["chunks"]), u["chunks"][0][1]
                            act.activation(u["pt"][k % 2][0:rows, b, 0:nch, :],
                                           turned[(p + b) % 2][0:rows, 0:P * nch]
                                           .rearrange("p (c q) -> p c q", q=P), ACT.Copy).then_inc(t_taken, 1)
                w.unit += len(units)
                w.part += parts_of(units, len(units))
                w.item += sum(u["closes"] for u in units)

            def small_done(a):
                act.wait_ge(aux_done, a + 1)

            def mixer(layer):
                norm_x(x_updated)
                if layer == 0:
                    act.wait_ge(vec_ready, w.vec + 1)
                    act.activation(sinq[0:QK, :], f_a[0:QK, :], ACT.Sin).then_inc(act_ready, 1)
                    act.wait_ge(vec_ready, w.vec + 2)
                    act.activation(cosq[0:QK, :], f_n[0:QK, :], ACT.Sin).then_inc(act_ready, 1)
                    w.vec += 2
                    w.act += 2
                small_load(f_w1[:, :], d["f_w1"][layer])
                small_load(f_w23[:, :, :], d["f_w23"][layer])
                small_load(f_w4[:, :], d["f_w4"][layer])
                small_load(f_z[:, :], d["f_z"])
                act.dma_start(decay[:, :, :], d["decay"]).then_inc(tables_in, 16)
                act.dma_start(dft[:, :, :, :], d["dft"]).then_inc(tables_in, 16)
                w.tables += 3
                latents = []
                for k in range(14):
                    n, m = w.gemm()
                    if 2 <= k < 4:
                        done(n)
                        take(g_sig[:, k - 2, :], ring[m % 4][:, :], m, ACT.Sigmoid)
                    elif 4 <= k < 8:
                        done(n)
                        take(hm_q[:, k - 4, :], ring[m % 4][:, :], m)
                        latents.append(m)
                    if k in SINES:
                        l = SINES.index(k)
                        w.small()
                        act.wait_ge(vec_ready, w.vec + l + 1)
                        act.activation(f_h[l % 2][:, :], f_a[0:HYF, :], ACT.Sin).then_inc(act_ready, 1)
                w.vec += 3
                w.act += 3
                places_ = [w.small()[1] for _ in range(8)]
                for t in range(TB):
                    for o in range(2):
                        wait_taken(act, places_[2 * t + o])
                        if t:
                            act.wait_ge(sq_used, w.sq - 1)
                        act.activation(f_abs[o][:, :],
                                       filt[:, o, t, :, :].rearrange("p b c -> p (b c)"), ACT.Abs)\
                           .then_inc(sq_ready, 1)
                        w.sq += 1
                for _ in range(2):
                    w.bank()
                act.wait_ge(sq_used, w.sq)
                act.wait_ge(vec_ready, w.vec + 9)
                act.dma_start(idft[:, :, :, :], d["idft"]).then_inc(tables_in, 16)
                small_load(w_qb[:, :, :], d["w_qb"][layer])
                v0 = w.vec + 11
                for j in range(TB):
                    w.small()
                    w.small()
                    if j == 0:
                        w.small()
                    elif j == 1:
                        norm([y_conv[:, t, :] for t in range(2)], CONVC,
                             lambda t: act.wait_ge(vec_ready, v0 + 1 + t))
                        w.full -= 2
                        for t in range(2):
                            act.wait_ge(vec_ready, v0 + 3 + t)
                            act.activation(y_conv[:, t, :], y_conv[:, t, :], ACT.Silu,
                                           bias=col("ln_b", layer, t)).then_inc(act_ready, 1)
                        w.act += 2
                    elif j == 2:
                        norm([hm_q[:, 0, :], hm_q[:, 1, :]], QRANK, lambda c: wait_taken(act, latents[c]))
                    else:
                        norm([hm_q[:, 2, :]], KVRANK, lambda c: wait_taken(act, latents[2]))
                w.vec += 16
                for o in range(2):
                    if o == 1:
                        act.wait_ge(vec_ready, w.vec)
                        small_load(w_kvb[:, :, :], d["w_kvb"][layer])
                    for t in range(TB):
                        a, m = w.small()
                        small_done(a)
                        take(v_tok[:, t, :], ring[m % 4][:, 0:HYC], m)
                    w.aux += TB
                    w.m += TB
                    if o == 0:
                        norm([y_conv[:, t, :] for t in range(2)], CONVC, lambda t: act.wait_ge(act_ready, w.act))
                    w.aux += 2
                    w.m += 2
                    w.vec += TB + 2
                for c in range(2):
                    act.wait_ge(vec_ready, w.vec)
                    act.wait_ge(sq_used, w.sq - 1)
                    act.activation(sq[w.sq % 2][:, :], hy[:, 4 + c, :], ACT.Square).then_inc(sq_ready, 1)
                    w.sq += 1
                for t in range(TB):
                    a, m = w.small()
                    small_done(a)
                    take(v_all[:, t, :], ring[m % 4][:, :], m)
                norm([], HYC, None)
                w.full += 2
                for h in range(0, HEADS, 2):
                    a, m = w.small()
                    small_done(a)
                    act.activation(k_all[0:NOPE, h, :], ring[m % 4][0:NOPE, :], ACT.Copy)
                    take(k_all[0:NOPE, h + 1, :], ring[m % 4][NOPE:P, :], m)
                w.small()
                w.rope += 1
                for h in range(HEADS + 1):
                    if h < HEADS:
                        a, m = w.small()
                        small_done(a)
                        if h >= 2:
                            act.wait_ge(rope_done, w.rope)
                        take(htmp[h % 2][0:QK, :], ring[m % 4][0:QK, :], m)
                    if h >= 1:
                        w.small()
                        w.rope += 1
                w.vec += 1
                attention(mla_units())
                act.wait_ge(o_taken, w.item)

                def convolutions_high():
                    act.wait_ge(u_full, w.full)
                    for c in range(4):
                        src = y_conv[:, c, :] if c < 2 else hy[:, 2 + c, :]
                        act.activation(u_hi[:, 4 + c, :], src, ACT.Copy).then_inc(u_hi_ready, 1)
                    w.split += 4

                norm([y_mla[:, c, :] for c in range(4)], 512, lambda c: None, high_tiles(0, 4),
                     between=convolutions_high)
                w.n += 8
                w.m += 8

            act.dma_start(rot[:, :], d["rot1"]).then_inc(small_in, 16)
            act.dma_start(cosq[0:QK, :].bitcast(I32), d["positions"]).then_inc(small_in, 16)
            w.loads += 2
            act.wait_ge(consts_in, 16 * 3)
            w.vec += 1
            for layer in range(DEPTH):
                norm_x((lambda c: None) if layer == 0 else x_updated, scaled_later=True)
                ffn(PARTS, 2)
                mixer(layer)
                norm_x(x_updated, scaled_later=True, over_operands=True)
                ffn(PARTS, 2)
            norm_x(x_updated, split=False)

            u0 = w.full
            norm([x[:, c, :] for c in range(KC)], D, lambda c: act.wait_ge(u_full, u0 - KC + c + 1), high_tiles())
            small_load(w_ra[:, :, :, :], d["w_ra"])
            small_load(mem_t[:, :, :], d["mem_t"])
            act.activation(lamt[:, 0, :], cols[:, places["lam"]:places["lam"] + KC], ACT.Abs)\
               .then_inc(act_ready, 1)
            act.wait_ge(act_ready, w.act + 1)
            act.activation(lamt[:, 1, :], lamt[:, 0, :], ACT.Exp, scale=-1.0).then_inc(act_ready, 1)
            w.act += 2
            w.vec += 1
            for t in range(KC):
                n, m = w.gemm()
                done(n)
                if t >= 2:
                    act.wait_ge(vec_ready, w.vec - 3)
                take(xpad[t % 2][:, 3:T + 3], ring[m % 4][:, :], m)
                n, m = w.gemm()
                done(n)
                act.wait_ge(vec_ready, w.vec)
                take(gel[:, :], ring[m % 4][:, :], m, ACT.Gelu_apprx_tanh)
                n, m = w.gemm()
                done(n)
                take(gm1[:, :], ring[m % 4][:, :], m, ACT.Sigmoid)
                w.vec += 1
                for k, (dst, b) in enumerate(((rs, "b_a"), (isg, "b_i"))):
                    a, m = w.small()
                    small_done(a)
                    take(dst[:, :], ring[m % 4][:, :], m, ACT.Sigmoid, bias=col(b, None, t))
                    if k == 0:
                        m_r = m
                wait_taken(act, m_r)
                act.activation(th[:, :], rs[:, :], ACT.Tanh, scale=lamt[:, 7, t:t + 1]).then_inc(act_ready, 1)
                act.wait_ge(act_ready, w.act + 1)
                act.activation(sqt[:, :], th[:, :], ACT.Sqrt).then_inc(act_ready, 1)
                w.act += 2
                w.vec += 1
            act.wait_ge(vec_ready, w.vec)
            act.wait_ge(small_in, 16 * w.loads)
            small_load(w_xo[:, :, :], d["w_xo"])
            for k in range(2):
                n, m = w.gemm()
                done(n)
                take(qx[:, k, :], ring[m % 4][:, :], m)
            norm([mem_t[:, c, :] for c in range(KC)], D, lambda c: None, [mem_hi[:, c, :] for c in range(KC)],
                 size=MEM)
            for k in range(2):
                n, m = w.gemm()
                done(n)
                take(kx[:, k, :], ring[m % 4][:, 0:MEM], m)
            for k in range(2):
                n, m = w.gemm()
                done(n)
                take(vx[:, :, P * k:P * k + P], ring[m % 4][:, 0:MEM].rearrange("p (t c) -> p t c", c=P), m)
            attention(cross_units())
            for t in range(KC):
                n, m = w.gemm()
                done(n)
                if t >= 2:
                    act.wait_ge(vec_ready, w.vec + t - 1)
                take(gm2[t % 2][:, :], ring[m % 4][:, :], m, ACT.Sigmoid)
                w.small()
            w.vec += KC
            small_load(rot[:, :], d["rot2"])
            small_load(cosq[:, :], d["cos2"])
            small_load(sinq[:, :], d["sin2"])
            act.wait_ge(vec_ready, w.vec)
            act.wait_ge(small_in, 16 * w.loads)
            for k in range(13):
                if k < 12:
                    n, m = w.gemm()
                    done(n)
                    if k >= 2:
                        act.wait_ge(rope_done, w.rope)
                    take(htmp[k % 2][:, :], ring[m % 4][:, :], m)
                if k >= 1:
                    w.small()
                    w.rope += 1
            for k in range(4):
                n, m = w.gemm()
                done(n)
                take(sg[k % 2][:, :], ring[m % 4][:, :], m)
                a, m = w.small()
                small_done(a)
                take(v2[:, k // 2, :, k % 2, :], ring[m % 4][:, :].rearrange("p (t c) -> p t c", c=P), m)
            n, m = w.gemm()
            done(n)
            take(sg[0][0:48, :], ring[m % 4][0:48, :], m, ACT.Sigmoid)
            a, m = w.small()
            small_done(a)
            take(gates[:, :, :], ring[m % 4][:, 0:48 * TB].rearrange("p (t c) -> p t c", c=48), m)
            for k in range(4):
                n, m = w.gemm()
                done(n)
                take(c_raw[:, k, :], ring[m % 4][:, :], m)
            for k in range(KC):
                n, m = w.gemm()
                done(n)
                take(gm0[:, k, :], ring[m % 4][:, :], m, ACT.Sigmoid)
            for side in range(2):
                if side == 1:
                    act.wait_ge(rope_done, w.rope)
                small_load(w_c1[:, :, :], d["w_c1"][side])
                small_load(w_c2[:, :, :], d["w_c2"][side])
                if side == 0:
                    act.dma_start(cos_c[:, :, :], d["cos_c"]).then_inc(small_in, 16)
                    act.dma_start(cmask[:, :, :], d["cmask"]).then_inc(small_in, 16)
                    act.dma_start(causal[:, :], d["causal"]).then_inc(small_in, 16)
                    w.loads += 3
                w.vec += 1
                for mh in range(2):
                    a, m = w.small()
                    small_done(a)
                    take(c_hid[:, mh, :], ring[m % 4][:, 0:GROUPS * NCMP], m, ACT.Gelu_apprx_tanh)
                a, m = w.small()
                small_done(a)
                if side == 0:
                    take(htmp[0][0:HD, 0:GROUPS * NCMP], ring[m % 4][0:HD, 0:GROUPS * NCMP], m)
                    w.small()
                    w.rope += 1
                else:
                    for e in range(2):
                        dst = v_cmp[CPAD * e:CPAD * e + NCMP, :, e, :]
                        src = ring[m % 4][CPAD * e:CPAD * e + NCMP, 0:GROUPS * HD]\
                            .rearrange("p (g c) -> p g c", c=HD)
                        if e == 0:
                            act.activation(dst, src, ACT.Copy)
                        else:
                            take(dst, src, m)
            attention(nsa_units(True))
            attention(nsa_units(False))
            act.wait_ge(o_taken, w.item)
            for c in range(KC):
                act.activation(u_hi[:, c, :], y2[:, c, :], ACT.Copy).then_inc(u_hi_ready, 1)
            w.split += KC
            w.n += 8
            w.m += 8
            norm_x(x_updated, scaled_later=True, over_operands=True)
            ffn(PARTS2, 1)
            norm_x(x_updated, split=False)

        @block.vector
        def _(dve):
            w = Walk()
            links = [0]

            def step(ins):
                links[0] += 1
                ins.then_inc(dve_link, 1)
                return links[0]

            def link(ins):
                dve.wait_ge(dve_link, step(ins))

            def done(n, i=None):
                dve.wait_ge(gemm_done, at_turn(n + 1, 4, i))

            def small_done(a):
                dve.wait_ge(aux_done, a + 1)

            def arrived(ins):
                w.vec += 1
                return ins.then_inc(vec_ready, 1)

            def norm(srcs, gains, outs=None, lows=None, highs=None, size=T, signal=None, gathered=False):
                m = w.bank()
                if not gathered:
                    w.sq += len(srcs)
                wait_taken(dve, m)
                if w.full:
                    dve.wait_ge(u_full, w.full)
                if w.hid:
                    dve.wait_ge(hid_full, w.hid)
                dve.reciprocal(rinv[:, 0:size], std[:, 0:size]).then_inc(rinv_ready, 1)
                w.norm += 1
                dve.wait_ge(rinv_ready, w.norm)
                count = len(srcs)
                for c in range(count + 1):
                    if c < count:
                        if outs is not None:
                            out = outs[c]
                        else:
                            out = full[(w.split + c) % 3][:, 0:size]
                            if w.split + c >= 3:
                                dve.wait_ge(u_ready, w.split + c - 2)
                        dve.scalar_tensor_tensor(out, srcs[c], gains(c), rinv[:, 0:size], ALU.mult,
                                                 ALU.mult).then_inc(signal or u_full, 1)
                    if c >= 1 and outs is None:
                        dve.wait_ge(u_hi_ready, w.split + c)
                        dve.tensor_tensor(lows[c - 1], full[(w.split + c - 1) % 3][:, 0:size],
                                          highs[c - 1].bitcast(F32), ALU.subtract).then_inc(u_ready, 1)
                w.full += count
                if outs is None:
                    w.split += count

            def x_tiles():
                return [x[:, c, :] for c in range(KC)]

            def norm_x(name, layer, gathered=True):
                norm(x_tiles(), lambda c: col(name, layer, c), lows=[u_lo[:, c, :] for c in range(KC)],
                     highs=[u_hi[:, c, :] for c in range(KC)], gathered=gathered)

            def pass_over_x(scale, gains=None, over_operands=False):
                def scaled(c):
                    if w.split + c >= 3:
                        dve.wait_ge(u_ready, w.split + c - 2)
                    if w.hid:
                        dve.wait_ge(hid_full, w.hid)
                    dve.tensor_scalar(full[(w.split + c) % 3][:, :], x[:, c, :], gains(c), None,
                                      ALU.mult).then_inc(u_full, 1)

                def low(c):
                    dve.wait_ge(u_hi_ready, w.split + c + 1)
                    dve.tensor_tensor(u_lo[:, c, :], full[(w.split + c) % 3][:, :],
                                      u_hi[:, c, :].bitcast(F32), ALU.subtract).then_inc(u_ready, 1)

                at_once = gains is not None and not over_operands
                for c in range(KC + 1):
                    if c < KC:
                        tile = x[:, c, :]
                        if scale is not None:
                            n, m = w.gemm()
                            done(n)
                            dve.scalar_tensor_tensor(tile, ring[m % 4][:, :], scale, tile, ALU.mult,
                                                     ALU.add).then_inc(taken[m % 4], 1)
                            wait_taken(dve, m)
                        if at_once:
                            scaled(c)
                    if c:
                        dve.wait_ge(sq_ready, w.sq + 1)
                        square = sq[w.sq % 2][:, :]
                        if c == 1:
                            dve.tensor_copy(std[:, :], square).then_inc(sq_used, 1)
                        else:
                            dve.wait_ge(sq_used, w.sq)
                            dve.tensor_tensor(std[:, :], std[:, :], square, ALU.add).then_inc(sq_used, 1)
                        w.sq += 1
                        if at_once:
                            low(c - 1)
                if over_operands:
                    for c in range(KC + 1):
                        if c < KC:
                            scaled(c)
                        if c:
                            low(c - 1)
                if gains is not None:
                    w.full += KC
                    w.split += KC
                    m = w.bank()
                    wait_taken(dve, m)
                    dve.wait_ge(u_full, w.full)
                    if w.hid:
                        dve.wait_ge(hid_full, w.hid)
                    dve.reciprocal(rinv[:, :], std[:, :]).then_inc(rinv_ready, 1)
                    w.norm += 1
                    dve.wait_ge(rinv_ready, w.norm)

            def looped(turns, body):
                body(None)
                with dve.Fori(1, turns) as i:
                    body(i)

            def add_to_x(scale):
                def turn(i):
                    for j in range(4):
                        m = w.m + j
                        tile = x[:, j, :] if i is None else \
                            x[:, bass.ds(i * 4 + j, 1), :].rearrange("p o t -> p (o t)")
                        done(w.n + j, i)
                        dve.scalar_tensor_tensor(tile, ring[m % 4][:, :], scale, tile, ALU.mult,
                                                 ALU.add).then_inc(taken[m % 4], 1)
                looped(2, turn)
                w.n += 8
                w.m += 8

            def ffn(parts, per, gains=None):
                for p, part in enumerate(parts):
                    def chunk(i, c):
                        turn_size = 4 // per
                        hid = htmp[c % 2][:, :]
                        if per == 2:
                            gate, up = w.m + 2 * c, w.m + 2 * c + 1
                            done(w.n + 2 * c, i)
                            dve.tensor_tensor(full[c % 2][:, :], ring[gate % 4][:, :], rinv[:, :],
                                              ALU.mult).then_inc(taken[gate % 4], 1)
                            done(w.n + 2 * c + 1, i)
                            dve.tensor_tensor(hid, ring[up % 4][:, :], rinv[:, :],
                                              ALU.mult).then_inc(taken[up % 4], 1)
                            dve.wait_ge(gate_ready, at_turn(w.gate + c + 1, turn_size, i))
                            wait_taken(dve, up, i)
                            dve.tensor_tensor(hid, hid, sg[c % 2][:, :], ALU.mult).then_inc(hid_full, 1)
                        else:
                            m = w.m + c
                            dve.wait_ge(act_ready, at_turn(w.act + c + 1, 4, i))
                            dve.tensor_tensor(full[c % 2][:, :], sg[c % 2][:, :], rinv[:, :],
                                              ALU.mult).then_inc(taken[m % 4], 1)
                            wait_taken(dve, m, i)
                            dve.tensor_tensor(hid, full[c % 2][:, :], full[c % 2][:, :],
                                              ALU.mult).then_inc(hid_full, 1)
                        dst = h_lo[:, c, :] if i is None else \
                            h_lo[:, bass.ds(i * turn_size + c, 1), :].rearrange("p o t -> p (o t)")
                        high = h_hi[:, c, :] if i is None else \
                            h_hi[:, bass.ds(i * turn_size + c, 1), :].rearrange("p o t -> p (o t)")
                        dve.wait_ge(h_hi_ready, at_turn(w.hid + c + 1, turn_size, i))
                        dve.tensor_tensor(dst, htmp[c % 2][:, :], high.bitcast(F32),
                                          ALU.subtract).then_inc(h_ready, 1)

                    def turn(i):
                        for c in range(4 // per):
                            chunk(i, c)

                    looped(per * part // 4, turn)
                    w.n += per * part
                    w.m += per * part
                    w.hid += part
                    if per == 1:
                        w.act += part
                    else:
                        w.gate += part
                    scale = 0.5 if per == 2 else 1.0
                    if p < len(parts) - 1:
                        add_to_x(scale)
                    else:
                        pass_over_x(scale, gains)

            def reduce_angle(a, n):
                link(dve.tensor_scalar(n, a, 1.0 / (2.0 * math.pi), MAGIC, ALU.mult, ALU.add))
                link(dve.tensor_scalar(n, n, MAGIC, None, ALU.subtract))
                for part in TWO_PI:
                    link(dve.scalar_tensor_tensor(a, n, -part, a, ALU.mult, ALU.add))

            def clamp_angle(a):
                return dve.tensor_scalar(a, a, 3.1415925, -3.1415925, ALU.min, ALU.max)

            def rotate(raw, outs, cos, sin, rows, cols_, m_raw):
                a, m = w.small()
                if m_raw is not None:
                    wait_taken(dve, m_raw)
                if w.rope:
                    dve.wait_ge(rope_done, w.rope)
                t1, t2 = sq[0][0:rows, 0:cols_], sq[1][0:rows, 0:cols_]
                step(dve.tensor_tensor(t1, raw, cos, ALU.mult))
                small_done(a)
                dve.tensor_tensor(t2, ring[m % 4][0:rows, 0:cols_], sin, ALU.mult)\
                   .then_inc(taken[m % 4], 1)
                dve.wait_ge(dve_link, links[0])
                wait_taken(dve, m)
                for k, (out, r0) in enumerate(outs):
                    r1 = r0 + out.shape[0]
                    a_, b_ = (s_[r0:r1, 0:cols_] for s_ in sq)
                    if len(out.shape) == 3:
                        a_, b_ = (s_.rearrange("p (g n) -> p g n", n=NCMP) for s_ in (a_, b_))
                    ins = dve.tensor_tensor(out, a_, b_, ALU.add)
                    if k == len(outs) - 1:
                        ins.then_inc(rope_done, 1)
                w.rope += 1

            def attention(units, take_tile):
                u0, p0, i0 = w.unit, w.part, w.item
                for s in range(len(units) + VALUES + 1):
                    if s < len(units):
                        u, k = units[s], u0 + s
                        j, n = k % 8, u["n"]
                        sc = score[s % 2]
                        dve.wait_ge(s_full, k + 1)
                        if u["kind"] == "plain":
                            link(dve.tensor_reduce(mx[:, j, 0:1], sc[:, 0, 0:n], AX.X, ALU.max))
                            dve.tensor_scalar(nb[:, j, 0:1], mx[:, j, 0:1], -u["scale"], None, ALU.mult)\
                               .then_inc(s_max, 1)
                        elif u["kind"] == "pair":
                            edge = sc[:, :, n - P:n]
                            link(dve.tensor_tensor(edge, edge, causal[:, :].unsqueeze(1).broadcast_to([P, 2, P]),
                                                   ALU.add))
                            link(dve.tensor_reduce(mx[:, j, 0:2], sc[:, :, 0:n], AX.X, ALU.max))
                            step(dve.tensor_scalar(nb[:, j, 0:1], mx[:, j, 0:1], -u["scale"], None, ALU.mult))
                            dve.tensor_scalar(nb[:, j, 1:2], mx[:, j, 1:2], col("padfloor", None, u["i"]),
                                              -u["scale"], ALU.max, ALU.mult).then_inc(s_max, 1)
                        else:
                            rows_ = sc[:, 0, 0:2 * TB * CPAD].rearrange("p (t n) -> p t n", n=CPAD)
                            each = sc[:, 0, 0:2 * TB * CPAD].rearrange("p (t e n) -> p t e n", e=2, n=CPAD)
                            mask = cmask[:, :, :].unsqueeze(2).broadcast_to([P, TB, 2, CPAD])
                            link(dve.tensor_tensor(each, each, mask, ALU.add))
                            link(dve.tensor_reduce(mx[:, j, :], rows_, AX.X, ALU.max))
                            link(dve.tensor_scalar(mx[:, j, :], mx[:, j, :], FLOOR, None, ALU.max))
                            if s >= 4:
                                dve.wait_ge(t_full, p0 + parts_of(units, s - 3))
                            dve.tensor_tensor(u["keep"][k % 4][:, 0, 0:2 * TB * CPAD]
                                              .rearrange("p (t n) -> p t n", n=CPAD), rows_,
                                              mx[:, j, :].unsqueeze(2).broadcast_to([P, 2 * TB, CPAD]),
                                              ALU.subtract).then_inc(s_max, 1)
                    if 0 <= s - 1 < len(units):
                        u, k = units[s - 1], u0 + s - 1
                        j, n = k % 8, u["n"]
                        keep = u["keep"][k % 4]
                        dve.wait_ge(exp_done, p0 + parts_of(units, s))
                        if u["kind"] == "plain":
                            link(dve.reciprocal(ri[:, j, 0:1], sums[:, j, 0:1]))
                            dve.tensor_scalar(keep[:, 0:n], keep[:, 0:n], ri[:, j, 0:1], None, ALU.mult)\
                               .then_inc(p_norm, 1)
                        elif u["kind"] == "pair":
                            link(dve.scalar_tensor_tensor(sums[:, j, 1:2], e0[:, j, 0:1],
                                                          col("npad", None, u["i"]), sums[:, j, 1:2],
                                                          ALU.mult, ALU.add))
                            link(dve.reciprocal(ri[:, j, 0:2], sums[:, j, 0:2]))
                            for b in range(2):
                                dve.tensor_scalar(keep[:, b, 0:n], keep[:, b, 0:n], ri[:, j, b:b + 1],
                                                  u["gate"][:, b:b + 1], ALU.mult, ALU.mult).then_inc(p_norm, 1)
                        else:
                            rows_ = keep[:, 0, 0:2 * TB * CPAD].rearrange("p (t n) -> p t n", n=CPAD)
                            link(dve.tensor_reduce(sums[:, j, :], rows_, AX.X, ALU.add))
                            link(dve.tensor_scalar(sums[:, j, :], sums[:, j, :], 1e-30, None, ALU.max))
                            link(dve.reciprocal(ri[:, j, :], sums[:, j, :]))
                            inv = ri[:, j, :].rearrange("p (t e) -> p t e", e=2)
                            link(dve.tensor_tensor(inv, inv, u["gate"], ALU.mult))
                            dve.tensor_tensor(rows_, rows_,
                                              ri[:, j, :].unsqueeze(2).broadcast_to([P, 2 * TB, CPAD]),
                                              ALU.mult).then_inc(p_norm, 1)
                    if s > VALUES and units[s - VALUES - 1]["closes"]:
                        dve.wait_ge(pv_done, u0 + s - VALUES)
                        if w.item:
                            dve.wait_ge(o_taken, w.item)
                        take_tile(w.item - i0, product[w.item % 2][:, :]).then_inc(o_taken, 1)
                        w.item += 1
                w.unit += len(units)
                w.part += parts_of(units, len(units))

            def mixer(layer):
                def c(name, k, rows=P):
                    return col(name, layer, k, rows)

                norm_x("g_mix", layer)
                if layer == 0:
                    dve.wait_ge(small_in, 16 * w.loads)
                    ang, n_ = f_a[0:QK, :], f_n[0:QK, :]
                    link(dve.tensor_copy(ang, cosq[0:QK, :].bitcast(I32)))
                    link(dve.tensor_scalar(ang, ang, col("invf", None, 0, QK), None, ALU.mult))
                    reduce_angle(ang, n_)
                    arrived(clamp_angle(ang))
                    dve.wait_ge(vec_ready, w.vec)
                    link(dve.scalar_tensor_tensor(n_, ang, -1.0, ang, ALU.mult, ALU.max))
                    arrived(dve.tensor_scalar(n_, n_, -1.0, math.pi / 2, ALU.mult, ALU.add))
                    w.act += 2
                taps = [0]

                def convolve(count):
                    for tap in range(taps[0], taps[0] + count):
                        for t in range(2):
                            src = conv_pad[:, t, tap:tap + T]
                            acc = y_conv[:, t, :]
                            dve.wait_ge(dve_link, links[0] - (1 if taps[0] < tap < TAPS - 1 else 0))
                            if tap == 0:
                                ins = dve.tensor_scalar(acc, src, c("conv_w", TAPS * t), c("conv_b", t),
                                                        ALU.mult, ALU.add)
                            else:
                                ins = dve.scalar_tensor_tensor(acc, src, c("conv_w", TAPS * t + tap), acc,
                                                               ALU.mult, ALU.add)
                            if tap < TAPS - 1:
                                step(ins)
                            else:
                                arrived(ins)
                    taps[0] += count

                for k in range(14):
                    n, m = w.gemm()
                    if k < 2:
                        done(n)
                        dve.tensor_copy(a_in[:, k, :], ring[m % 4][:, :]).then_inc(taken[m % 4], 1)
                        m_a = m
                        if k == 1:
                            step(dve.memset(conv_pad[:, :, 0:TAPS // 2], 0.0))
                            step(dve.memset(conv_pad[:, :, PADW - TAPS // 2:PADW], 0.0))
                            wait_taken(dve, m_a)
                    elif k < 4:
                        wait_taken(dve, m)
                        step(dve.tensor_tensor(conv_pad[:, k - 2, TAPS // 2:TAPS // 2 + T], a_in[:, k - 2, :],
                                               g_sig[:, k - 2, :], ALU.mult))
                    elif k < 8:
                        convolve(3)
                    else:
                        done(n)
                        src, h = ring[m % 4], k - 8
                        link(dve.tensor_scalar(hy[:, h, :], src[:, :], c("short_w", 3 * h + 1), c("short_b", h),
                                               ALU.mult, ALU.add))
                        link(dve.scalar_tensor_tensor(hy[:, h, 1:T], src[:, 0:T - 1], c("short_w", 3 * h),
                                                      hy[:, h, 1:T], ALU.mult, ALU.add))
                        dve.scalar_tensor_tensor(hy[:, h, 0:T - 1], src[:, 1:T], c("short_w", 3 * h + 2),
                                                 hy[:, h, 0:T - 1], ALU.mult, ALU.add).then_inc(taken[m % 4], 1)
                        convolve(2)
                    if k in SINES:
                        l = SINES.index(k)
                        a, m = w.small()
                        small_done(a)
                        arg, n_ = f_a[0:HYF, :], f_n[0:HYF, :]
                        if l:
                            dve.wait_ge(act_ready, w.act + l)
                        dve.tensor_scalar(arg, ring[m % 4][0:HYF, :], c("fb", l, HYF), c("freq", 0, HYF),
                                          ALU.add, ALU.mult).then_inc(taken[m % 4], 1)
                        wait_taken(dve, m)
                        reduce_angle(arg, n_)
                        arrived(clamp_angle(arg))
                w.act += 3
                dve.wait_ge(tables_in, 16 * (w.tables + 2))
                w.tables += 3
                for t in range(TB):
                    for o in range(2):
                        a, m = w.small()
                        small_done(a)
                        dve.tensor_tensor(filt[:, o, t, :, :].rearrange("p b c -> p (b c)"), ring[m % 4][:, :],
                                          decay[:, t, :], ALU.mult).then_inc(taken[m % 4], 1)
                    for m_ in (m - 1, m):
                        wait_taken(dve, m_)
                    step(dve.tensor_tensor(fsum[:, t, :, :], filt[:, :, t, 0, :], filt[:, :, t, 1, :], ALU.add))
                    dve.tensor_tensor(fdif[:, t, :, :], filt[:, :, t, 0, :], filt[:, :, t, 1, :], ALU.subtract)\
                       .then_inc(vec_ready, 2 if t < TB - 1 else 3)
                    convolve(1)
                w.vec += 9
                convolve(TAPS - taps[0])
                sums_at = [w.bank() for _ in range(2)]
                w.sq += 2 * TB
                rk = sg[0][:, :].rearrange("p (o c) -> p o c", o=2)
                dve.wait_ge(sq_used, w.sq)
                for o, m in enumerate(sums_at):
                    dve.reciprocal(rk[:, o, :], ring[m % 4][:, 0:HYC]).then_inc(taken[m % 4], 1)
                for m in sums_at:
                    wait_taken(dve, m)
                for j in range(TB):
                    for part in range(2):
                        a, m = w.small()
                        small_done(a)
                        src = ring[m % 4][:, :].rearrange("p (o c) -> p o c", o=2)
                        if part == 0:
                            step(dve.tensor_tensor(spec[:, :, j, 2, :], src, rk, ALU.mult))
                        dve.tensor_tensor(spec[:, :, j, part, :], src, rk, ALU.mult).then_inc(taken[m % 4], 1)
                    m_spec = m
                    if j == 0:
                        a, m = w.small()
                        small_done(a)
                        for t in range(2):
                            arrived(dve.scalar_tensor_tensor(y_conv[:, t, :], ring[m % 4][:, :], -1.0 / CONVC,
                                                             y_conv[:, t, :], ALU.mult, ALU.add))
                        dve.wait_ge(vec_ready, w.vec)
                        dve.sem_inc(taken[m % 4], 1)
                    elif j == 1:
                        m = w.bank()
                        w.sq += 2
                        wait_taken(dve, m)
                        dve.wait_ge(u_full, w.full)
                        dve.reciprocal(rinv[:, :], std[:, :]).then_inc(rinv_ready, 1)
                        w.norm += 1
                        dve.wait_ge(rinv_ready, w.norm)
                        for t in range(2):
                            arrived(dve.scalar_tensor_tensor(y_conv[:, t, :], y_conv[:, t, :], c("ln_g", t),
                                                             rinv[:, :], ALU.mult, ALU.mult))
                        w.act += 2
                    elif j == 2:
                        dve.wait_ge(vec_ready, w.vec)
                        norm([hm_q[:, k, :] for k in range(2)], lambda k: c("g_q", k),
                             outs=[qn[:, k, :] for k in range(2)])
                    else:
                        norm([hm_q[:, 2, :]], lambda k: c("g_kv", 0), outs=[kvn[:, 0, :]])
                wait_taken(dve, m_spec)
                dve.wait_ge(dve_link, links[0])
                w.vec += 1
                dve.sem_inc(vec_ready, 1)
                for o in range(2):
                    w.aux += TB
                    w.m += TB
                    for j in range(TB):
                        a, m = w.small()
                        small_done(a)
                        src = ring[m % 4][:, :].rearrange("p (h c) -> p h c", h=2)
                        if j:
                            dve.wait_ge(vec_ready, w.vec)
                        step(dve.tensor_tensor(prod[0][:, :, :], src, spec[:, o, j, 0:2, :], ALU.mult))
                        dve.tensor_tensor(prod[1][:, :, :], src, spec[:, o, j, 1:3, :], ALU.mult)\
                           .then_inc(taken[m % 4], 1)
                        dve.wait_ge(dve_link, links[0])
                        step(dve.tensor_tensor(y_spec[:, j, 0, :], prod[0][:, 0, :], prod[0][:, 1, :],
                                               ALU.subtract))
                        wait_taken(dve, m)
                        arrived(dve.tensor_tensor(y_spec[:, j, 1, :], prod[1][:, 0, :], prod[1][:, 1, :],
                                                  ALU.add))
                    if o == 0:
                        norm([y_conv[:, k, :] for k in range(2)], lambda k: c("g_out", 4 + k),
                             outs=[y_conv[:, k, :] for k in range(2)])
                    dve.wait_ge(vec_ready, w.vec)
                    dve.wait_ge(dve_link, links[0])
                    for ch in range(2):
                        a, m = w.small()
                        small_done(a)
                        tmp = prod[ch][:, :, :].rearrange("p h c -> p (h c)")
                        dve.scalar_tensor_tensor(tmp, hy[:, 2 * o + ch, :], c("hy_d", 2 * o + ch),
                                                 ring[m % 4][:, :], ALU.mult, ALU.add).then_inc(taken[m % 4], 1)
                        wait_taken(dve, m)
                        arrived(dve.tensor_tensor(hy[:, 2 * o + 2 + ch, :], tmp, hy[:, 2 * o + 2 + ch, :],
                                                  ALU.mult))
                w.loads += 2
                w.aux += TB
                w.m += TB
                norm([hy[:, 4 + k, :] for k in range(2)], lambda k: c("g_out", 6 + k),
                     outs=[hy[:, 4 + k, :] for k in range(2)])
                w.aux += HEADS // 2
                w.m += HEADS // 2
                cos, sin = cosq[0:QK, :], sinq[0:QK, :]
                rotate(hm_q[0:QK, 3, :], [(kpe_r[0:QK, :], 0)], cos, sin, QK, T, None)
                prev = None
                for h in range(HEADS + 1):
                    this = None
                    if h < HEADS:
                        this = w.small()[1]
                    if prev is not None:
                        rotate(htmp[(h - 1) % 2][0:QK, :], [(q_all[0:QK, h - 1, :], 0)], cos, sin, QK, T, prev)
                        if h == 1:
                            dve.wait_ge(rope_done, w.rope - 1)
                        ins = dve.tensor_copy(k_all[NOPE:QK, h - 1, :], kpe_r[NOPE:QK, :])
                    prev = this
                arrived(ins)

                attention(mla_units(), lambda tile, src: dve.tensor_copy(y_mla[:, tile, :], src))
                for k in range(4):
                    src = y_conv[:, k, :] if k < 2 else hy[:, 2 + k, :]
                    dve.wait_ge(u_hi_ready, w.split + 1)
                    dve.tensor_tensor(u_lo[:, 4 + k, :], src, u_hi[:, 4 + k, :].bitcast(F32),
                                      ALU.subtract).then_inc(u_ready, 1)
                    w.split += 1
                norm([y_mla[:, k, :] for k in range(4)], lambda k: c("g_out", k),
                     lows=[u_lo[:, k, :] for k in range(4)], highs=[u_hi[:, k, :] for k in range(4)])
                pass_over_x(1.0, lambda k: col("g_ffn2", layer, k), over_operands=True)

            arrived(dve.memset(ones[:, :], 1.0))
            dve.wait_ge(consts_in, 16 * 3)
            w.loads += 2
            pass_over_x(None, lambda k: col("g_ffn1", 0, k))
            for layer in range(DEPTH):
                ffn(PARTS, 2)
                mixer(layer)
                ffn(PARTS, 2, (lambda k: col("g_ffn1", layer + 1, k)) if layer < DEPTH - 1 else None)
            norm(x_tiles(), lambda c: col("g_final1", None, c), outs=x_tiles(), gathered=True)

            norm_x("g_mix2", None, gathered=False)
            w.loads += 2
            w.act += 2
            dve.wait_ge(act_ready, w.act)
            lam = cols[:, places["lam"]:places["lam"] + KC]
            e, s, t_, z, p = (lamt[:, k, :] for k in (1, 2, 3, 4, 5))
            link(dve.tensor_scalar(t_, e, 2.0, None, ALU.add))
            link(dve.reciprocal(t_, t_))
            link(dve.tensor_tensor(s, e, t_, ALU.mult))
            link(dve.tensor_tensor(z, s, s, ALU.mult))
            link(dve.tensor_scalar(p, z, 1.0 / 17, 1.0 / 15, ALU.mult, ALU.add))
            for k in (13, 11, 9, 7, 5, 3, 1):
                link(dve.tensor_tensor(p, p, z, ALU.mult))
                link(dve.tensor_scalar(p, p, 1.0 / k, None, ALU.add))
            link(dve.tensor_tensor(p, p, s, ALU.mult))
            link(dve.tensor_scalar(t_, lam, -1.0, 0.0, ALU.mult, ALU.max))
            link(dve.scalar_tensor_tensor(t_, p, 2.0, t_, ALU.mult, ALU.add))
            link(dve.tensor_scalar(lamt[:, 7, :], t_, 4.0, None, ALU.mult))
            for k in range(2):
                link(dve.memset(xpad[k][:, 0:3], 0.0))
            w.vec += 1
            dve.sem_inc(vec_ready, 1)
            for t in range(KC):
                n, m = w.gemm()
                wait_taken(dve, m)
                src, acc = xpad[t % 2], xc[t % 2]
                link(dve.tensor_scalar(acc[:, :], src[:, 0:T], col("conv_w2", None, 4 * t),
                                       col("conv_b2", None, t), ALU.mult, ALU.add))
                for k in range(1, 4):
                    ins = dve.scalar_tensor_tensor(acc[:, :], src[:, k:k + T], col("conv_w2", None, 4 * t + k),
                                                   acc[:, :], ALU.mult, ALU.add)
                    if k < 3:
                        link(ins)
                    else:
                        arrived(ins)
                w.gemm()
                _, m_g = w.gemm()
                w.small()
                a, m_i = w.small()
                dve.wait_ge(act_ready, w.act + 1)
                link(dve.tensor_scalar(rw[:, :], th[:, :], 1.0, None, ALU.add))
                link(dve.reciprocal(rw[:, :], rw[:, :]))
                link(dve.tensor_scalar(ra[:, :], th[:, :], -1.0, 1.0, ALU.mult, ALU.add))
                link(dve.tensor_tensor(ra[:, :], ra[:, :], rw[:, :], ALU.mult))
                dve.wait_ge(act_ready, w.act + 2)
                link(dve.scalar_tensor_tensor(ru[:, :], sqt[:, :], 2.0, rw[:, :], ALU.mult, ALU.mult))
                wait_taken(dve, m_i)
                link(dve.tensor_tensor(ru[:, :], ru[:, :], isg[:, :], ALU.mult))
                link(dve.tensor_tensor(ru[:, :], ru[:, :], acc[:, :], ALU.mult))
                link(dve.tensor_tensor_scan(rh[:, :], ra[:, :], ru[:, :], 0.0, ALU.mult, ALU.add))
                link(dve.tensor_tensor(rh[:, :], rh[:, :], gel[:, :], ALU.mult))
                wait_taken(dve, m_g)
                arrived(dve.tensor_tensor(y2[:, t, :], rh[:, :], gm1[:, :], ALU.mult))
                w.act += 2
            dve.wait_ge(small_in, 16 * w.loads)
            w.loads += 1
            w.n += 2
            w.m += 2
            norm([mem_t[:, k, :] for k in range(KC)], lambda k: col("g_mem", None, k),
                 lows=[mem_lo[:, k, :] for k in range(KC)], highs=[mem_hi[:, k, :] for k in range(KC)], size=MEM)
            w.n += 4
            w.m += 4

            attention(cross_units(), lambda tile, src: dve.tensor_copy(ox[:, tile, :], src))
            for t in range(KC):
                _, m_g = w.gemm()
                a, m = w.small()
                wait_taken(dve, m_g)
                small_done(a)
                dve.tensor_tensor(sq[t % 2][:, :], ring[m % 4][:, :], gm2[t % 2][:, :], ALU.mult)\
                   .then_inc(taken[m % 4], 1)
                wait_taken(dve, m)
                arrived(dve.tensor_tensor(y2[:, t, :], y2[:, t, :], sq[t % 2][:, :], ALU.add))
            w.loads += 3
            dve.wait_ge(small_in, 16 * w.loads)
            prev = None
            for k in range(13):
                this = None
                if k < 12:
                    this = w.gemm()[1]
                if prev is not None:
                    item = k - 1
                    if item < 4:
                        outs = [(k2[HD * half:HD * half + HD, item // 2, 2 * (item % 2) + par, :], HD * par)
                                for par in range(2) for half in range(2)]
                    else:
                        outs = [(q2[:, item - 4, :], 0)]
                    rotate(htmp[item % 2][:, :], outs, cosq[:, :], sinq[:, :], P, T, prev)
                prev = this
            for k in range(5):
                w.gemm()
                w.small()
            w.n += 4 + KC
            w.m += 4 + KC
            gathered = w.m - KC - 1
            wait_taken(dve, w.m - 1)
            dve.wait_ge(rope_done, w.rope)
            step(dve.memset(k_cmp[:, :, :, :], 0.0))
            step(dve.memset(v_cmp[:, :, :, :], 0.0))
            for side in range(2):
                w.loads += 5 if side == 0 else 2
                for g in range(GROUPS):
                    src = c_raw[HD * (g % 2):HD * (g % 2) + HD, 2 * side + g // 2, :]
                    step(dve.tensor_copy(c_dup[0:HD, g, :], src))
                    step(dve.tensor_copy(c_dup[HD:P, g, 0:T - 1], src[:, 1:T]))
                dve.wait_ge(dve_link, links[0])
                for i in range(16):
                    ins = dve.tensor_scalar(c_blk[:, i, :, :], c_dup[:, :, 2 * i:2 * i + 16 * (NCMP - 1) + 1:16],
                                            col(("pos_k", "pos_v")[side], None, i), None, ALU.add)
                arrived(ins)
                w.aux += 3
                w.m += 3
                m_raw = w.m - 1
                if side == 0:
                    dve.wait_ge(small_in, 16 * w.loads)
                    flat = GROUPS * NCMP
                    rotate(htmp[0][0:HD, 0:flat],
                           [(k_cmp[HD * half:HD * half + HD, :, half, 0:NCMP], 0)
                            for half in range(2)], cos_c[:, 0, :], cos_c[:, 1, :], HD, flat, m_raw)
            wait_taken(dve, m_raw)

            def merge(tile, src):
                link(dve.tensor_tensor(sq[0][:, :], src, gm0[:, tile, :], ALU.mult))
                return dve.tensor_tensor(y2[:, tile, :], y2[:, tile, :], sq[0][:, :], ALU.add)

            attention(nsa_units(True), merge)
            attention(nsa_units(False), merge)
            dve.wait_ge(o_taken, w.item)
            for c in range(KC):
                dve.wait_ge(u_hi_ready, w.split + 1)
                dve.tensor_tensor(u_lo[:, c, :], y2[:, c, :], u_hi[:, c, :].bitcast(F32),
                                  ALU.subtract).then_inc(u_ready, 1)
                w.split += 1
            pass_over_x(1.0, lambda k: col("g_mlp", None, k), over_operands=True)
            ffn(PARTS2, 1)
            norm(x_tiles(), lambda c: col("g_final2", None, c), outs=[out_t[:, c, :] for c in range(KC)],
                 signal=out_ready, gathered=True)
    return nc


def _blocks(w, k):
    n = w.shape[1] // P
    return w.reshape(k, P, n, P).transpose(2, 1, 0, 3).reshape(n, P, k * P)


def _rows(v):
    return np.ascontiguousarray(v).reshape(-1, P).T


def _pad_rows(v):
    out = np.zeros((P, v.shape[1]), np.float32)
    out[:v.shape[0]] = v
    return out


def shape_constants():
    f = np.float32
    k = {"ident": np.eye(P, dtype=f)}
    rot1 = np.zeros((P, P), f)
    half = ROPE // 2
    for j in range(half):
        rot1[NOPE + half + j, NOPE + j] = -1
        rot1[NOPE + j, NOPE + half + j] = 1
    k["rot1"] = rot1
    rot2 = np.zeros((P, P), f)
    for h in range(2):
        for j in range(8):
            rot2[HD * h + 8 + j, HD * h + j] = -1
            rot2[HD * h + j, HD * h + 8 + j] = 1
    k["rot2"] = rot2
    inv2 = (f(1.0) / (f(500000.0) ** (np.arange(0, 16, 2, dtype=f) / f(16)))).astype(f)

    def tables(pos, rows):
        ang = (inv2[:, None] * pos[None, :].astype(f)).astype(f).astype(np.float64)
        c = np.ones((HD, len(pos)))
        s = np.zeros((HD, len(pos)))
        c[0:16] = np.tile(np.cos(ang), (2, 1))
        s[0:16] = np.tile(np.sin(ang), (2, 1))
        return np.tile(c, (rows // HD, 1)).astype(f), np.tile(s, (rows // HD, 1)).astype(f)

    k["cos2"], k["sin2"] = tables(np.arange(T), P)
    cc, sc = tables(np.arange(NCMP) * 16 + 31, HD)
    k["cos_c"] = np.stack([np.tile(cc, (1, GROUPS)), np.tile(sc, (1, GROUPS))], 1)
    ang = 2 * np.pi * np.outer(np.arange(T), np.arange(T) + 0.5) / (2 * T)
    cs = np.stack([np.cos(ang), np.sin(ang)])
    k["dft"] = cs.reshape(2, TB, P, T).transpose(2, 0, 1, 3).astype(f)
    k["idft"] = (cs.transpose(0, 2, 1) / T).reshape(2, TB, P, T).transpose(2, 0, 1, 3).astype(f)
    t = np.linspace(0.0, 1.0, T, dtype=f)[:, None]
    bands = (EMB - 1) // 2
    ang = (f(2.0 * math.pi) * np.arange(T, dtype=f)[:, None] / f(T)).astype(f)
    fb = np.linspace(1e-4, bands - 1, bands, dtype=f)[None, :]
    a = (fb * ang).astype(f).astype(np.float64)
    k["f_z"] = np.concatenate([t, np.cos(a), -np.sin(a)], 1).T.astype(f)
    deltas = np.linspace(math.log(1e-2) / 1.5, math.log(1e-2) / 0.3, HYC, dtype=f)
    win = np.exp((-t * np.abs(deltas)).astype(np.float64))
    back = win.copy()
    back[0] = 0.0
    k["decay"] = np.concatenate([win, back], 1).reshape(TB, P, T).transpose(1, 0, 2).astype(f)
    q = np.arange(T)
    end = np.arange(NCMP) * 16 + 31
    cmask = np.full((T, CPAD), NEG)
    cmask[:, 0:NCMP] = np.where(end[None, :] <= q[:, None], 0.0, NEG)
    k["cmask"] = cmask.reshape(TB, P, CPAD).transpose(1, 0, 2).astype(f)
    k["causal"] = np.where(np.arange(P)[None, :] <= np.arange(P)[:, None], 0.0, NEG).astype(f)
    return {n: np.ascontiguousarray(v) for n, v in k.items()}


def layout(a):
    k = shape_constants()
    w = {8: [], 10: [], 12: []}

    def ffn(i, name):
        gate, up, down = (a[f"{name}_w_{x}"][i] for x in ("gate", "up", "down"))
        first = 0
        for part in PARTS:
            c = slice(P * first, P * (first + part))
            pair = np.stack([_blocks(gate[:, c], KC), _blocks(up[:, c], KC)], 1)
            w[8].append(pair.reshape(2 * part, P, D))
            w[part].append(_blocks(down[c], part))
            first += part

    for i in range(DEPTH):
        ffn(i, "ffn1")
        w_in = a["w_in"][i]
        key = np.zeros((D, P), np.float32)
        key[:, NOPE:QK] = w_in[:, QRANK + KVRANK:QRANK + KVRANK + ROPE]
        convs = w_in[:, QRANK + KVRANK + ROPE:]
        w[8].append(_blocks(np.concatenate([convs[:, 0:2 * CONVC], w_in[:, 0:QRANK + KVRANK], key,
                                            convs[:, 2 * CONVC:]], 1), KC))
        w[8].append(_blocks(a["w_out"][i], KC))
        ffn(i, "ffn2")
    z = a["w_in_2"][0]
    ends = np.cumsum([0, 1024, 256, 256, 256, 256, 256, 256, 48, 1024, 1024, 256, 3072])
    q, kc, vc, ks, vs, kw, vw, ng, xr, gr, qx, mg = (z[:, s:e] for s, e in zip(ends[:-1], ends[1:]))
    trio = np.stack([_blocks(v, KC) for v in (xr, gr, mg[:, D:2 * D])], 1)
    w[8].append(trio.reshape(3 * KC, P, D))
    w[8].append(_blocks(qx, KC))
    w[8].append(_blocks(a["w_mem_kv_2"][0], KC))
    w[8].append(_blocks(mg[:, 2 * D:], KC))
    gate_cols = np.zeros((D, P), np.float32)
    gate_cols[:, 0:48] = ng
    for v in (ks, kw, q, vs, vw, gate_cols, kc, vc, mg[:, 0:D], a["w_o_2"][0]):
        w[8].append(_blocks(v, KC))
    first = 0
    for part in PARTS2:
        c = slice(P * first, P * (first + part))
        w[8].append(_blocks(a["w_up_2"][0][:, c], KC))
        w[part].append(_blocks(a["w_down_2"][0][c], part))
        first += part
    for n, v in w.items():
        k[f"w{n}"] = np.concatenate(v, 0)

    cols = []
    for i in range(DEPTH):
        conv = a["conv_dw_w"][i].reshape(TAPS, 2, P).transpose(2, 1, 0).reshape(P, 2 * TAPS)
        short = a["hy_short_w"][i].reshape(3, 6, P).transpose(2, 1, 0).reshape(P, 18)
        biases = np.stack([a[f"hy_filt_b{j}"][i] for j in (1, 2, 3)], 1)
        cols += [_rows(a["ffn1_norm"][i]), _rows(a["mix_norm"][i]), _rows(a["mla_q_norm"][i]),
                 _rows(a["mla_kv_norm"][i]), conv, _rows(a["conv_dw_b"][i]), _rows(a["conv_ln_g"][i]),
                 _rows(a["conv_ln_b"][i]), short, _rows(a["hy_short_b"][i]), _pad_rows(biases),
                 _pad_rows(a["hy_filt_freq"][i][:, None]), _rows(a["hy_bias_d"][i]), _rows(a["out_norm"][i]),
                 _rows(a["ffn2_norm"][i])]
    conv2 = a["conv_w_2"][0].reshape(4, KC, P).transpose(2, 1, 0).reshape(P, 4 * KC)
    tok = np.arange(T)
    invf = np.zeros((P, 1), np.float32)
    f = np.float32
    inv = f(1.0) / (f(10000.0) ** (np.arange(0, ROPE, 2, dtype=f) / f(ROPE)))
    invf[NOPE:QK, 0] = np.tile(inv, 2)
    cols += [_rows(a["final_norm"]), _rows(a["g_mix_2"][0]), conv2, _rows(a["conv_b_2"][0]),
             _rows(a["b_rg_a_2"][0]), _rows(a["b_rg_i_2"][0]), _rows(a["rg_lambda_2"][0]),
             _rows(a["g_mem_2"][0]), _rows(a["g_mlp_2"][0]), _rows(a["g_final_2"]),
             _rows(a["cmp_pos_k_2"][0]), _rows(a["cmp_pos_v_2"][0]), np.full((P, 1), EPS, f),
             (T - 1 - tok).reshape(TB, P).T.astype(f),
             np.where(tok < T - 1, 0.0, NEG).reshape(TB, P).T.astype(f), invf]
    k["cols"] = np.concatenate(cols, 1)

    k["xt"] = np.ascontiguousarray(a["x"][0].reshape(T, KC, P).transpose(2, 1, 0))
    k["positions"] = np.ascontiguousarray(np.broadcast_to(a["positions"], (QK, T)))
    k["f_w1"] = a["hy_filt_w1"]
    k["f_w23"] = np.stack([a["hy_filt_w2"], a["hy_filt_w3"]], 2)
    k["f_w4"] = a["hy_filt_w4"]
    k["w_qb"] = a["mla_w_qb"].reshape(DEPTH, 2, P, HEADS * QK).transpose(0, 2, 1, 3)
    k["w_kvb"] = a["mla_w_kvb"].reshape(DEPTH, P, HEADS, 2, VDIM).transpose(0, 1, 3, 2, 4).reshape(DEPTH, P, 2, T)
    ra = np.zeros((P, 2, KC, P), f)
    for j, name in enumerate(("w_rg_a_2", "w_rg_i_2")):
        for t in range(KC):
            for b in range(2):
                s = slice(64 * b, 64 * b + 64)
                ra[s, j, t, s] = a[name][0, 2 * t + b]
    k["w_ra"] = ra
    k["mem_t"] = a["mem_2"][0].reshape(MEM, KC, P).transpose(2, 1, 0)
    k["w_xo"] = a["w_xo_2"][0].reshape(2, P, D).transpose(1, 0, 2)
    k["w_c1"] = np.stack([a[f"w_cmp_{s}1_2"][0].reshape(16, P, 256).transpose(1, 0, 2) for s in "kv"])
    k["w_c2"] = np.stack([a[f"w_cmp_{s}2_2"][0].reshape(2, P, HD).transpose(1, 0, 2) for s in "kv"])
    return {n: np.ascontiguousarray(v) for n, v in k.items()}


def kernel(**inputs):
    import concourse.bacc as bacc
    from concourse.bass_utils import run_bass_kernel_spmd

    arrays = layout({n: np.asarray(v) for n, v in inputs.items()})
    nc = bacc.Bacc("TRN2", target_bir_lowering=False, num_devices=1)
    d = {n: nc.dram_tensor(f"in_{n}", v.shape, mybir.dt.from_np(v.dtype), kind="ExternalInput").ap()
         for n, v in arrays.items()}
    d["out"] = nc.dram_tensor("out", (P, KC, T), F32, kind="ExternalOutput").ap()
    build(nc, d)
    r = run_bass_kernel_spmd(nc, [{f"in_{n}": v for n, v in arrays.items()}], core_ids=[0])
    y = r.results[0]["out"]
    return np.ascontiguousarray(y.transpose(2, 1, 0)).reshape(1, T, D)
```
